# Optimizing a Trainium2 kernel written in Bass

```python
import math
import jax
import jax.numpy as jnp
from jax import lax
import numpy as np

D_MODEL = 1024
BATCH = 1
SEQ = 512
DEPTH = 2

CTX_LEN = 256
GRID_W = 64
N_BRANCH = 4
BRANCH_WIDTH = 256
RET_HEADS = 4
RET_DK = 64
RET_DV = 64
RET_CHUNK = 128
RET_THETA = 10000.0
GLA_HEADS = 4
GLA_DK = 64
GLA_DV = 64
GLA_RANK = 16
GLA_TAU = 16.0
GLA_CHUNK = 64
GQA_HEADS = 4
GQA_KV_HEADS = 2
GQA_DH = 64
DIFF_HEADS = 4
DIFF_DQK = 32
DIFF_DV = 64
Q_BLOCK = 128
ROPE_THETA = 10000.0
D_FF = 2816
CONV_W = 3
RMS_EPS = 1e-6

IN_SPLITS = (
    ('ret_q', RET_HEADS * RET_DK), ('ret_k', RET_HEADS * RET_DK),
    ('ret_v', RET_HEADS * RET_DV), ('ret_g', RET_HEADS * RET_DV),
    ('gla_q', GLA_HEADS * GLA_DK), ('gla_k', GLA_HEADS * GLA_DK),
    ('gla_v', GLA_HEADS * GLA_DV), ('gla_r', GLA_HEADS * GLA_DV), ('gla_a', 2 * GLA_RANK),
    ('gqa_q', GQA_HEADS * GQA_DH), ('gqa_k', GQA_KV_HEADS * GQA_DH), ('gqa_v', GQA_KV_HEADS * GQA_DH),
    ('dif_q', DIFF_HEADS * 2 * DIFF_DQK), ('dif_k', DIFF_HEADS * 2 * DIFF_DQK), ('dif_v', DIFF_HEADS * DIFF_DV),
    ('gates', N_BRANCH * D_MODEL),
)
IN_WIDTH = sum(w for _, w in IN_SPLITS)

kernel_name = 'hybrid_parallel_ret_gla_gqa_diff_convffn'

def rms_norm(x, w=None):
    xf = x.astype(jnp.float32)
    y = xf * lax.rsqrt(jnp.mean(xf * xf, axis=-1, keepdims=True) + RMS_EPS)
    if w is not None:
        y = y * w.astype(jnp.float32)
    return y.astype(x.dtype)

def modulate(h, shift, scale):
    return h * (1.0 + scale) + shift

def split_cols(z):
    out = {}
    off = 0
    for name, w in IN_SPLITS:
        out[name] = z[..., off:off + w]
        off += w
    return out

def split_heads(z, n_heads):
    b, t, w = z.shape
    return z.reshape(b, t, n_heads, w // n_heads).transpose(0, 2, 1, 3)

def merge_heads(o):
    b, h, t, d = o.shape
    return o.transpose(0, 2, 1, 3).reshape(b, t, h * d)

def seq_dir(a, d):
    return jnp.flip(a, axis=2) if d == 1 else a

def apply_rope(x, cos, sin):
    h = x.shape[-1] // 2
    x1, x2 = x[..., :h], x[..., h:]
    cos = cos.astype(x.dtype)
    sin = sin.astype(x.dtype)
    return jnp.concatenate([x1 * cos - x2 * sin, x1 * sin + x2 * cos], axis=-1)

def axial_rope(rows, dim):
    axis_dim = dim // 2
    freqs = ROPE_THETA ** (-jnp.arange(0, axis_dim, 2, dtype=jnp.float32) / axis_dim)
    row = jnp.repeat(jnp.arange(rows, dtype=jnp.float32), GRID_W)
    col = jnp.tile(jnp.arange(GRID_W, dtype=jnp.float32), rows)
    ang = jnp.concatenate([row[:, None] * freqs, col[:, None] * freqs], axis=-1)
    return jnp.cos(ang), jnp.sin(ang)

def rope_1d(n_tok, dim):
    freqs = RET_THETA ** (-jnp.linspace(0.0, 1.0, dim // 2, dtype=jnp.float32))
    ang = jnp.arange(n_tok, dtype=jnp.float32)[:, None] * freqs
    return jnp.cos(ang), jnp.sin(ang)

def to_chunks(a, chunk):
    b, h, t, d = a.shape
    return a.reshape(b, h, t // chunk, chunk, d).transpose(2, 0, 1, 3, 4)

def from_chunks(o):
    n, b, h, c, d = o.shape
    return o.transpose(1, 2, 0, 3, 4).reshape(b, h, n * c, d)

def retention_scan(q, k, v, log_gamma, s0, with_out):
    c = RET_CHUNK
    idx = jnp.arange(c, dtype=jnp.float32)
    lg = log_gamma[:, None]
    dist = idx[:, None] - idx[None, :]
    decay = jnp.where(dist >= 0, jnp.exp(lg[:, :, None] * jnp.maximum(dist, 0.0)), 0.0)
    q_decay = jnp.exp(lg * (idx + 1.0))[None, :, :, None]
    k_decay = jnp.exp(lg * (c - 1.0 - idx))[None, :, :, None]
    chunk_decay = jnp.exp(log_gamma * c)[None, :, None, None]

    def step(s, inp):
        qi, ki, vi = inp
        s_new = s * chunk_decay + jnp.einsum('bhjd,bhjv->bhdv', ki * k_decay, vi)
        if not with_out:
            return s_new, None
        scores = jnp.einsum('bhid,bhjd->bhij', qi, ki) * decay
        o = jnp.einsum('bhij,bhjv->bhiv', scores, vi) + jnp.einsum('bhid,bhdv->bhiv', qi, s) * q_decay
        return s_new, o

    s_fin, out = lax.scan(step, s0, (to_chunks(q, c), to_chunks(k, c), to_chunks(v, c)))
    return (from_chunks(out) if with_out else None), s_fin

def gla_scan(q, k, v, log_a, s0, with_out):
    c = GLA_CHUNK
    causal = jnp.tril(jnp.ones((c, c), dtype=bool))[:, :, None]

    def step(s, inp):
        qi, ki, vi, gi = inp
        b = jnp.cumsum(gi, axis=2)
        b_last = b[:, :, -1:, :]
        s_new = jnp.exp(b_last[:, :, 0, :, None]) * s + jnp.einsum('bhjd,bhjv->bhdv', ki * jnp.exp(b_last - b), vi)
        if not with_out:
            return s_new, None
        rel = jnp.exp(jnp.where(causal, b[:, :, :, None, :] - b[:, :, None, :, :], -jnp.inf))
        att = jnp.einsum('bhid,bhjd,bhijd->bhij', qi, ki, rel)
        o = jnp.einsum('bhij,bhjv->bhiv', att, vi) + jnp.einsum('bhid,bhdv->bhiv', qi * jnp.exp(b), s)
        return s_new, o

    xs = (to_chunks(q, c), to_chunks(k, c), to_chunks(v, c), to_chunks(log_a, c))
    s_fin, out = lax.scan(step, s0, xs)
    return (from_chunks(out) if with_out else None), s_fin

def blocked_attention(q, k, v, scale):
    b, hk, g, t, d = q.shape
    nb = t // Q_BLOCK
    qb = q.reshape(b, hk, g, nb, Q_BLOCK, d).transpose(3, 0, 1, 2, 4, 5)

    def attend(qi):
        s = jnp.einsum('bkgqd,bksd->bkgqs', qi, k, preferred_element_type=jnp.float32) * scale
        p = jax.nn.softmax(s, axis=-1).astype(v.dtype)
        return jnp.einsum('bkgqs,bksv->bkgqv', p, v)

    o = lax.map(attend, qb)
    return o.transpose(1, 2, 3, 0, 4, 5).reshape(b, hk, g, t, v.shape[-1])

def retention_branch(zl, zc, log_gamma, rope, need_ctx):
    cos, sin = rope
    scale = RET_DK ** -0.5
    ql = apply_rope(split_heads(zl['ret_q'], RET_HEADS), cos, sin)
    kl = apply_rope(split_heads(zl['ret_k'], RET_HEADS), cos, sin) * scale
    vl = split_heads(zl['ret_v'], RET_HEADS)
    qc = split_heads(zc['ret_q'], RET_HEADS)
    kc = split_heads(zc['ret_k'], RET_HEADS) * scale
    vc = split_heads(zc['ret_v'], RET_HEADS)
    s0 = jnp.zeros((ql.shape[0], RET_HEADS, RET_DK, RET_DV), jnp.float32)
    lat, ctx = [], []
    for d in range(2):
        oc, s_ctx = retention_scan(seq_dir(qc, d), seq_dir(kc, d), seq_dir(vc, d), log_gamma[d], s0, need_ctx)
        ol, _ = retention_scan(seq_dir(ql, d), seq_dir(kl, d), seq_dir(vl, d), log_gamma[d], s_ctx, True)
        lat.append(seq_dir(ol, d))
        if need_ctx:
            ctx.append(seq_dir(oc, d))

    def out(o, g):
        return merge_heads(rms_norm(o)).astype(g.dtype) * jax.nn.silu(g)

    y_l = out(lat[0] + lat[1], zl['ret_g'])
    y_c = out(ctx[0] + ctx[1], zc['ret_g']) if need_ctx else None
    return y_l, y_c

def gla_branch(zl, zc, gate_up, gate_b, norm_w, need_ctx):
    def prep(z):
        q = split_heads(z['gla_q'], GLA_HEADS) * GLA_DK ** -0.5
        k = split_heads(z['gla_k'], GLA_HEADS)
        v = split_heads(z['gla_v'], GLA_HEADS)
        b, t, _ = z['gla_a'].shape
        lr = z['gla_a'].reshape(b, t, 2, GLA_RANK)
        logit = jnp.einsum('btnr,nrk->btnk', lr, gate_up) + gate_b
        log_a = jax.nn.log_sigmoid(logit.astype(jnp.float32)) / GLA_TAU
        return q, k, v, [split_heads(log_a[:, :, d], GLA_HEADS) for d in range(2)]

    ql, kl, vl, al = prep(zl)
    qc, kc, vc, ac = prep(zc)
    s0 = jnp.zeros((ql.shape[0], GLA_HEADS, GLA_DK, GLA_DV), jnp.float32)
    lat, ctx = [], []
    for d in range(2):
        oc, s_ctx = gla_scan(seq_dir(qc, d), seq_dir(kc, d), seq_dir(vc, d), seq_dir(ac[d], d), s0, need_ctx)
        ol, _ = gla_scan(seq_dir(ql, d), seq_dir(kl, d), seq_dir(vl, d), seq_dir(al[d], d), s_ctx, True)
        lat.append(seq_dir(ol, d))
        if need_ctx:
            ctx.append(seq_dir(oc, d))

    def out(o, r):
        return merge_heads(rms_norm(o, norm_w)).astype(r.dtype) * jax.nn.silu(r)

    y_l = out(lat[0] + lat[1], zl['gla_r'])
    y_c = out(ctx[0] + ctx[1], zc['gla_r']) if need_ctx else None
    return y_l, y_c

def gqa_branch(zl, zc, q_norm, k_norm, rope, need_ctx):
    cos, sin = rope
    group = GQA_HEADS // GQA_KV_HEADS

    def prep(z, use_rope):
        q = rms_norm(split_heads(z['gqa_q'], GQA_HEADS), q_norm)
        k = rms_norm(split_heads(z['gqa_k'], GQA_KV_HEADS), k_norm)
        v = split_heads(z['gqa_v'], GQA_KV_HEADS)
        if use_rope:
            q = apply_rope(q, cos, sin)
            k = apply_rope(k, cos, sin)
        b, _, t, _ = q.shape
        return q.reshape(b, GQA_KV_HEADS, group, t, GQA_DH), k, v

    ql, kl, vl = prep(zl, True)
    qc, kc, vc = prep(zc, False)
    scale = GQA_DH ** -0.5
    b, _, _, t, _ = ql.shape
    ol = blocked_attention(ql, jnp.concatenate([kl, kc], axis=2), jnp.concatenate([vl, vc], axis=2), scale)
    y_l = merge_heads(ol.reshape(b, GQA_HEADS, t, GQA_DH))
    y_c = None
    if need_ctx:
        oc = blocked_attention(qc, kc, vc, scale)
        y_c = merge_heads(oc.reshape(b, GQA_HEADS, qc.shape[3], GQA_DH))
    return y_l, y_c

def diff_branch(zl, zc, q_norm, k_norm, lam_vecs, subln, layer_idx, rope, need_ctx):
    cos, sin = rope
    lam_init = 0.8 - 0.6 * math.exp(-0.3 * layer_idx)
    lv = lam_vecs.astype(jnp.float32)
    lam = jnp.exp(jnp.sum(lv[0] * lv[1])) - jnp.exp(jnp.sum(lv[2] * lv[3])) + lam_init

    def qk_maps(a):
        b, t, _ = a.shape
        return a.reshape(b, t, DIFF_HEADS, 2, DIFF_DQK).transpose(0, 3, 2, 1, 4).reshape(b, 2 * DIFF_HEADS, t, DIFF_DQK)

    def prep(z, use_rope):
        q = rms_norm(qk_maps(z['dif_q']), q_norm)
        k = rms_norm(qk_maps(z['dif_k']), k_norm)
        if use_rope:
            q = apply_rope(q, cos, sin)
            k = apply_rope(k, cos, sin)
        v = split_heads(z['dif_v'], DIFF_HEADS)
        return q[:, :, None], k, v

    ql, kl, vl = prep(zl, True)
    qc, kc, vc = prep(zc, False)
    scale = DIFF_DQK ** -0.5

    def combine(o):
        b, _, _, t, _ = o.shape
        o = o.reshape(b, 2, DIFF_HEADS, t, DIFF_DV)
        o = o[:, 0] - lam.astype(o.dtype) * o[:, 1]
        return merge_heads(rms_norm(o, subln) * (1.0 - lam_init))

    v_lat = jnp.concatenate([vl, vc], axis=2)
    ol = blocked_attention(ql, jnp.concatenate([kl, kc], axis=2), jnp.concatenate([v_lat, v_lat], axis=1), scale)
    y_l = combine(ol)
    y_c = combine(blocked_attention(qc, kc, jnp.concatenate([vc, vc], axis=1), scale)) if need_ctx else None
    return y_l, y_c

def merge_branches(ys, gate_logits, w_branch, w_out):
    b, t, _ = gate_logits.shape
    g = jax.nn.sigmoid(gate_logits.reshape(b, t, N_BRANCH, D_MODEL))
    m = g[:, :, 0] * (ys[0] @ w_branch[0])
    for i in range(1, N_BRANCH):
        m = m + g[:, :, i] * (ys[i] @ w_branch[i])
    return m @ w_out

def token_mixer(hl, hc, w_in, ret_decay, gla_gate_up, gla_gate_b, gla_norm, gqa_qnorm, gqa_knorm,
                dif_qnorm, dif_knorm, dif_lambda, dif_subln, w_branch, w_out, tables, layer_idx, need_ctx):
    ret_rope, rope64, rope32 = tables
    zl = split_cols(hl @ w_in)
    zc = split_cols(hc @ w_in)
    log_gamma = jax.nn.log_sigmoid(ret_decay.astype(jnp.float32))
    a = retention_branch(zl, zc, log_gamma, ret_rope, need_ctx)
    b = gla_branch(zl, zc, gla_gate_up, gla_gate_b, gla_norm, need_ctx)
    c = gqa_branch(zl, zc, gqa_qnorm, gqa_knorm, rope64, need_ctx)
    d = diff_branch(zl, zc, dif_qnorm, dif_knorm, dif_lambda, dif_subln, layer_idx, rope32, need_ctx)
    y_l = merge_branches([a[0], b[0], c[0], d[0]], zl['gates'], w_branch, w_out)
    y_c = merge_branches([a[1], b[1], c[1], d[1]], zc['gates'], w_branch, w_out) if need_ctx else None
    return y_l, y_c

def depthwise_conv(x, w, bias):
    pad = CONV_W // 2
    t = x.shape[1]
    xp = jnp.pad(x, ((0, 0), (pad, pad), (0, 0)))
    y = xp[:, 0:t] * w[0]
    for j in range(1, CONV_W):
        y = y + xp[:, j:j + t] * w[j]
    return y + bias

def conv_ffn(h, w_up, conv_w, conv_b, w_down):
    u = h @ w_up
    a = depthwise_conv(u[..., :D_FF], conv_w, conv_b)
    return (jax.nn.silu(a) * u[..., D_FF:]) @ w_down

def setup_inputs(seed: int = 0) -> dict:
    key = jax.random.key(seed)
    ks = iter(jax.random.split(key, 32))

    def nrm(shape, s):
        return jax.random.normal(next(ks), shape, jnp.float32) * s

    L = DEPTH
    ret_logit = jnp.log(2.0 ** (5.0 + jnp.arange(RET_HEADS, dtype=jnp.float32)) - 1.0)
    return {
        'x': nrm((BATCH, SEQ, D_MODEL), 1.0),
        'c': nrm((BATCH, D_MODEL), 1.0),
        'ctx': nrm((BATCH, CTX_LEN, D_MODEL), 1.0),
        'c_ctx': nrm((D_MODEL,), 1.0),
        'w_mod': nrm((L, D_MODEL, 6 * D_MODEL), 0.5 * D_MODEL ** -0.5),
        'b_mod': nrm((L, 6 * D_MODEL), 0.02),
        'norm1': 1.0 + nrm((L, D_MODEL), 0.02),
        'norm2': 1.0 + nrm((L, D_MODEL), 0.02),
        'w_in': nrm((L, D_MODEL, IN_WIDTH), D_MODEL ** -0.5),
        'ret_decay': ret_logit[None, None, :] + nrm((L, 2, RET_HEADS), 0.1),
        'gla_gate_up': nrm((L, 2, GLA_RANK, GLA_HEADS * GLA_DK), GLA_RANK ** -0.5),
        'gla_gate_b': nrm((L, 2, GLA_HEADS * GLA_DK), 0.1),
        'gla_norm': 1.0 + nrm((L, GLA_DV), 0.02),
        'gqa_qnorm': 1.0 + nrm((L, GQA_DH), 0.02),
        'gqa_knorm': 1.0 + nrm((L, GQA_DH), 0.02),
        'dif_qnorm': 1.0 + nrm((L, DIFF_DQK), 0.02),
        'dif_knorm': 1.0 + nrm((L, DIFF_DQK), 0.02),
        'dif_lambda': nrm((L, 4, DIFF_DQK), 0.1),
        'dif_subln': 1.0 + nrm((L, DIFF_DV), 0.02),
        'w_branch': nrm((L, N_BRANCH, BRANCH_WIDTH, D_MODEL), BRANCH_WIDTH ** -0.5),
        'w_out': nrm((L, D_MODEL, D_MODEL), D_MODEL ** -0.5),
        'w_up': nrm((L, D_MODEL, 2 * D_FF), D_MODEL ** -0.5),
        'conv_w': nrm((L, CONV_W, D_FF), CONV_W ** -0.5),
        'conv_b': nrm((L, D_FF), 0.02),
        'w_down': nrm((L, D_FF, D_MODEL), D_FF ** -0.5),
    }

def reference(x, c, ctx, c_ctx, w_mod, b_mod, norm1, norm2, w_in, ret_decay, gla_gate_up, gla_gate_b,
              gla_norm, gqa_qnorm, gqa_knorm, dif_qnorm, dif_knorm, dif_lambda, dif_subln, w_branch, w_out,
              w_up, conv_w, conv_b, w_down):
    n_tok = x.shape[1]
    rows = n_tok // GRID_W
    tables = (rope_1d(n_tok, RET_DK), axial_rope(rows, GQA_DH), axial_rope(rows, DIFF_DQK))
    xc = ctx
    for l in range(DEPTH):
        need_ctx = l < DEPTH - 1
        mod_l = (jax.nn.silu(c) @ w_mod[l] + b_mod[l])[:, None, :]
        mod_c = (jax.nn.silu(c_ctx) @ w_mod[l] + b_mod[l])[None, None, :]
        sh1, sc1, g1, sh2, sc2, g2 = jnp.split(mod_l, 6, axis=-1)
        sh1c, sc1c, g1c, sh2c, sc2c, g2c = jnp.split(mod_c, 6, axis=-1)
        hl = modulate(rms_norm(x, norm1[l]), sh1, sc1)
        hc = modulate(rms_norm(xc, norm1[l]), sh1c, sc1c)
        y_l, y_c = token_mixer(hl, hc, w_in[l], ret_decay[l], gla_gate_up[l], gla_gate_b[l], gla_norm[l],
                               gqa_qnorm[l], gqa_knorm[l], dif_qnorm[l], dif_knorm[l], dif_lambda[l],
                               dif_subln[l], w_branch[l], w_out[l], tables, l, need_ctx)
        x = x + g1 * y_l
        x = x + g2 * conv_ffn(modulate(rms_norm(x, norm2[l]), sh2, sc2), w_up[l], conv_w[l], conv_b[l], w_down[l])
        if need_ctx:
            xc = xc + g1c * y_c
            xc = xc + g2c * conv_ffn(modulate(rms_norm(xc, norm2[l]), sh2c, sc2c),
                                     w_up[l], conv_w[l], conv_b[l], w_down[l])
    return x


_drawn_inputs = setup_inputs


def setup_inputs(seed=0):
    import zlib

    import numpy as np

    out = dict(_drawn_inputs(seed))
    spreads = {}
    factors = {'norm1': 6.057,
     'norm2': 6.457,
     'gla_gate_b': 7.786,
     'gla_norm': 8.0,
     'gqa_qnorm': 8.0,
     'gqa_knorm': 8.0,
     'dif_qnorm': 8.0,
     'dif_knorm': 8.0,
     'dif_lambda': 8.0,
     'dif_subln': 8.0,
     'conv_b': 8.0}
    for name, (base, spread) in spreads.items():
        noise = np.random.default_rng([zlib.crc32(name.encode()), seed]).standard_normal(out[name].shape)
        drawn = base * np.exp(spread * noise) if base else spread * noise
        out[name] = jnp.asarray(drawn.astype(out[name].dtype))
    for name, factor in factors.items():
        out[name] = (out[name] * factor).astype(out[name].dtype)
    return out
```

```python
import math
from contextlib import ExitStack

import numpy as np
import concourse.bass as bass
import concourse.mybir as mybir
from concourse.alu_op_type import AluOpType as ALU

F32 = mybir.dt.float32
U8 = mybir.dt.uint8
ACT = mybir.ActivationFunctionType
AX = mybir.AxisListType.X

P = 128
D = 1024
KT = D // P
LAT, CTX = 512, 256
T = LAT + CTX
TL, TC = LAT // P, CTX // P
NT = TL + TC
DEPTH = 2
GRID_W = 64
DFF = 2816
FT = DFF // P
MODT = 6 * D // P
RANK = 16
EPS = 1e-6
GATES = 3360
RING = 4
LEVELS = [64, 32, 16, 8, 4, 2, 1]

BR = {
    "ret": dict(n=0, feat=[0, 128, 256, 384], nq=2, tok=[512, 640, 768, 896]),
    "gla": dict(n=1, feat=[1024, 1152, 1280, 1408, 2048], nq=2, tok=[1536, 1664, 1792, 1920]),
    "gqa": dict(n=2, feat=[2080, 2208, 2336], nq=2, tok=[2464]),
    "dif": dict(n=3, feat=[2592, 2720, 2848, 2976], nq=2, tok=[3104, 3232]),
}
VA_BMOD, VA_N1, VA_N2, VA_CB, VA_ROWS = 0, MODT, MODT + KT, MODT + 2 * KT, MODT + 2 * KT + FT
VB_CW, VB_C, VB_QN, VB_ROWS = 0, 3 * FT, 3 * FT + 2 * KT, 3 * FT + 2 * KT + 4
SMALL = [("ident", P), ("ones", P), ("sum64", P), ("sum32", P), ("perm64", P), ("perm32", P),
         ("tri", 2 * P), ("rest", 2 * P), ("two", P), ("swap", P)]


def constants():
    f = np.float32
    j, i = np.arange(P)[:, None], np.arange(P)[None, :]
    c = {}
    c["ident"] = (j == i).astype(f)
    c["two"] = 2 * c["ident"]
    c["swap"] = (j == (i + P // 2) % P).astype(f)
    c["ones"] = np.full((P, P), 1.0 / D, f)
    for d in (64, 32):
        c[f"sum{d}"] = (j // d == i // d).astype(f) / d
        half = d // 2
        first = i % d < half
        c[f"perm{d}"] = (((j == i + half) & first) * -1.0 + ((j == i - half) & ~first) * 1.0).astype(f)
    c["tri"] = np.concatenate([(j <= i), (j >= i)], 1).astype(f) / 16
    c["rest"] = np.concatenate([(j > i), (j < i)], 1).astype(f) / 16
    small = np.concatenate([c[n] for n, _ in SMALL], 1).astype(f)

    def rot(ang, dim):
        cs, sn = np.cos(ang).astype(f).T, np.sin(ang).astype(f).T
        reps = P // (dim // 2)
        return np.tile(cs, (reps, 1)), np.tile(sn, (reps, 1))

    freqs = f(10000.0) ** (-np.linspace(0.0, 1.0, 32, dtype=f))
    ret = rot(np.arange(LAT, dtype=f)[:, None] * freqs, 64)

    def axial(dim):
        ax = dim // 2
        fr = f(10000.0) ** (-np.arange(0, ax, 2, dtype=f) / f(ax))
        tok = np.arange(LAT)
        return rot(np.concatenate([(tok // GRID_W).astype(f)[:, None] * fr,
                                   (tok % GRID_W).astype(f)[:, None] * fr], -1), dim)

    rope = np.concatenate([*ret, *axial(64), *axial(32)], 1).astype(f)
    p = np.arange(P)[:, None]
    e = np.arange(7 * P)[None, :]
    near = (P * (3 - e // P) + e % P - p).astype(f)
    e = np.arange(5 * P)[None, :]
    u = P * (3 - e // P) + e % P - p
    dist = np.concatenate([near, CTX + u, LAT - u], 1).astype(f)
    mask = np.zeros((P, 2, len(LEVELS), P), f)
    for n, h in enumerate(LEVELS):
        same = (j // (2 * h)) == (i // (2 * h))
        mask[:, 0, n] = same & (j % (2 * h) < h) & (i % (2 * h) >= h)
        mask[:, 1, n] = same & (j % (2 * h) >= h) & (i % (2 * h) < h)
    return dict(k_small=small, k_rope=rope, k_dist=dist, k_mask=mask.reshape(P, -1))


class Tally:

    def __init__(self):
        self.count, self.at = {}, {}

    def add(self, sem, key, by=1):
        self.count[sem] = self.count.get(sem, 0) + by
        self.at[key] = (sem, self.count[sem], 0)

    def loop(self, keys, iters, by=1):
        per = {}
        for sem, key in keys:
            per[sem] = per.get(sem, 0) + by
        seen = {}
        for sem, key in keys:
            seen[sem] = seen.get(sem, 0) + by
            self.at[key] = (sem, self.count.get(sem, 0) + seen[sem], per[sem])
        for sem, n in per.items():
            self.count[sem] = self.count.get(sem, 0) + n * iters


class Chain:

    def __init__(self, eng, sem):
        self.eng, self.sem, self.n, self.it = eng, sem, 0, None

    def __call__(self, ins):
        ins.then_inc(self.sem, 1)
        self.n += 1
        if self.it is None:
            self.eng.wait_ge(self.sem, self.n)
        else:
            self.eng.wait_ge(self.sem, self.it[0] * self.it[1] + self.n)

    def enter(self, i, per):
        self.it, self.start = (i, per), self.n

    def leave(self, iters):
        i, per = self.it
        assert self.n - self.start == per, (self.n - self.start, per)
        self.n, self.it = self.start + per * iters, None


def schedule(depth=DEPTH):
    ev = Tally()
    chunk, fill, fills = {}, {}, [0] * 4
    nch = [0]

    def chunks(keys, iters=1):
        for n, key in enumerate(keys):
            chunk[key] = (nch[0] + n, len(keys) if iters > 1 else 0)
        nch[0] += len(keys) * iters

    def take(key, p, ready=None, iters=1, per=0):
        fill[key] = (p, fills[p], per, ready)
        fills[p] += 1
        if ready is None:
            ev.add(f"full{p}", ("full", key))

    for l in range(depth):
        nq = NT if l < depth - 1 else TL
        if l == 0:
            for k in range(KT):
                take(("x", k), k % 4)
            for i in range(2 * depth):
                take(("vec", i), i % 4)
        chunks([("mod", l, u) for u in range(4)], MODT // 4)
        take(("mod", l), 3, "chunk")
        ev.add("mod_ready", ("modr", l))
        for which in (1, 2):
            if which == 2:
                for b in ("ret", "gla", "gqa", "dif"):
                    for n in range(len(BR[b]["feat"])):
                        chunks([("f", l, b, n)])
                        take(("f", l, b, n), nch[0] % 2, "chunk")
                    for n in range(len(BR[b]["tok"])):
                        chunks([("t", l, b, n)])
                        take(("t", l, b, n), nch[0] % 2, "chunk")
                    if b == "ret":
                        for h in range(4):
                            ev.add("strip_exponents", ("sti", l, h))
                            ev.add("strip_exps", ("ste", l, h))
                    if b != "gla":
                        for n in range(len(BR[b]["feat"])):
                            if b != "ret":
                                ev.add("squares", ("qksq", l, b, n))
                                take(("qkn", l, b, n), 2)
                                ev.add("turnable", ("turnable", l, b, n))
                            take(("rope", l, b, n), 3)
                            ev.add("turned", ("turned", l, b, n))
                    if b == "gla":
                        for t in range(NT):
                            take(("logit", l, t), 0)
                            ev.add("gla_abs", ("abs", l, t))
                            ev.add("gla_ln", ("ln", l, t))
                            ev.add("gla_la", ("la", l, t))
                            take(("cum", l, t), 1)
                            take(("rest", l, t), 2)
                            take(("ktok", l, t), 3)
                            take(("U", l, t), 0)
                        for t in range(nq):
                            ev.add("gla_eb", ("eb", l, t))
                            take(("diag", l, t), 2)
                            for n in range(len(LEVELS)):
                                ev.add("gla_dd", ("dd", l, t, n))
                                ev.add("gla_e", ("e", l, t, n))
                                ev.add("gla_qk", ("qk", l, t, n))
                                take(("lev", l, t, n), n % 2)
                            take(("o", l, b, t), 3)
                    if b == "gqa":
                        take(("swap", l), 2)
                    for t in range(nq):
                        for h in range(4):
                            if b == "ret":
                                take(("s", l, b, t, h), h % 2)
                                ev.add("weights_used", ("pv", l, b, t, h))
                            if b in ("gqa", "dif"):
                                for m in range(2 if b == "dif" else 1):
                                    take(("s", l, b, t, h, m), m if b == "dif" else h % 2)
                                    ev.add("max_ready", ("max", l, b, t, h, m))
                                if b == "dif":
                                    ev.add("differed", ("dif", l, b, t, h))
                                take(("pt", l, b, t, h), 2)
                                ev.add("weights_used", ("pv", l, b, t, h))
                        if b != "gla":
                            take(("o", l, b, t), 3, ("pv", l, b, t, 3))
                    if b != "gqa":
                        ev.add("o_squares", ("osq", l, b))
                        ev.add("o_roots", ("oroot", l, b))
                        if b in ("ret", "gla"):
                            ev.add("o_silu", ("osilu", l, b))
                        ev.add("o_normed", ("onorm", l, b))
                    take(("y", l, b, 0), 0)
                    take(("y", l, b, 1), 1)
                keys = [("g", l, u, b) for u in range(4) for b in range(5)]
                chunks(keys, 2)
                base = list(fills)
                for u in range(4):
                    for b in range(4):
                        take(("g", l, u, b), b % 2, "chunk")
                    for b in range(4):
                        fill[("yb", l, u, b)] = (2 + b % 2, fills[2 + b % 2], 0, "chunk" if b == 3 else None)
                        fills[2 + b % 2] += 1
                close(fill, fills, base, 2, [k for k in fill if k[0] in ("g", "yb") and k[1] == l])
                ev.loop([(f"full{2 + b % 2}", ("full", ("yb", l, u, b))) for u in range(4) for b in range(3)], 2)
                ev.loop([("merged", ("merged", l, u)) for u in range(4)], 2)
                chunks([("out", l, u) for u in range(4)], 2)
                base = list(fills)
                for u in range(4):
                    take(("out", l, u), u % 2, "chunk")
                close(fill, fills, base, 2, [("out", l, u) for u in range(4)])
            for k in range(KT):
                ev.add("squares", ("sq", l, which, k))
                ev.add("squares_used", ("squ", l, which, k))
            take(("norm", l, which), 2, ("squ", l, which, KT - 1))
            for k in range(KT):
                ev.add("scaled", ("scaled", l, which, k))
                ev.add("h_ready", ("h", l, which, k))
        chunks([("up", l, u) for u in range(4)], FT // 2)
        base = list(fills)
        for u in range(4):
            take(("up", l, u), u, "chunk")
        close(fill, fills, base, FT // 2, [("up", l, u) for u in range(4)])
        ev.loop([("conv_centre", ("cc", l, u)) for u in range(2)], FT // 2)
        ev.loop([("conv_silu", ("cs", l, u)) for u in range(2)], FT // 2)
        chunks([("down", l, u, j) for u in range(4) for j in range(3)], 2)
        base = list(fills)
        for u in range(4):
            take(("down", l, u), u % 2, "chunk")
        close(fill, fills, base, 2, [("down", l, u) for u in range(4)])
    for t in range(TL):
        take(("final", t), t)
        ev.add("final_ready", ("fr", t))
    return ev, chunk, fill, fills


def close(fill, fills, base, iters, keys):
    per = [a - b for a, b in zip(fills, base)]
    for key in keys:
        p, n, _, ready = fill[key]
        fill[key] = (p, n, per[p], ready)
    for p in range(4):
        fills[p] = base[p] + per[p] * iters


def bass_hybrid_backbone(nc, A, out):
    ev, chunk, fill, _ = schedule()
    ctx = ExitStack()
    with ctx:
        def sb(name, shape, dt=F32):
            return ctx.enter_context(nc.sbuf_tensor(name, shape, dt))

        xT = sb("xT", [P, KT, T])
        hT = sb("hT", [P, KT, T])
        ring = sb("ring", [P, RING, KT, P])
        small = sb("small", [P, sum(w for _, w in SMALL)])
        rope = sb("rope", [P, 6, LAT])
        dist = sb("dist", [P, 17 * P])
        mask = sb("mask", [P, 2, len(LEVELS), P], U8)
        rows = sb("rows", [P, 2 * DEPTH, P])
        vec = sb("vec", [P, 2 * DEPTH, P])
        gate_b = sb("gate_b", [P, DEPTH, 512])
        gate_up = sb("gate_up", [32, DEPTH, 512])
        onorm = sb("onorm", [P, 2, DEPTH, 64])
        decay = sb("decay", [P, DEPTH * 8])
        lams = sb("lams", [P, DEPTH * 4 * 32])
        tiny = sb("tiny", [P, 256])
        modv = sb("modv", [P, MODT, 2])
        arena = sb("arena", [P, 24192])
        used = [0]

        def part(n):
            used[0] += n
            return arena[:, used[0] - n:used[0]]

        q = part(5 * T).rearrange("p (c t) -> p c t", t=T)
        v = part(4 * T).rearrange("p (c n t) -> p c n t", c=4, n=NT)
        yT = part(8 * T).rearrange("p (c t) -> p c t", t=T)
        scratch0 = used[0]
        scratch = arena[:, scratch0:]
        size = {n: w for n, w in SMALL}
        offs, o = {}, 0
        for n, w in SMALL:
            offs[n] = o
            o += w
        K = {n: small[:, offs[n]:offs[n] + w] for n, w in SMALL}
        ident = K["ident"]

        pair = [ctx.enter_context(nc.psum_tensor(f"pair{i}", [P, 1024], F32)) for i in range(4)]

        S = {}
        for name in (["consts", "x_in", "out_done", "chunk_done", "dve", "act", "setup"]
                     + [f"landed{i}" for i in range(RING)] + [f"freed{i}" for i in range(4)]
                     + [f"full{i}" for i in range(4)] + sorted(k for k in ev.count if not k.startswith("full"))
                     + [f"set{i}" for i in range(8)]):
            S[name] = ctx.enter_context(nc.semaphore(name))

        def at(key, i=0):
            sem, n, per = ev.at[key]
            return S[sem], n + per * i if per else n

        def sem(key):
            return S[ev.at[key][0]]

        def chunk_no(key, i=0):
            n, per = chunk[key]
            return n, (n + per * i if per else n)

        def slot(key):
            return ring[:, chunk[key][0] % RING]

        def landed(key, i=0):
            n, per = chunk[key]
            return S[f"landed{n % RING}"], 16 * (n // RING + 1) + (16 * (per // RING) * i if per else 0)

        def room(key, i=0):
            p, n, per, _ = fill[key]
            assert n > 0
            return S[f"freed{p}"], n + per * i if per else n

        def filled(key, i=0, ck=None):
            ready = fill[key][3]
            if ready is None:
                return at(("full", key), i)
            if ready == "chunk":
                return S["chunk_done"], chunk_no(ck or key, i)[1] + 1
            return at(ready, i)

        def emptied(key, i=0):
            p, n, per, _ = fill[key]
            return S[f"freed{p}"], n + 1 + (per * i if per else 0)

        def psum(key):
            return pair[fill[key][0]]

        def freed(key):
            return S[f"freed{fill[key][0]}"]

        def fullsem(key):
            return S[f"full{fill[key][0]}"]

        def segs(w):
            return [(0, min(w, LAT))] + ([(LAT, w)] if w > LAT else [])

        def is_q(b, n):
            return n < BR[b]["nq"]

        def colv(l, which, n):
            return vec[:, 2 * l + which, n:n + 1]

        lg = tiny[:, 0:16]
        neg_lam = tiny[:, 16:18]
        pp1 = tiny[:, 20:36]
        cs = tiny[:, 40:56].rearrange("p (s k) -> p s k", s=2)
        a1 = tiny[:, 64:96].rearrange("p (w k s) -> p w k s", w=2, k=KT)
        nmx = tiny[:, 96:104]
        rsum = [tiny[:, 104:112], tiny[:, 184:192]]
        dtmp = tiny[:, 112:120]
        oss = tiny[:, 120:144]
        lamt = tiny[:, 144:148]
        eps = tiny[:, 150:151]
        rd = tiny[:, 152:184]

        last = DEPTH - 1
        W = {l: (T if l < last else LAT) for l in range(DEPTH)}
        NQ = {l: W[l] // P for l in range(DEPTH)}

        def cut(*sizes):
            o, res = scratch0, []
            for s in sizes:
                res.append(arena[:, o:o + s])
                o += s
            assert o <= arena.shape[1], (o, arena.shape)
            return res

        xin = arena[:, 0:6 * D].rearrange("p (t d) -> p t d", t=NT)
        sqb, rs, tb = cut(2 * T, T, 2 * T)
        sqb = sqb.rearrange("p (b t) -> p b t", b=2)
        tb = tb.rearrange("p (b t) -> p b t", b=2)
        o_flat, prep_flat = cut(6 * 256, 2 * T)
        o_sb = o_flat.rearrange("p (t c) -> p t c", c=256)
        prep = prep_flat.rearrange("p (b t) -> p b t", b=2)
        NEAR, FAR = 7 * P, 5 * P
        _, strip, pt_r = cut(6 * 256 + 2 * T, 4 * (NEAR + FAR), 2 * T)
        e0, e2, e1 = pt_r[:, 0:NEAR], pt_r[:, NEAR:NEAR + FAR], o_flat[:, 0:NEAR]
        strip = strip.rearrange("p (h n) -> p h n", h=4)
        pt_r = pt_r.rearrange("p (b t) -> p b t", b=2)
        _, prob, pt_s = cut(6 * 256 + 2 * T, 4 * T, 2 * T)
        prob = prob.rearrange("p (b m t) -> p b m t", b=2, m=2)
        pt_s = pt_s.rearrange("p (b t) -> p b t", b=2)
        G = {}
        _, bT, el, work = cut(6 * 256, 4 * T, 4 * NT, 9 * 512)
        bT = bT.rearrange("p (c t) -> p c t", t=T)
        el = el.rearrange("p (c t) -> p c t", c=4)
        for n, name in enumerate(["lx", "la", "ab", "ex", "kd"]):
            G[name] = work[:, 512 * n:512 * (n + 1)]
        quad = [work[:, 512 * n:512 * (n + 1)].rearrange("p (d c t) -> p d c t", d=2, c=2) for n in range(9)]
        G["dd"], G["ql"], G["kl"], G["qe"], G["eb"] = quad[0:2], quad[2:4], quad[4:6], quad[6], quad[7]
        G["pt"] = work[:, 4096:4608].rearrange("p (s c t) -> p s c t", s=2, c=2)
        yfree = yT.rearrange("p c t -> p (c t)")[:, 4 * T:8 * T]
        G["U"] = yfree[:, 0:1536].rearrange("p (t c n) -> p t c n", t=NT, c=4)
        G["S"] = yfree[:, 1536:3072].rearrange("p (t c n) -> p t c n", t=NT, c=4)
        mT, sig, prod = cut(KT * T, 4 * T, T)
        mT = mT.rearrange("p (c t) -> p c t", t=T)
        sig = sig.rearrange("p (c t) -> p c t", t=T)
        ff = arena[:, 0:FT * T].rearrange("p (c t) -> p c t", t=T)
        conv = arena[:, FT * T:(FT + 2) * T].rearrange("p (c t) -> p c t", t=T)
        res = arena[:, 0:TL * D].rearrange("p (t d) -> p t d", t=TL)

        mask_in = arena[:, 6 * D:6 * D + 2 * len(LEVELS) * P]
        loads = [(small[:], A["k_small"]), (rope[:].rearrange("p c t -> p (c t)"), A["k_rope"]),
                 (dist[:], A["k_dist"]), (mask_in, A["k_mask"]),
                 (decay[:], A["ret_decay"].rearrange("l d h -> (l d h)").partition_broadcast(P)),
                 (lams[:], A["dif_lambda"].rearrange("l m d -> (l m d)").partition_broadcast(P)),
                 (gate_b[:].rearrange("p l n -> p (l n)"), A["gla_gate_b"].rearrange("l d n -> (l d n)").partition_broadcast(P)),
                 (onorm[:, 0].rearrange("p l n -> p (l n)"), A["gla_norm"].rearrange("l n -> (l n)").partition_broadcast(P)),
                 (onorm[:, 1].rearrange("p l n -> p (l n)"), A["dif_subln"].rearrange("l n -> (l n)").partition_broadcast(P))]
        for l in range(DEPTH):
            for r0, name, n in ((VA_BMOD, "b_mod", MODT), (VA_N1, "norm1", KT), (VA_N2, "norm2", KT), (VA_CB, "conv_b", FT)):
                loads.append((rows[r0:r0 + n, 2 * l], A[name][l].rearrange("(r n) -> r n", n=P)))
            loads.append((rows[VB_CW:VB_CW + 3 * FT, 2 * l + 1], A["conv_w"][l].rearrange("w (r n) -> (w r) n", n=P)))
            loads.append((rows[VB_C:VB_C + KT, 2 * l + 1], A["c"].rearrange("b (r n) -> (b r) n", n=P)))
            loads.append((rows[VB_C + KT:VB_C + 2 * KT, 2 * l + 1], A["c_ctx"].rearrange("(r n) -> r n", n=P)))
            for r, name, dim in ((0, "gqa_qnorm", 64), (1, "gqa_knorm", 64), (2, "dif_qnorm", 32), (3, "dif_knorm", 32)):
                for s in range(P // dim):
                    loads.append((rows[VB_QN + r:VB_QN + r + 1, 2 * l + 1, s * dim:(s + 1) * dim], A[name][l:l + 1]))
        late_loads = [(gate_up[RANK * d:RANK * (d + 1), l, 256 * d:256 * (d + 1)], A["gla_gate_up"][l, d])
                      for l in range(DEPTH) for d in range(2)]
        N_CONST = len(loads) + len(late_loads)

        block = ctx.enter_context(nc.Block())

        w_in_v = [A["w_in"][l].rearrange("(k p) n -> p k n", p=P) for l in range(DEPTH)]

        @block.sync
        def _(sp):
            def load(key, src, i=None, k=KT, w=P, ahead=0):
                n, now = chunk_no(key, 0 if i is None else i)
                if n >= RING or i is not None:
                    if ahead >= 0:
                        sp.wait_ge(S["chunk_done"], now - RING + 1 + ahead)
                sp.dma_start(slot(key)[:, 0:k, 0:w], src).then_inc(S[f"landed{n % RING}"], 16)

            sp.dma_start(xin[:, 0:TL], A["x"].rearrange("b (t p) d -> p (b t) d", p=P)).then_inc(S["x_in"], 16)
            sp.dma_start(xin[:, TL:NT], A["ctx"].rearrange("b (t p) d -> p (b t) d", p=P)).then_inc(S["x_in"], 16)
            for l in range(DEPTH):
                wm = A["w_mod"][l].rearrange("(k p) (c n) -> c p k n", p=P, n=P)
                if l == 0:
                    for u in range(4):
                        load(("mod", l, u), wm[u])
                done = 1 if l == 0 else 0
                with sp.Fori(0, MODT // 4 - done) as i:
                    for u in range(4):
                        load(("mod", l, u), wm[bass.ds(4 * i + (4 * done + u), 1)].squeeze(0), i + done)
                for b in ("ret", "gla", "gqa", "dif"):
                    for kind in ("feat", "tok"):
                        for n, c in enumerate(BR[b][kind]):
                            key = (kind[0], l, b, n)
                            w = 32 if c == 2048 else P
                            load(key, w_in_v[l][:, :, c:c + w], w=w)
                wg = A["w_in"][l, :, GATES:].rearrange("(k p) (c n) -> c p k n", p=P, n=P)
                wb = A["w_branch"][l].rearrange("b (k p) (c n) -> c p (b k) n", p=P, n=P)
                with sp.Fori(0, 2) as i:
                    for u in range(4):
                        for b in range(4):
                            load(("g", l, u, b), wg[bass.ds(4 * i + u + KT * b, 1)].squeeze(0), i, ahead=b // 3)
                        load(("g", l, u, 4), wb[bass.ds(4 * i + u, 1)].squeeze(0), i, ahead=-1)
                wo = A["w_out"][l].rearrange("(k p) (c n) -> c p k n", p=P, n=P)
                with sp.Fori(0, 2) as i:
                    for u in range(4):
                        load(("out", l, u), wo[bass.ds(4 * i + u, 1)].squeeze(0), i)
                wu = A["w_up"][l].rearrange("(k p) (s c n) -> s c p k n", p=P, s=2, n=P)
                with sp.Fori(0, FT // 2) as i:
                    for u in range(4):
                        load(("up", l, u), wu[u % 2, bass.ds(2 * i + u // 2, 1)].squeeze(0), i)
                wd = A["w_down"][l].rearrange("(k p) (c n) -> c p k n", p=P, n=P)
                with sp.Fori(0, 2) as i:
                    for u in range(4):
                        for j in range(3):
                            k = min(8, FT - 8 * j)
                            load(("down", l, u, j), wd[bass.ds(4 * i + u, 1), :, 8 * j:8 * j + k].squeeze(0), i, k=k)
            sp.wait_ge(S["out_done"], 16 * TL)

        @block.tensor
        def _(pe):
            pe.wait_ge(S["consts"], 16 * N_CONST)

            def projection(key, rhs, width, i=0, M=P, kt=KT):
                pe.wait_ge(*room(key, i))
                acc = psum(key)
                pe.wait_ge(*landed(key, i))
                for a, b in segs(width):
                    for k in range(kt):
                        mm = pe.matmul(acc[0:M, a:b], slot(key)[:, k, 0:M], rhs[:, k, a:b], start=k == 0, stop=k == kt - 1)
                mm.then_inc(S["chunk_done"], 1)

            def token_projection(key, tiles):
                pe.wait_ge(*room(key))
                acc = psum(key)
                pe.wait_ge(*landed(key))
                for t in range(tiles):
                    for k in range(KT):
                        mm = pe.matmul(acc[:, t * P:(t + 1) * P], hT[:, k, t * P:(t + 1) * P], slot(key)[:, k],
                                       start=k == 0, stop=k == KT - 1)
                mm.then_inc(S["chunk_done"], 1)

            def norm(l, which):
                pe.wait_ge(*room(("norm", l, which)))
                acc = psum(("norm", l, which))
                for k in range(KT):
                    pe.wait_ge(*at(("sq", l, which, k)))
                    for a, b in segs(W[l] if which == 2 else T):
                        mm = pe.matmul(acc[:, a:b], K["ones"], sqb[:, k % 2, a:b], start=k == 0, stop=k == KT - 1)
                    mm.then_inc(sem(("squ", l, which, k)), 1)

            def prep_tiles(l, b):
                dim = 32 if b == "dif" else 64
                for n in range(len(BR[b]["feat"])):
                    w = W[l] if is_q(b, n) else T
                    if b != "ret":
                        pe.wait_ge(*room(("qkn", l, b, n)))
                        acc = psum(("qkn", l, b, n))
                        pe.wait_ge(*at(("qksq", l, b, n)))
                        for x, y in segs(w):
                            mm = pe.matmul(acc[:, x:y], K[f"sum{dim}"], prep[:, 0, x:y], start=True, stop=True)
                        mm.then_inc(fullsem(("qkn", l, b, n)), 1)
                    pe.wait_ge(*room(("rope", l, b, n)))
                    acc = psum(("rope", l, b, n))
                    if b == "ret":
                        pe.wait_ge(*emptied(("f", l, b, n)))
                    else:
                        pe.wait_ge(*at(("turnable", l, b, n)))
                    pe.matmul(acc[:, 0:LAT], K[f"perm{dim}"], q[:, n, 0:LAT], start=True, stop=True).then_inc(
                        fullsem(("rope", l, b, n)), 1)

            def retention(l):
                b = "ret"

                def scores(t, h):
                    pe.wait_ge(*room(("s", l, b, t, h)))
                    acc = psum(("s", l, b, t, h))
                    pb = 64 * (h % 2)
                    for m in (range(NT) if t < TL else range(TL, NT)):
                        mm = pe.matmul(acc[:, m * P:(m + 1) * P], q[pb:pb + 64, 2 + h // 2, m * P:(m + 1) * P],
                                       q[pb:pb + 64, h // 2, t * P:(t + 1) * P], start=True, stop=True)
                    mm.then_inc(fullsem(("s", l, b, t, h)), 1)

                order = [(t, h) for t in range(NQ[l]) for h in range(4)]
                pe.wait_ge(*at(("turned", l, b, 3)))
                scores(*order[0])
                for n, (t, h) in enumerate(order):
                    if n + 1 < len(order):
                        scores(*order[n + 1])
                    if h == 0:
                        pe.wait_ge(*room(("o", l, b, t)))
                        acc = psum(("o", l, b, t))
                    values(l, b, t, h, acc, pt_r[:, h % 2].rearrange("p (m n) -> p m n", n=P))

            def values(l, b, t, h, acc, pt):
                pe.wait_ge(*emptied(("s", l, b, t, h) if b == "ret" else ("pt", l, b, t, h)))
                ms = list(range(NT) if t < TL else range(TL, NT))
                hv = h // 2 if b == "gqa" else h
                for m in ms:
                    mm = pe.matmul(acc[:, 64 * h:64 * h + 64], pt[:, m], v[:, hv // 2, m, 64 * (hv % 2):64 * (hv % 2) + 64],
                                   start=m == ms[0], stop=m == ms[-1])
                mm.then_inc(sem(("pv", l, b, t, h)), 1)

            def softmax(l, b):
                maps = 2 if b == "dif" else 1

                def scores(t, h):
                    for m in range(maps):
                        pe.wait_ge(*room(("s", l, b, t, h, m)))
                        acc = psum(("s", l, b, t, h, m))
                        if b == "dif":
                            lo, n, qi, ki = 64 * (h % 2) + 32 * m, 32, h // 2, 2 + h // 2
                        else:
                            lo, n, qi, ki = 64 * (h % 2), 64, h // 2, 2 if h // 2 == h % 2 else 3
                        for x, y in (segs(T) if t < TL else [(LAT, T)]):
                            mm = pe.matmul(acc[:, x:y], q[lo:lo + n, qi, t * P:(t + 1) * P], q[lo:lo + n, ki, x:y],
                                           start=True, stop=True)
                        mm.then_inc(fullsem(("s", l, b, t, h, m)), 1)

                order = [(t, h) for t in range(NQ[l]) for h in range(4)]
                pe.wait_ge(*at(("turned", l, b, len(BR[b]["feat"]) - 1)))
                if b == "gqa":
                    pe.wait_ge(*room(("swap", l)))
                    acc = psum(("swap", l))
                    for x, y in segs(T):
                        mm = pe.matmul(acc[:, x:y], K["swap"], q[:, 2, x:y], start=True, stop=True)
                    mm.then_inc(fullsem(("swap", l)), 1)
                    pe.wait_ge(*emptied(("swap", l)))
                scores(*order[0])
                for n, (t, h) in enumerate(order):
                    if n + 1 < len(order):
                        scores(*order[n + 1])
                    pe.wait_ge(*room(("pt", l, b, t, h)))
                    acc = psum(("pt", l, b, t, h))
                    if b == "dif":
                        pe.wait_ge(*at(("dif", l, b, t, h)))
                    else:
                        pe.wait_ge(*emptied(("s", l, b, t, h, 0)))
                    for m in (range(NT) if t < TL else range(TL, NT)):
                        mm = pe.transpose(acc[:, m * P:(m + 1) * P], prob[:, h % 2, 0, m * P:(m + 1) * P], ident)
                    mm.then_inc(fullsem(("pt", l, b, t, h)), 1)
                    if h == 0:
                        pe.wait_ge(*room(("o", l, b, t)))
                        accO = psum(("o", l, b, t))
                    values(l, b, t, h, accO, pt_s[:, h % 2].rearrange("p (m n) -> p m n", n=P))

            def gla(l):
                pe.wait_ge(*emptied(("f", l, "gla", 4)))
                pe.wait_ge(*emptied(("t", l, "gla", 1)))
                for t in range(NT):
                    ts = slice(t * P, (t + 1) * P)
                    pe.wait_ge(*room(("logit", l, t)))
                    acc = psum(("logit", l, t))
                    pe.matmul(acc[:, 0:512], q[0:32, 4, ts], gate_up[:, l], start=True, stop=True).then_inc(
                        fullsem(("logit", l, t)), 1)
                    pe.wait_ge(*room(("ktok", l, t)))
                    acc = psum(("ktok", l, t))
                    for c in range(2):
                        mm = pe.transpose(acc[:, c * P:(c + 1) * P], q[:, 2 + c, ts], ident)
                    mm.then_inc(fullsem(("ktok", l, t)), 1)
                    pe.wait_ge(*room(("cum", l, t)))
                    acc = psum(("cum", l, t))
                    pe.wait_ge(*at(("la", l, t)))
                    for d in range(2):
                        for c in range(2):
                            lo = d * 256 + c * P
                            mm = pe.matmul(acc[:, (2 * d + c) * P:(2 * d + c + 1) * P], G["la"][:, lo:lo + P],
                                           K["tri"][:, d * P:(d + 1) * P], start=True, stop=True)
                    mm.then_inc(fullsem(("cum", l, t)), 1)
                    pe.wait_ge(*room(("rest", l, t)))
                    acc = psum(("rest", l, t))
                    for d in range(2):
                        mm = pe.matmul(acc[:, d * 256:d * 256 + 256], K["rest"][:, d * P:(d + 1) * P],
                                       G["la"][:, d * 256:d * 256 + 256], start=True, stop=True)
                    mm.then_inc(fullsem(("rest", l, t)), 1)
                    pe.wait_ge(*room(("U", l, t)))
                    acc = psum(("U", l, t))
                    pe.wait_ge(*emptied(("ktok", l, t)))
                    for d in range(2):
                        for c in range(2):
                            mm = pe.matmul(acc[:, (2 * d + c) * P:(2 * d + c + 1) * P],
                                           G["kd"][:, d * 256 + c * P:d * 256 + (c + 1) * P], v[:, c, t], start=True, stop=True)
                    mm.then_inc(fullsem(("U", l, t)), 1)
                for t in range(NQ[l]):
                    ts = slice(t * P, (t + 1) * P)
                    pe.wait_ge(*room(("diag", l, t)))
                    acc = psum(("diag", l, t))
                    for h in range(4):
                        pb = 64 * (h % 2)
                        lo = 512 * (h % 2) + P * (h // 2)
                        mm = pe.matmul(acc[:, lo:lo + P], q[pb:pb + 64, 2 + h // 2, ts], q[pb:pb + 64, h // 2, ts],
                                       start=True, stop=True)
                    mm.then_inc(fullsem(("diag", l, t)), 1)
                    for n in range(len(LEVELS)):
                        pe.wait_ge(*room(("lev", l, t, n)))
                        acc = psum(("lev", l, t, n))
                        pe.wait_ge(*at(("qk", l, t, n)))
                        for d in range(2):
                            for h in range(4):
                                pb = 64 * (h % 2)
                                lo = 512 * (h % 2) + 256 * d + P * (h // 2)
                                mm = pe.matmul(acc[:, lo:lo + P],
                                               G["kl"][n % 2][pb:pb + 64, d, h // 2], G["ql"][n % 2][pb:pb + 64, d, h // 2],
                                               start=True, stop=True)
                        mm.then_inc(fullsem(("lev", l, t, n)), 1)
                    pe.wait_ge(*room(("o", l, "gla", t)))
                    acc = psum(("o", l, "gla", t))
                    pe.wait_ge(*emptied(("lev", l, t, len(LEVELS) - 1)))
                    for h in range(4):
                        pb = 64 * (h % 2)
                        lo = 512 * (h % 2) + 64 * (h // 2)
                        pe.matmul(acc[:, lo:lo + 64], G["pt"][:, h % 2, h // 2], v[:, h // 2, t, pb:pb + 64], start=True, stop=False)
                        for d in range(2):
                            mm = pe.matmul(acc[:, lo:lo + 64], G["qe"][pb:pb + 64, d, h // 2],
                                           G["S"][pb:pb + 64, t, 2 * d + h // 2], start=False, stop=d == 1)
                    mm.then_inc(fullsem(("o", l, "gla", t)), 1)

            def turn_outputs(l, b):
                if b == "gqa":
                    pe.wait_ge(*emptied(("o", l, b, NQ[l] - 1)))
                else:
                    pe.wait_ge(*at(("onorm", l, b)))
                for c in range(2):
                    pe.wait_ge(*room(("y", l, b, c)))
                    acc = psum(("y", l, b, c))
                    for t in range(NQ[l]):
                        mm = pe.transpose(acc[:, t * P:(t + 1) * P], o_sb[:, t, c * P:(c + 1) * P], ident)
                    mm.then_inc(fullsem(("y", l, b, c)), 1)

            pe.wait_ge(S["x_in"], 16 * 2)
            for k in range(KT):
                if k >= 4:
                    pe.wait_ge(*room(("x", k)))
                acc = psum(("x", k))
                for t in range(NT):
                    mm = pe.transpose(acc[:, t * P:(t + 1) * P], xin[:, t, k * P:(k + 1) * P], ident)
                mm.then_inc(fullsem(("x", k)), 1)
            for i in range(2 * DEPTH):
                pe.wait_ge(*room(("vec", i)))
                acc = psum(("vec", i))
                nr = VA_ROWS if i % 2 == 0 else VB_ROWS
                pe.transpose(acc[:, 0:nr], rows[0:nr, i], ident[0:nr, 0:nr]).then_inc(fullsem(("vec", i)), 1)
            pe.wait_ge(S["set0"], 1)

            for l in range(DEPTH):
                pe.wait_ge(*room(("mod", l)))
                acc = psum(("mod", l))
                with pe.Fori(0, MODT // 4) as i:
                    for u in range(4):
                        key = ("mod", l, u)
                        pe.wait_ge(*landed(key, i))
                        for k in range(KT):
                            mm = pe.matmul(acc[:, bass.ds(8 * i + 2 * u, 2)], slot(key)[:, k], cs[:, :, k], start=k == 0, stop=k == KT - 1)
                        mm.then_inc(S["chunk_done"], 1)
                norm(l, 1)
                pe.wait_ge(*at(("h", l, 1, KT - 1)))
                for b in ("ret", "gla", "gqa", "dif"):
                    for n, c in enumerate(BR[b]["feat"]):
                        projection(("f", l, b, n), hT, W[l] if is_q(b, n) else T, M=32 if c == 2048 else P)
                    for n in range(len(BR[b]["tok"])):
                        token_projection(("t", l, b, n), NQ[l] if n >= 2 else NT)
                    if b == "gla":
                        gla(l)
                    else:
                        prep_tiles(l, b)
                        pe.wait_ge(*emptied(("t", l, b, len(BR[b]["tok"]) - 1)))
                        pe.wait_ge(*emptied(("t", l, b, max(0, len(BR[b]["tok"]) - 2))))
                        if b == "ret":
                            retention(l)
                        else:
                            softmax(l, b)
                    turn_outputs(l, b)
                pe.wait_ge(*emptied(("y", l, "dif", 0)))
                pe.wait_ge(*emptied(("y", l, "dif", 1)))
                with pe.Fori(0, 2) as i:
                    for u in range(4):
                        for b in range(4):
                            projection(("g", l, u, b), hT, W[l], i)
                        pe.wait_ge(*landed(("g", l, u, 4), i))
                        for b in range(4):
                            pe.wait_ge(*room(("yb", l, u, b), i))
                            acc = psum(("yb", l, u, b))
                            for x, y in segs(W[l]):
                                for k in range(2):
                                    mm = pe.matmul(acc[:, x:y], slot(("g", l, u, 4))[:, 2 * b + k], yT[:, 2 * b + k, x:y],
                                                   start=k == 0, stop=k == 1)
                            mm.then_inc(fullsem(("yb", l, u, b)) if b < 3 else S["chunk_done"], 1)
                pe.wait_ge(*at(("merged", l, 3), 1))
                with pe.Fori(0, 2) as i:
                    for u in range(4):
                        projection(("out", l, u), mT, W[l], i)
                norm(l, 2)
                pe.wait_ge(*at(("h", l, 2, KT - 1)))
                with pe.Fori(0, FT // 2) as i:
                    for u in range(4):
                        projection(("up", l, u), hT, W[l], i)
                pe.wait_ge(*emptied(("up", l, 3), FT // 2 - 1))
                with pe.Fori(0, 2) as i:
                    for u in range(4):
                        pe.wait_ge(*room(("down", l, u), i))
                        acc = psum(("down", l, u))
                        for j in range(3):
                            key = ("down", l, u, j)
                            pe.wait_ge(*landed(key, i))
                            for x, y in segs(W[l]):
                                for k in range(min(8, FT - 8 * j)):
                                    mm = pe.matmul(acc[:, x:y], slot(key)[:, k], ff[:, 8 * j + k, x:y],
                                                   start=j == 0 and k == 0, stop=8 * j + k == FT - 1)
                            mm.then_inc(S["chunk_done"], 1)
            pe.wait_ge(*emptied(("down", last, 3), 1))
            for t in range(TL):
                pe.wait_ge(*room(("final", t)))
                acc = psum(("final", t))
                for k in range(KT):
                    mm = pe.transpose(acc[:, k * P:(k + 1) * P], xT[:, k, t * P:(t + 1) * P], ident)
                mm.then_inc(fullsem(("final", t)), 1)

        @block.scalar
        def _(act):
            link = Chain(act, S["act"])
            for dst, src in loads:
                act.dma_start(dst, src).then_inc(S["consts"], 16)
            act.wait_ge(S["set7"], 1)
            for dst, src in late_loads:
                act.dma_start(dst, src).then_inc(S["consts"], 16)
            for k in range(KT):
                act.wait_ge(*filled(("x", k)))
                acc = psum(("x", k))
                act.activation(xT[:, k], acc[:, 0:T], ACT.Copy).then_inc(freed(("x", k)), 1)
            act.wait_ge(*emptied(("vec", 1)))
            act.activation(tiny[:, 40:56], vec[:, 1, VB_C:VB_C + 2 * KT], ACT.Silu).then_inc(S["set0"], 1)
            act.wait_ge(S["set1"], 1)
            link(act.activation(pp1, pp1, ACT.Exp))
            act.activation(lamt, lamt, ACT.Exp).then_inc(S["set2"], 1)
            act.activation(pp1, pp1, ACT.Ln, bias=1.0).then_inc(S["set3"], 1)

            def norm(l, which):
                w = W[l] if which == 2 else T
                act.wait_ge(*filled(("norm", l, which)))
                acc = psum(("norm", l, which))
                act.activation(rs[:, 0:w], acc[:, 0:w], ACT.Sqrt, bias=eps).then_inc(freed(("norm", l, which)), 1)
                act.wait_ge(*at(("modr", l)))
                for k in range(KT):
                    act.wait_ge(*at(("scaled", l, which, k)))
                    for s, (x, y) in enumerate(segs(w)):
                        ins = act.activation(hT[:, k, x:y], tb[:, k % 2, x:y], ACT.Identity,
                                             scale=a1[:, which - 1, k, s:s + 1],
                                             bias=modv[:, 24 * (which - 1) + k, s:s + 1])
                    ins.then_inc(sem(("h", l, which, k)), 1)

            def out_of_psum(dst, key, w, scale=1.0):
                act.wait_ge(*filled(key))
                acc = psum(key)
                act.activation(dst, acc[0:dst.shape[0], 0:w], ACT.Copy, scale=scale).then_inc(freed(key), 1)

            def softmax(l, b):
                maps = 2 if b == "dif" else 1
                scale = (32 if b == "dif" else 64) ** -0.5
                order = [(t, h) for t in range(NQ[l]) for h in range(4)]

                def transposed(n):
                    t, h = order[n]
                    lo = 0 if t < TL else LAT
                    if n >= 2:
                        act.wait_ge(*at(("pv", l, b, *order[n - 2])))
                    act.wait_ge(*filled(("pt", l, b, t, h)))
                    acc = psum(("pt", l, b, t, h))
                    act.activation(pt_s[:, h % 2, lo:T], acc[:, lo:T], ACT.Copy).then_inc(freed(("pt", l, b, t, h)), 1)

                for n, (t, h) in enumerate(order):
                    lo = 0 if t < TL else LAT
                    if n >= 2:
                        act.wait_ge(*filled(("pt", l, b, *order[n - 2])))
                    for m in range(maps):
                        key = ("s", l, b, t, h, m)
                        act.wait_ge(*at(("max", l, b, t, h, m)))
                        c = (h * maps + m) % 8
                        act.activation(prob[:, h % 2, m, lo:T], pair[fill[key][0]][:, lo:T], ACT.Exp, scale=scale,
                                       bias=nmx[:, c:c + 1],
                                       accum_out=rsum[t % 2][:, 4 * m + h:4 * m + h + 1]).then_inc(freed(key), 1)
                    if b == "dif" and n >= 1:
                        transposed(n - 1)
                if b == "dif":
                    transposed(len(order) - 1)

            def gla(l):
                for t in range(NT):
                    ts = slice(t * P, (t + 1) * P)
                    act.wait_ge(*at(("abs", l, t)))
                    link(act.activation(G["ab"], G["ab"], ACT.Exp))
                    act.activation(G["ab"], G["ab"], ACT.Ln, bias=1.0).then_inc(sem(("ln", l, t)), 1)
                    act.wait_ge(*filled(("cum", l, t)))
                    acc = psum(("cum", l, t))
                    cum = acc[:, 0:512].rearrange("p (c t) -> p c t", c=4)
                    act.activation(bT[:, :, ts], cum, ACT.Copy)
                    act.activation(el[:, 0:2, t:t + 1], cum[:, 0:2, P - 1:P], ACT.Exp)
                    act.activation(el[:, 2:4, t:t + 1], cum[:, 2:4, 0:1], ACT.Exp).then_inc(freed(("cum", l, t)), 1)
                    act.wait_ge(*filled(("rest", l, t)))
                    acc = psum(("rest", l, t))
                    act.activation(G["ex"], acc[:, 0:512], ACT.Exp).then_inc(freed(("rest", l, t)), 1)
                act.wait_ge(*emptied(("U", l, NT - 1)))
                act.wait_ge(*emptied(("cum", l, NT - 1)))
                for t in range(NQ[l]):
                    act.activation(G["eb"].rearrange("p d c t -> p (d c) t"), bT[:, :, t * P:(t + 1) * P], ACT.Exp).then_inc(
                        sem(("eb", l, t)), 1)
                    for n in range(len(LEVELS)):
                        act.wait_ge(*at(("dd", l, t, n)))
                        act.activation(G["dd"][n % 2], G["dd"][n % 2], ACT.Exp).then_inc(sem(("e", l, t, n)), 1)

            for l in range(DEPTH):
                norm(l, 1)
                for b in ("ret", "gla", "gqa", "dif"):
                    for n, c in enumerate(BR[b]["feat"]):
                        w = W[l] if is_q(b, n) else T
                        M = 32 if c == 2048 else P
                        act.wait_ge(*filled(("f", l, b, n)))
                        acc = psum(("f", l, b, n))
                        act.activation(q[0:M, n, 0:w], acc[0:M, 0:w], ACT.Copy,
                                       scale=0.125 if b == "gla" and is_q(b, n) else 1.0).then_inc(freed(("f", l, b, n)), 1)
                    for n in range(len(BR[b]["tok"])):
                        nt = NQ[l] if n >= 2 else NT
                        act.wait_ge(*filled(("t", l, b, n)))
                        acc = psum(("t", l, b, n))
                        act.activation(v[:, n, 0:nt].rearrange("p n t -> p (n t)"), acc[:, 0:nt * P], ACT.Copy).then_inc(
                            freed(("t", l, b, n)), 1)
                    if b == "ret":
                        for h in range(4):
                            act.wait_ge(*at(("sti", l, h)))
                            act.activation(e0, e0, ACT.Exp)
                            act.activation(e1, e1, ACT.Exp, scale=-1.0)
                            act.activation(strip[:, h, NEAR:], dist[:, NEAR:NEAR + FAR], ACT.Exp,
                                           scale=lg[:, 8 * l + h:8 * l + h + 1])
                            act.activation(e2, dist[:, NEAR + FAR:], ACT.Exp,
                                           scale=lg[:, 8 * l + 4 + h:8 * l + 5 + h]).then_inc(sem(("ste", l, h)), 1)
                    if b in ("gqa", "dif"):
                        for n in range(len(BR[b]["feat"])):
                            w = W[l] if is_q(b, n) else T
                            act.wait_ge(*filled(("qkn", l, b, n)))
                            acc = psum(("qkn", l, b, n))
                            act.activation(prep[:, 1, 0:w], acc[:, 0:w], ACT.Sqrt, bias=eps).then_inc(
                                freed(("qkn", l, b, n)), 1)
                        if b == "gqa":
                            out_of_psum(q[:, 3, :], ("swap", l), T)
                        softmax(l, b)
                    if b == "gla":
                        gla(l)
                    if b != "gqa":
                        act.wait_ge(*at(("osq", l, b)))
                        act.activation(oss[:, 0:4 * NQ[l]], oss[:, 0:4 * NQ[l]], ACT.Sqrt, scale=1.0 / 64,
                                       bias=eps).then_inc(sem(("oroot", l, b)), 1)
                    if b in ("ret", "gla"):
                        for c in range(2):
                            act.wait_ge(*emptied(("t", l, b, 2 + c)))
                        act.activation(v[:, 2:4, 0:NQ[l]], v[:, 2:4, 0:NQ[l]], ACT.Silu).then_inc(sem(("osilu", l, b)), 1)
                    for c in range(2):
                        out_of_psum(yT[:, 2 * BR[b]["n"] + c, 0:W[l]], ("y", l, b, c), W[l])
                with act.Fori(0, 2) as i:
                    for u in range(4):
                        for b in range(4):
                            p, n, per, _ = fill[("yb", l, u, 1)]
                            act.wait_ge(S[f"freed{p}"], n + per * i)
                            act.wait_ge(*filled(("g", l, u, b), i))
                            acc = psum(("g", l, u, b))
                            act.activation(sig[:, b, 0:W[l]], acc[:, 0:W[l]], ACT.Sigmoid).then_inc(freed(("g", l, u, b)), 1)
                norm(l, 2)
                cb, cw = vec[:, 2 * l, VA_CB:VA_CB + FT], vec[:, 2 * l + 1, VB_CW:VB_CW + 3 * FT]
                with act.Fori(0, FT // 2) as i:
                    for u in range(2):
                        p, n, per, _ = fill[("up", l, 2 * u + 1)]
                        act.wait_ge(S[f"freed{p}"], n + per * i)
                        act.wait_ge(*filled(("up", l, 2 * u), i))
                        acc = psum(("up", l, 2 * u))
                        act.activation(conv[:, u, 0:W[l]], acc[:, 0:W[l]], ACT.Identity,
                                       scale=cw[:, bass.ds(FT + 2 * i + u, 1)],
                                       bias=cb[:, bass.ds(2 * i + u, 1)]).then_inc(sem(("cc", l, u)), 1)
                        act.wait_ge(*emptied(("up", l, 2 * u), i))
                        act.activation(conv[:, u, 0:W[l]], conv[:, u, 0:W[l]], ACT.Silu).then_inc(sem(("cs", l, u)), 1)
            for t in range(TL):
                act.wait_ge(*at(("fr", t)))
                act.dma_start(out[0, t * P:(t + 1) * P, :], res[:, t]).then_inc(S["out_done"], 16)

        @block.vector
        def _(dve):
            link = Chain(dve, S["dve"])
            dve.memset(eps, EPS)
            dve.memset(gate_up[:], 0.0).then_inc(S["set7"], 1)
            dve.wait_ge(S["consts"], 16 * N_CONST)
            link(dve.tensor_copy(mask[:].rearrange("p d l t -> p (d l t)"), mask_in))
            for i in range(2 * DEPTH):
                dve.wait_ge(*filled(("vec", i)))
                acc = psum(("vec", i))
                nr = VA_ROWS if i % 2 == 0 else VB_ROWS
                dve.tensor_copy(vec[:, i, 0:nr], acc[:, 0:nr]).then_inc(freed(("vec", i)), 1)
                dve.wait_ge(*emptied(('vec', i)))
            dve.scalar_tensor_tensor(out=pp1, in0=decay[:], scalar=-1.0, in1=decay[:], op0=ALU.mult, op1=ALU.min)
            lv = lams[:].rearrange("p (a b d) -> p a b d", b=2, d=32)
            link(dve.tensor_tensor(lv[:, :, 0], lv[:, :, 0], lv[:, :, 1], ALU.mult))
            dve.tensor_reduce(lamt, lv[:, :, 0], AX, ALU.add).then_inc(S["set1"], 1)
            dve.wait_ge(S["set3"], 1)
            link(dve.scalar_tensor_tensor(out=lg, in0=decay[:], scalar=0.0, in1=pp1, op0=ALU.min, op1=ALU.subtract))
            for l in range(DEPTH):
                init = 0.8 - 0.6 * math.exp(-0.3 * l)
                link(dve.tensor_tensor(neg_lam[:, l:l + 1], lamt[:, 2 * l + 1:2 * l + 2], lamt[:, 2 * l:2 * l + 1], ALU.subtract))
                link(dve.tensor_scalar(neg_lam[:, l:l + 1], neg_lam[:, l:l + 1], -init, None, ALU.add))
                link(dve.tensor_scalar(onorm[:, 1, l], onorm[:, 1, l], 1.0 - init, None, ALU.mult))

            def modulation(l):
                dve.wait_ge(*filled(("mod", l), MODT // 4 - 1, ck=("mod", l, 3)))
                acc = psum(("mod", l))
                dve.tensor_tensor(modv[:], acc[:, 0:2 * MODT].rearrange("p (m s) -> p m s", s=2),
                                  vec[:, 2 * l, VA_BMOD:VA_BMOD + MODT].unsqueeze(2).to_broadcast([P, MODT, 2]),
                                  ALU.add).then_inc(freed(("mod", l)), 1)
                dve.wait_ge(*emptied(("mod", l)))
                for w in range(2):
                    nv = vec[:, 2 * l, VA_N1 + KT * w:VA_N1 + KT * (w + 1)].unsqueeze(2).to_broadcast([P, KT, 2])
                    ins = dve.scalar_tensor_tensor(out=a1[:, w], in0=modv[:, 24 * w + 8:24 * w + 16], scalar=1.0, in1=nv,
                                                   op0=ALU.add, op1=ALU.mult)
                ins.then_inc(sem(("modr", l)), 1)
                dve.wait_ge(*at(('modr', l)))

            def norm(l, which):
                w = W[l] if which == 2 else T
                for k in range(KT):
                    if l == 0 and which == 1:
                        dve.wait_ge(*emptied(("x", k)))
                    if k >= 2:
                        dve.wait_ge(*at(("squ", l, which, k - 2)))
                    dve.tensor_tensor(sqb[:, k % 2, 0:w], xT[:, k, 0:w], xT[:, k, 0:w], ALU.mult).then_inc(
                        sem(("sq", l, which, k)), 1)
                    dve.wait_ge(*at(('sq', l, which, k)))
                dve.wait_ge(*emptied(("norm", l, which)))
                link(dve.reciprocal(rs[:, 0:w], rs[:, 0:w]))
                for k in range(KT):
                    if k >= 2:
                        dve.wait_ge(*at(("h", l, which, k - 2)))
                    dve.tensor_tensor(tb[:, k % 2, 0:w], xT[:, k, 0:w], rs[:, 0:w], ALU.mult).then_inc(
                        sem(("scaled", l, which, k)), 1)
                    dve.wait_ge(*at(('scaled', l, which, k)))

            def prep_tiles(l, b):
                cos_sin = {"ret": 0, "gqa": 2, "dif": 4}[b]
                for n in range(len(BR[b]["feat"])):
                    w = W[l] if is_q(b, n) else T
                    z = q[:, n, 0:w]
                    dve.wait_ge(*emptied(("f", l, b, n)))
                    if b != "ret":
                        dve.tensor_tensor(prep[:, 0, 0:w], z, z, ALU.mult).then_inc(sem(("qksq", l, b, n)), 1)
                        dve.wait_ge(*at(('qksq', l, b, n)))
                        dve.wait_ge(*emptied(("qkn", l, b, n)))
                        link(dve.reciprocal(prep[:, 1, 0:w], prep[:, 1, 0:w]))
                        c = VB_QN + (0 if b == "gqa" else 2) + (0 if is_q(b, n) else 1)
                        dve.scalar_tensor_tensor(out=z, in0=z, scalar=colv(l, 1, c), in1=prep[:, 1, 0:w],
                                                 op0=ALU.mult, op1=ALU.mult).then_inc(sem(("turnable", l, b, n)), 1)
                        dve.wait_ge(*at(("turnable", l, b, n)))
                    dve.wait_ge(*filled(("rope", l, b, n)))
                    acc = psum(("rope", l, b, n))
                    z = q[:, n, 0:LAT]
                    dve.tensor_tensor(prep[:, 1, 0:LAT], acc[:, 0:LAT], rope[:, cos_sin + 1], ALU.mult).then_inc(
                        freed(("rope", l, b, n)), 1)
                    dve.wait_ge(*emptied(('rope', l, b, n)))
                    link(dve.tensor_tensor(z, z, rope[:, cos_sin], ALU.mult))
                    dve.wait_ge(*emptied(("rope", l, b, n)))
                    dve.tensor_tensor(z, z, prep[:, 1, 0:LAT], ALU.add).then_inc(sem(("turned", l, b, n)), 1)
                    dve.wait_ge(*at(('turned', l, b, n)))
                dve.wait_ge(*at(("turned", l, b, len(BR[b]["feat"]) - 1)))

            def strips(l):
                D = dist[:, 0:NEAR]
                for h in range(4):
                    dve.tensor_scalar(e0, D, 0.0, lg[:, 8 * l + h:8 * l + h + 1], ALU.max, ALU.mult)
                    dve.tensor_scalar(e1, D, 0.0, lg[:, 8 * l + 4 + h:8 * l + 5 + h], ALU.min, ALU.mult).then_inc(
                        sem(("sti", l, h)), 1)
                    dve.wait_ge(*at(("ste", l, h)))
                    link(dve.scalar_tensor_tensor(out=strip[:, h, 0:NEAR], in0=D, scalar=0.0, in1=e0, op0=ALU.is_ge, op1=ALU.mult))
                    link(dve.scalar_tensor_tensor(out=e1, in0=D, scalar=0.0, in1=e1, op0=ALU.is_le, op1=ALU.mult))
                    link(dve.tensor_tensor(strip[:, h, 0:NEAR], strip[:, h, 0:NEAR], e1, ALU.add))
                    link(dve.tensor_tensor(strip[:, h, NEAR:], strip[:, h, NEAR:], e2, ALU.add))

            def retention(l):
                b = "ret"
                order = [(t, h) for t in range(NQ[l]) for h in range(4)]
                for n, (t, h) in enumerate(order):
                    key = ("s", l, b, t, h)
                    if n >= 2:
                        dve.wait_ge(*at(("pv", l, b, *order[n - 2])))
                    dve.wait_ge(*filled(key))
                    acc = psum(key)
                    pt = pt_r[:, h % 2]
                    if t < TL:
                        dve.scalar_tensor_tensor(out=pt[:, 0:LAT], in0=acc[:, 0:LAT], scalar=0.125,
                                                 in1=strip[:, h, P * (3 - t):P * (3 - t) + LAT], op0=ALU.mult, op1=ALU.mult)
                        far = strip[:, h, NEAR + P * (3 - t):NEAR + P * (3 - t) + CTX]
                    else:
                        far = strip[:, h, P * (3 - t + TL):P * (3 - t + TL) + CTX]
                    dve.scalar_tensor_tensor(out=pt[:, LAT:T], in0=acc[:, LAT:T], scalar=0.125, in1=far,
                                             op0=ALU.mult, op1=ALU.mult).then_inc(freed(key), 1)
                    dve.wait_ge(*emptied(key))
                    if h == 0 and t > 0:
                        output(l, b, t - 1)
                output(l, b, NQ[l] - 1)

            def output(l, b, t):
                dve.wait_ge(*filled(("o", l, b, t)))
                acc = psum(("o", l, b, t))
                if b == "gla":
                    src = acc[:].rearrange("p (s c d) -> p c s d", s=2, d=64)[:, 0:2]
                else:
                    src = acc[:, 0:256].rearrange("p (c s d) -> p c s d", s=2, d=64)
                dve.tensor_copy(o_sb[:, t].rearrange("p (c s d) -> p c s d", s=2, d=64), src).then_inc(freed(("o", l, b, t)), 1)
                dve.wait_ge(*emptied(('o', l, b, t)))

            def softmax(l, b):
                maps = 2 if b == "dif" else 1
                scale = (32 if b == "dif" else 64) ** -0.5
                order = [(t, h) for t in range(NQ[l]) for h in range(4)]

                def maxima(n):
                    t, h = order[n]
                    lo = 0 if t < TL else LAT
                    for m in range(maps):
                        c = (h * maps + m) % 8
                        dve.wait_ge(*filled(("s", l, b, t, h, m)))
                        acc = psum(("s", l, b, t, h, m))
                        link(dve.tensor_reduce(nmx[:, c:c + 1], acc[:, lo:T], AX, ALU.max))
                        dve.tensor_scalar(nmx[:, c:c + 1], nmx[:, c:c + 1], -scale, None, ALU.mult).then_inc(
                            sem(("max", l, b, t, h, m)), 1)
                        dve.wait_ge(*at(('max', l, b, t, h, m)))

                def normalised(t):
                    dve.wait_ge(*filled(("o", l, b, t)))
                    acc = psum(("o", l, b, t))
                    r = rd[:, 4 * (t % 2):4 * (t % 2) + 4]
                    link(dve.reciprocal(r, rsum[t % 2][:, 0:4]))
                    dve.tensor_tensor(o_sb[:, t].rearrange("p (h d) -> p h d", d=64),
                                      acc[:, 0:256].rearrange("p (h d) -> p h d", d=64),
                                      r.unsqueeze(2).to_broadcast([P, 4, 64]), ALU.mult).then_inc(freed(("o", l, b, t)), 1)
                    dve.wait_ge(*emptied(('o', l, b, t)))

                maxima(0)
                for n, (t, h) in enumerate(order):
                    lo = 0 if t < TL else LAT
                    if n + 1 < len(order):
                        maxima(n + 1)
                    if b == "dif":
                        for m in range(2):
                            dve.wait_ge(*emptied(("s", l, b, t, h, m)))
                        s0, s1 = (rsum[t % 2][:, 4 * m + h:4 * m + h + 1] for m in range(2))
                        r = rd[:, 16 + h:17 + h]
                        link(dve.reciprocal(r, s1))
                        link(dve.scalar_tensor_tensor(out=r, in0=r, scalar=s0, in1=neg_lam[:, l:l + 1], op0=ALU.mult, op1=ALU.mult))
                        dve.scalar_tensor_tensor(out=prob[:, h % 2, 0, lo:T], in0=prob[:, h % 2, 1, lo:T], scalar=r,
                                                 in1=prob[:, h % 2, 0, lo:T], op0=ALU.mult, op1=ALU.add).then_inc(
                            sem(("dif", l, b, t, h)), 1)
                        dve.wait_ge(*at(('dif', l, b, t, h)))
                    else:
                        if n >= 2:
                            dve.wait_ge(*at(("pv", l, b, *order[n - 2])))
                        dve.wait_ge(*filled(("pt", l, b, t, h)))
                        acc = psum(("pt", l, b, t, h))
                        dve.tensor_copy(pt_s[:, h % 2, lo:T], acc[:, lo:T]).then_inc(freed(("pt", l, b, t, h)), 1)
                        dve.wait_ge(*emptied(('pt', l, b, t, h)))
                    if h == 0 and t > 0:
                        normalised(t - 1)
                normalised(NQ[l] - 1)

            def gla(l):
                for n in range(len(BR["gla"]["feat"])):
                    dve.wait_ge(*emptied(("f", l, "gla", n)))
                for t in range(NT):
                    dve.wait_ge(*filled(("logit", l, t)))
                    acc = psum(("logit", l, t))
                    dve.tensor_tensor(G["lx"], acc[:, 0:512], gate_b[:, l], ALU.add).then_inc(freed(("logit", l, t)), 1)
                    dve.wait_ge(*emptied(("logit", l, t)))
                    dve.scalar_tensor_tensor(out=G["ab"], in0=G["lx"], scalar=-1.0, in1=G["lx"], op0=ALU.mult, op1=ALU.min).then_inc(sem(("abs", l, t)), 1)
                    dve.wait_ge(*at(("ln", l, t)))
                    dve.scalar_tensor_tensor(out=G["la"], in0=G["lx"], scalar=0.0, in1=G["ab"], op0=ALU.min,
                                             op1=ALU.subtract).then_inc(sem(("la", l, t)), 1)
                    dve.wait_ge(*at(('la', l, t)))
                    dve.wait_ge(*filled(("ktok", l, t)))
                    acc = psum(("ktok", l, t))
                    dve.wait_ge(*emptied(("rest", l, t)))
                    for d in range(2):
                        ins = dve.tensor_tensor(G["kd"][:, 256 * d:256 * d + 256], acc[:, 0:256],
                                                G["ex"][:, 256 * d:256 * d + 256], ALU.mult)
                    ins.then_inc(freed(("ktok", l, t)), 1)
                    dve.wait_ge(*emptied(('ktok', l, t)))
                    dve.wait_ge(*filled(("U", l, t)))
                    acc = psum(("U", l, t))
                    blocks = acc[:, 0:512].rearrange("p (c n) -> p c n", c=4)
                    dve.tensor_copy(G["U"][0:64, t], blocks[0:64, :, 0:64])
                    dve.tensor_copy(G["U"][64:128, t], blocks[64:128, :, 64:128]).then_inc(freed(("U", l, t)), 1)
                    dve.wait_ge(*emptied(('U', l, t)))
                dve.wait_ge(*emptied(("U", l, NT - 1)))
                dve.wait_ge(*emptied(("cum", l, NT - 1)))
                orders = ([4, 5, 0, 1, 2, 3], [5, 4, 3, 2, 1, 0])
                for d in range(2):
                    link(dve.memset(G["S"][:, orders[d][0], 2 * d:2 * d + 2], 0.0))
                for s in range(NT - 1):
                    for d in range(2):
                        cur, nxt = orders[d][s], orders[d][s + 1]
                        for c in (2 * d, 2 * d + 1):
                            link(dve.scalar_tensor_tensor(out=G["S"][:, nxt, c], in0=G["S"][:, cur, c],
                                                          scalar=el[:, c, cur:cur + 1], in1=G["U"][:, cur, c],
                                                          op0=ALU.mult, op1=ALU.add))
                for t in range(NQ[l]):
                    ts = slice(t * P, (t + 1) * P)
                    qt = q[:, 0:2, ts].unsqueeze(1).to_broadcast([P, 2, 2, P])
                    kt = q[:, 2:4, ts].unsqueeze(1).to_broadcast([P, 2, 2, P])

                    def exponents(n):
                        h = LEVELS[n]
                        for d in range(2):
                            bb = bT[:, 2 * d:2 * d + 2, ts].rearrange("p c (n s h) -> p c n s h", s=2, h=h)
                            dd = G["dd"][n % 2][:, d].rearrange("p c (n s h) -> p c n s h", s=2, h=h)
                            lo, up = bb[:, :, :, 0], bb[:, :, :, 1]
                            ref = (lo[..., h - 1:h] if d == 0 else up[..., 0:1]).to_broadcast([P, 2, P // (2 * h), h])
                            q_half, k_half = (1, 0) if d == 0 else (0, 1)
                            dve.tensor_tensor(dd[:, :, :, q_half], bb[:, :, :, q_half], ref, ALU.subtract)
                            ins = dve.tensor_tensor(dd[:, :, :, k_half], ref, bb[:, :, :, k_half], ALU.subtract)
                        ins.then_inc(sem(("dd", l, t, n)), 1)
                        dve.wait_ge(*at(('dd', l, t, n)))

                    def select(n):
                        dve.wait_ge(*filled(("lev", l, t, n)))
                        acc = psum(("lev", l, t, n))
                        for d in range(2):
                            ins = dve.copy_predicated(G["pt"], mask[:, d, n].unsqueeze(1).unsqueeze(1).to_broadcast([P, 2, 2, P]),
                                                      acc[:].rearrange("p (s d c t) -> p d s c t", s=2, d=2, c=2)[:, d])
                            if d == 0:
                                link(ins)
                        ins.then_inc(freed(("lev", l, t, n)), 1)
                        dve.wait_ge(*emptied(("lev", l, t, n)))

                    dve.wait_ge(*at(("eb", l, t)))
                    dve.tensor_tensor(G["qe"], qt, G["eb"], ALU.mult)
                    exponents(0)
                    dve.wait_ge(*filled(("diag", l, t)))
                    acc = psum(("diag", l, t))
                    dve.tensor_tensor(G["pt"], acc[:].rearrange("p (s c t) -> p s c t", s=2, t=P)[:, :, 0:2],
                                      K["two"].unsqueeze(1).unsqueeze(1).to_broadcast([P, 2, 2, P]), ALU.mult).then_inc(freed(("diag", l, t)), 1)
                    dve.wait_ge(*emptied(("diag", l, t)))
                    for n in range(len(LEVELS)):
                        if n + 1 < len(LEVELS):
                            exponents(n + 1)
                        dve.wait_ge(*at(("e", l, t, n)))
                        dve.tensor_tensor(G["ql"][n % 2], qt, G["dd"][n % 2], ALU.mult)
                        dve.tensor_tensor(G["kl"][n % 2], kt, G["dd"][n % 2], ALU.mult).then_inc(sem(("qk", l, t, n)), 1)
                        dve.wait_ge(*at(('qk', l, t, n)))
                        if n >= 1:
                            select(n - 1)
                    select(len(LEVELS) - 1)
                    output(l, "gla", t)

            def finish(l, b):
                nq = NQ[l]
                dve.wait_ge(*emptied(("o", l, b, nq - 1)))
                if b == "gqa":
                    return
                o4 = o_flat[:, 0:256 * nq].rearrange("p (g d) -> p g d", d=64)
                sq4 = prep_flat[:, 0:256 * nq].rearrange("p (g d) -> p g d", d=64)
                link(dve.tensor_tensor(sq4, o4, o4, ALU.mult))
                dve.tensor_reduce(oss[:, 0:4 * nq], sq4, AX, ALU.add).then_inc(sem(("osq", l, b)), 1)
                dve.wait_ge(*at(("oroot", l, b)))
                link(dve.reciprocal(oss[:, 0:4 * nq], oss[:, 0:4 * nq]))
                ins = dve.tensor_tensor(o4, o4, oss[:, 0:4 * nq].unsqueeze(2).to_broadcast([P, 4 * nq, 64]), ALU.mult)
                if b != "ret":
                    link(ins)
                    ins = dve.tensor_tensor(o4, o4, onorm[:, 0 if b == "gla" else 1, l].unsqueeze(1).to_broadcast([P, 4 * nq, 64]),
                                            ALU.mult)
                if b != "dif":
                    link(ins)
                    dve.wait_ge(*at(("osilu", l, b)))
                    oc = o_sb[:, 0:nq].rearrange("p t (c n) -> p c t n", c=2)
                    ins = dve.tensor_tensor(oc, oc, v[:, 2:4, 0:nq], ALU.mult)
                ins.then_inc(sem(("onorm", l, b)), 1)
                dve.wait_ge(*at(('onorm', l, b)))

            def residual(kind, l):
                g0 = 16 if kind == "out" else 40
                segments = segs(W[l])
                with dve.Fori(0, 2) as i:
                    for u in range(4):
                        key = (kind, l, u)
                        dve.wait_ge(*filled(key, i, ck=key if kind == "out" else ("down", l, u, 2)))
                        acc = psum(key)
                        for s, (x, y) in enumerate(segments):
                            xs = xT[:, bass.ds(4 * i + u, 1), x:y].squeeze(1)
                            ins = dve.scalar_tensor_tensor(out=xs, in0=acc[:, x:y],
                                                           scalar=modv[:, bass.ds(g0 + 4 * i + u, 1), s], in1=xs,
                                                           op0=ALU.mult, op1=ALU.add)
                        ins.then_inc(freed(key), 1)
                        dve.wait_ge(*emptied(key, i))
                for u in range(4):
                    dve.wait_ge(*emptied((kind, l, u), 1))

            for l in range(DEPTH):
                modulation(l)
                norm(l, 1)
                for b in ("ret", "gla", "gqa", "dif"):
                    if b == "ret":
                        strips(l)
                    if b == "gla":
                        gla(l)
                    else:
                        prep_tiles(l, b)
                        retention(l) if b == "ret" else softmax(l, b)
                    finish(l, b)
                w = W[l]
                per = 4 * 2
                with dve.Fori(0, 2) as i:
                    link.enter(i, per)
                    for u in range(4):
                        m = mT[:, bass.ds(4 * i + u, 1), 0:w].squeeze(1)
                        for b in range(4):
                            key = ("yb", l, u, b)
                            dve.wait_ge(*emptied(("g", l, u, b), i))
                            dve.wait_ge(*filled(key, i, ck=("g", l, u, 4)))
                            acc = psum(key)
                            if b == 0:
                                dve.tensor_tensor(m, acc[:, 0:w], sig[:, b, 0:w], ALU.mult).then_inc(freed(key), 1)
                                dve.wait_ge(*emptied(key, i))
                            else:
                                dve.tensor_tensor(prod[:, 0:w], acc[:, 0:w], sig[:, b, 0:w], ALU.mult).then_inc(freed(key), 1)
                                dve.wait_ge(*emptied(key, i))
                                ins = dve.tensor_tensor(m, m, prod[:, 0:w], ALU.add)
                                if b < 3:
                                    link(ins)
                                else:
                                    ins.then_inc(sem(("merged", l, u)), 1)
                                    dve.wait_ge(*at(("merged", l, u), i))
                    link.leave(2)
                residual("out", l)
                norm(l, 2)
                cw = vec[:, 2 * l + 1, VB_CW:VB_CW + 3 * FT]
                with dve.Fori(0, FT // 2) as i:
                    link.enter(i, 2 * len(segs(w)))
                    for u in range(2):
                        dve.wait_ge(*filled(("up", l, 2 * u), i))
                        acc = psum(("up", l, 2 * u))
                        dve.wait_ge(*at(("cc", l, u), i))
                        cu = conv[:, u]
                        for x, y in segs(w):
                            left = dve.scalar_tensor_tensor(out=cu[:, x + 1:y], in0=acc[:, x:y - 1],
                                                            scalar=cw[:, bass.ds(2 * i + u, 1)], in1=cu[:, x + 1:y],
                                                            op0=ALU.mult, op1=ALU.add)
                            link(left)
                        for x, y in segs(w):
                            right = dve.scalar_tensor_tensor(out=cu[:, x:y - 1], in0=acc[:, x + 1:y],
                                                             scalar=cw[:, bass.ds(2 * FT + 2 * i + u, 1)], in1=cu[:, x:y - 1],
                                                             op0=ALU.mult, op1=ALU.add)
                        right.then_inc(freed(("up", l, 2 * u)), 1)
                        dve.wait_ge(*emptied(('up', l, 2 * u), i))
                        dve.wait_ge(*at(("cs", l, u), i))
                        dve.wait_ge(*filled(("up", l, 2 * u + 1), i))
                        acc = psum(("up", l, 2 * u + 1))
                        dve.tensor_tensor(ff[:, bass.ds(2 * i + u, 1), 0:w].squeeze(1), cu[:, 0:w], acc[:, 0:w],
                                          ALU.mult).then_inc(freed(("up", l, 2 * u + 1)), 1)
                        dve.wait_ge(*emptied(('up', l, 2 * u + 1), i))
                    link.leave(FT // 2)
                residual("down", l)
            for t in range(TL):
                dve.wait_ge(*filled(("final", t)))
                acc = psum(("final", t))
                dve.tensor_copy(res[:, t], acc[:, 0:D]).then_inc(sem(("fr", t)), 1)
                dve.wait_ge(*at(('fr', t)))


_INS = ["x", "c", "ctx", "c_ctx", "w_mod", "b_mod", "norm1", "norm2", "w_in", "ret_decay", "gla_gate_up", "gla_gate_b",
        "gla_norm", "gqa_qnorm", "gqa_knorm", "dif_qnorm", "dif_knorm", "dif_lambda", "dif_subln", "w_branch", "w_out",
        "w_up", "conv_w", "conv_b", "w_down"]


def kernel(**inputs):
    import concourse.bacc as bacc
    from concourse.bass_utils import run_bass_kernel_spmd as run

    nc = bacc.Bacc("TRN2", target_bir_lowering=False, num_devices=1)
    arrays, args = {}, {}
    given = {name: np.ascontiguousarray(inputs[name]) for name in _INS}
    for name, a in {**given, **constants()}.items():
        arrays[f"in_{name}"] = a
        args[name] = nc.dram_tensor(f"in_{name}", a.shape, mybir.dt.from_np(a.dtype), kind="ExternalInput").ap()
    out = nc.dram_tensor("out_0", (1, LAT, D), F32, kind="ExternalOutput").ap()
    bass_hybrid_backbone(nc, args, out)
    r = run(nc, [arrays], core_ids=[0])
    return r.results[0]["out_0"]
```

```python
import math
from contextlib import ExitStack

import numpy as np
import concourse.bass as bass
import concourse.mybir as mybir
from concourse.alu_op_type import AluOpType as ALU

F32 = mybir.dt.float32
F32R = mybir.dt.float32r
U8 = mybir.dt.uint8
ACT = mybir.ActivationFunctionType
AX = mybir.AxisListType.X

P = 128
D = 1024
KT = D // P
LAT, CTX = 512, 256
T = LAT + CTX
TL, TC = LAT // P, CTX // P
NT = TL + TC
DEPTH = 2
GRID_W = 64
DFF = 2816
FT = DFF // P
MODT = 6 * D // P
RANK = 16
EPS = 1e-6
GATES = 3360
RING = 4
MOD0 = 16
MODCOL = 768
BEHIND_UP = [(), (0, 1), (2, 3), ()]
LEVELS = [64, 32, 16, 8, 4, 2, 1]

BR = {
    "ret": dict(n=0, feat=[0, 128, 256, 384], nq=2, tok=[512, 640, 768, 896]),
    "gla": dict(n=1, feat=[1024, 1152, 1280, 1408, 2048], nq=2, tok=[1536, 1664, 1792, 1920]),
    "gqa": dict(n=2, feat=[2080, 2208, 2336], nq=2, tok=[2464]),
    "dif": dict(n=3, feat=[2592, 2720, 2848, 2976], nq=2, tok=[3104, 3232]),
}
VA_BMOD, VA_N1, VA_N2, VA_CB, VA_ROWS = 0, MODT, MODT + KT, MODT + 2 * KT, MODT + 2 * KT + FT
VB_CW, VB_C, VB_QN, VB_ROWS = 0, 3 * FT, 3 * FT + 2 * KT, 3 * FT + 2 * KT + 4
SMALL = [("ident", P), ("ones", P), ("sum64", P), ("sum32", P), ("perm64", P), ("perm32", P),
         ("tri", 2 * P), ("rest", 2 * P), ("two", P), ("swap", P)]


def constants():
    f = np.float32
    j, i = np.arange(P)[:, None], np.arange(P)[None, :]
    c = {}
    c["ident"] = (j == i).astype(f)
    c["two"] = 2 * c["ident"]
    c["swap"] = (j == (i + P // 2) % P).astype(f)
    c["ones"] = np.full((P, P), 1.0 / D, f)
    for d in (64, 32):
        c[f"sum{d}"] = (j // d == i // d).astype(f) / d
        half = d // 2
        first = i % d < half
        c[f"perm{d}"] = (((j == i + half) & first) * -1.0 + ((j == i - half) & ~first) * 1.0).astype(f)
    c["tri"] = np.concatenate([(j <= i), (j >= i)], 1).astype(f) / 16
    c["rest"] = np.concatenate([(j > i), (j < i)], 1).astype(f) / 16
    small = np.concatenate([c[n] for n, _ in SMALL], 1).astype(f)

    def rot(ang, dim):
        cs, sn = np.cos(ang).astype(f).T, np.sin(ang).astype(f).T
        reps = P // (dim // 2)
        return np.tile(cs, (reps, 1)), np.tile(sn, (reps, 1))

    freqs = f(10000.0) ** (-np.linspace(0.0, 1.0, 32, dtype=f))
    ret = rot(np.arange(LAT, dtype=f)[:, None] * freqs, 64)

    def axial(dim):
        ax = dim // 2
        fr = f(10000.0) ** (-np.arange(0, ax, 2, dtype=f) / f(ax))
        tok = np.arange(LAT)
        return rot(np.concatenate([(tok // GRID_W).astype(f)[:, None] * fr,
                                   (tok % GRID_W).astype(f)[:, None] * fr], -1), dim)

    rope = np.concatenate([*ret, *axial(64), *axial(32)], 1).astype(f)
    p = np.arange(P)[:, None]
    e = np.arange(7 * P)[None, :]
    dist = (P * (3 - e // P) + e % P - p).astype(f)
    mask = np.zeros((P, 2, len(LEVELS), P), f)
    for n, h in enumerate(LEVELS):
        same = (j // (2 * h)) == (i // (2 * h))
        mask[:, 0, n] = same & (j % (2 * h) < h) & (i % (2 * h) >= h)
        mask[:, 1, n] = same & (j % (2 * h) >= h) & (i % (2 * h) < h)
    return dict(k_small=small, k_rope=rope, k_dist=dist, k_mask=mask.reshape(P, -1))


class Tally:

    def __init__(self):
        self.count, self.at = {}, {}

    def add(self, sem, key, by=1):
        self.count[sem] = self.count.get(sem, 0) + by
        self.at[key] = (sem, self.count[sem], 0)

    def loop(self, keys, iters, by=1):
        per = {}
        for sem, key in keys:
            per[sem] = per.get(sem, 0) + by
        seen = {}
        for sem, key in keys:
            seen[sem] = seen.get(sem, 0) + by
            self.at[key] = (sem, self.count.get(sem, 0) + seen[sem], per[sem])
        for sem, n in per.items():
            self.count[sem] = self.count.get(sem, 0) + n * iters


class Chain:

    def __init__(self, eng, sem):
        self.eng, self.sem, self.n, self.it = eng, sem, 0, None

    def __call__(self, ins):
        ins.then_inc(self.sem, 1)
        self.n += 1
        if self.it is None:
            self.eng.wait_ge(self.sem, self.n)
        else:
            self.eng.wait_ge(self.sem, self.it[0] * self.it[1] + self.n)

    def enter(self, i, per):
        self.it, self.start = (i, per), self.n

    def leave(self, iters):
        i, per = self.it
        assert self.n - self.start == per, (self.n - self.start, per)
        self.n, self.it = self.start + per * iters, None


def schedule(depth=DEPTH):
    ev = Tally()
    chunk, fill, fills = {}, {}, [0] * 4
    nch, turn = [0], [0]
    splits = {}
    ev.add("half_used", ("one",))

    def split_chunks(keys, iters):
        for n, key in enumerate(keys):
            splits[key] = keys[n - 1]
        ev.loop([("split_ready", ("split", key, j)) for key in keys for j in range(2)], iters)
        ev.loop([("half_used", ("half", key)) for key in keys], iters)

    def chunks(keys, iters=1):
        for n, key in enumerate(keys):
            chunk[key] = (nch[0] + n, len(keys) if iters > 1 else 0)
        nch[0] += len(keys) * iters

    def take(key, p, ready=None, iters=1, per=0):
        fill[key] = (p, fills[p], per, ready)
        fills[p] += 1
        if ready is None:
            ev.add(f"full{p}", ("full", key))

    for l in range(depth):
        nq = NT if l < depth - 1 else TL
        if l == 0:
            for k in range(KT):
                take(("x", k), k % 4)
            for i in range(2 * depth):
                take(("vec", i), i % 4)
        if l == 0:
            chunks([("mod", l, u) for u in range(4)], MOD0 // 4)
            ev.add("mod_ready", ("modr", l, 0))
        else:
            chunks([("modx", l, m) for m in range(4 * (FT // 2), MODT)])
            ev.add("mod_ready", ("modr", l, 1))
        for which in (1, 2):
            if which == 2:
                between = between_projections(l)
                for b in ("ret", "gla", "gqa", "dif"):
                    for kind in ("feat", "tok"):
                        for n in range(len(BR[b][kind])):
                            key = (kind[0], l, b, n)
                            chunks([key])
                            take(key, turn[0] % 2, "chunk")
                            turn[0] += 1
                            chunks([("modx", l, m) for m in between.get(key, [])])
                    if b == "ret":
                        for h in range(4):
                            ev.add("strip_exponents", ("sti", l, h))
                            ev.add("strip_exps", ("ste", l, h))
                    if b != "gla":
                        for n in range(len(BR[b]["feat"])):
                            if b != "ret":
                                ev.add("squares", ("qksq", l, b, n))
                                take(("qkn", l, b, n), 2)
                                ev.add("turnable", ("turnable", l, b, n))
                            take(("rope", l, b, n), 3)
                            ev.add("turned", ("turned", l, b, n))
                    if b == "gla":
                        for t in range(NT):
                            take(("logit", l, t), 0)
                            ev.add("gla_abs", ("abs", l, t))
                            ev.add("gla_ln", ("ln", l, t))
                            ev.add("gla_la", ("la", l, t))
                            take(("cum", l, t), 1)
                            take(("rest", l, t), 2)
                            take(("ktok", l, t), 3)
                            take(("U", l, t), 0)
                        for t in range(nq):
                            ev.add("gla_eb", ("eb", l, t))
                            take(("diag", l, t), 2)
                            for n in range(len(LEVELS)):
                                ev.add("gla_dd", ("dd", l, t, n))
                                ev.add("gla_e", ("e", l, t, n))
                                ev.add("gla_qk", ("qk", l, t, n))
                                take(("lev", l, t, n), n % 2)
                            take(("o", l, b, t), 3)
                    if b == "gqa":
                        take(("swap", l), 2)
                    for t in range(nq):
                        for h in range(4):
                            if b == "ret":
                                take(("s", l, b, t, h), h % 2)
                                ev.add("weights_used", ("pv", l, b, t, h))
                            if b in ("gqa", "dif"):
                                for m in range(2 if b == "dif" else 1):
                                    take(("s", l, b, t, h, m), m if b == "dif" else h % 2)
                                    ev.add("max_ready", ("max", l, b, t, h, m))
                                if b == "dif":
                                    ev.add("differed", ("dif", l, b, t, h))
                                take(("pt", l, b, t, h), 2)
                                ev.add("weights_used", ("pv", l, b, t, h))
                        if b != "gla":
                            take(("o", l, b, t), 3, ("pv", l, b, t, 3))
                    if b != "gqa":
                        ev.add("o_squares", ("osq", l, b))
                        ev.add("o_roots", ("oroot", l, b))
                        if b in ("ret", "gla"):
                            ev.add("o_silu", ("osilu", l, b))
                        ev.add("o_normed", ("onorm", l, b))
                    take(("y", l, b, 0), 0)
                    take(("y", l, b, 1), 1)
                if l == 0:
                    ev.add("mod_ready", ("modr", l, 1))
                keys = [("g", l, u, b) for u in range(4) for b in range(5)]
                chunks(keys, 2)
                ev.add("stream_split", ("hsplit", l, 1))
                split_chunks([key for key in keys if key[3] < 4], 2)
                base = list(fills)
                for u in range(4):
                    for b in range(4):
                        take(("g", l, u, b), b % 2, "chunk")
                    for b in range(4):
                        fill[("yb", l, u, b)] = (2 + b % 2, fills[2 + b % 2], 0, "chunk" if b == 3 else None)
                        fills[2 + b % 2] += 1
                close(fill, fills, base, 2, [k for k in fill if k[0] in ("g", "yb") and k[1] == l])
                ev.loop([(f"full{2 + b % 2}", ("full", ("yb", l, u, b))) for u in range(4) for b in range(3)], 2)
                ev.loop([("merged", ("merged", l, u)) for u in range(4)], 2)
                chunks([("out", l, u) for u in range(4)], 2)
                base = list(fills)
                for u in range(4):
                    take(("out", l, u), u % 2, "chunk")
                close(fill, fills, base, 2, [("out", l, u) for u in range(4)])
            for k in range(KT):
                ev.add("squares", ("sq", l, which, k))
                ev.add("squares_used", ("squ", l, which, k))
            take(("norm", l, which), 2, ("squ", l, which, KT - 1))
            for k in range(KT):
                ev.add("scaled", ("scaled", l, which, k))
                ev.add("h_ready", ("h", l, which, k))
        keys = []
        for u in range(4):
            keys += [("up", l, u)] + ([("mod", l + 1, m) for m in BEHIND_UP[u]] if l + 1 < depth else [])
        chunks(keys, FT // 2)
        ev.add("stream_split", ("hsplit", l, 2))
        split_chunks([("up", l, u) for u in range(4)], FT // 2)
        base = list(fills)
        for u in range(4):
            take(("up", l, u), u, "chunk")
        close(fill, fills, base, FT // 2, [("up", l, u) for u in range(4)])
        ev.loop([("conv_centre", ("cc", l, u)) for u in range(2)], FT // 2)
        ev.loop([("conv_silu", ("cs", l, u)) for u in range(2)], FT // 2)
        chunks([("down", l, u, j) for u in range(4) for j in range(3)], 2)
        base = list(fills)
        for u in range(4):
            take(("down", l, u), u % 2, "chunk")
        close(fill, fills, base, 2, [("down", l, u) for u in range(4)])
    for t in range(TL):
        take(("final", t), t)
        ev.add("final_ready", ("fr", t))
    return ev, chunk, fill, splits


def between_projections(l):
    keys = [(kind[0], l, b, n) for b in ("ret", "gla", "gqa", "dif") for kind in ("feat", "tok")
            for n in range(len(BR[b][kind]))]
    left = list(range(MOD0, MODT)) if l == 0 else []
    extra = len(left) - len(keys)
    return {key: [left.pop(0) for _ in range(2 if n < extra else 1)] for n, key in enumerate(keys) if left}


def close(fill, fills, base, iters, keys):
    per = [a - b for a, b in zip(fills, base)]
    for key in keys:
        p, n, _, ready = fill[key]
        fill[key] = (p, n, per[p], ready)
    for p in range(4):
        fills[p] = base[p] + per[p] * iters


def bass_hybrid_backbone(nc, A, out):
    ev, chunk, fill, splits = schedule()
    ctx = ExitStack()
    with ctx:
        def sb(name, shape, dt=F32):
            return ctx.enter_context(nc.sbuf_tensor(name, shape, dt))

        xT = sb("xT", [P, KT, T])
        hT_at = nc.sbuf_base
        hT = sb("hT", [P, KT, T])
        ring = sb("ring", [P, RING, KT, P])
        small = sb("small", [P, sum(w for _, w in SMALL)])
        rope = sb("rope", [P, 6, LAT])
        dist = sb("dist", [P, 7 * P])
        mask = sb("mask", [P, 2, len(LEVELS), P], U8)
        rows = sb("rows", [P, 2 * DEPTH, P])
        vec = sb("vec", [P, 2 * DEPTH, P])
        gate_b = sb("gate_b", [P, DEPTH, 512])
        gate_up = sb("gate_up", [32, DEPTH, 512])
        onorm = sb("onorm", [P, 2, DEPTH, 64])
        decay = sb("decay", [P, DEPTH * 8])
        lams = sb("lams", [P, DEPTH * 4 * 32])
        tiny = sb("tiny", [P, 256])
        modv = sb("modv", [P, MODT, 2])
        arena_at = nc.sbuf_base
        arena = sb("arena", [P, (FT + 2 + KT) * T])
        w_hi = sb("w_hi", [P, 2, KT // 2, P], F32R)
        w_lo = sb("w_lo", [P, 2, KT // 2, P], F32R)
        one = sb("one", [P, 1])
        used = [0]

        def part(n):
            used[0] += n
            return arena[:, used[0] - n:used[0]]

        q = part(5 * T).rearrange("p (c t) -> p c t", t=T)
        v = part(4 * T).rearrange("p (c n t) -> p c n t", c=4, n=NT)
        yT = part(8 * T).rearrange("p (c t) -> p c t", t=T)
        scratch0 = used[0]
        scratch = arena[:, scratch0:]
        size = {n: w for n, w in SMALL}
        offs, o = {}, 0
        for n, w in SMALL:
            offs[n] = o
            o += w
        K = {n: small[:, offs[n]:offs[n] + w] for n, w in SMALL}
        ident = K["ident"]

        pair = [ctx.enter_context(nc.psum_tensor(f"pair{i}", [P, 1024], F32)) for i in range(4)]

        S = {}
        for name in (["consts", "x_in", "out_done", "chunk_done", "dve", "act", "pool"]
                     + [f"landed{i}" for i in range(RING)] + [f"freed{i}" for i in range(4)]
                     + [f"full{i}" for i in range(4)] + sorted(k for k in ev.count if not k.startswith("full"))
                     + [f"set{i}" for i in range(8)]):
            S[name] = ctx.enter_context(nc.semaphore(name))

        def at(key, i=0):
            sem, n, per = ev.at[key]
            return S[sem], n + per * i if per else n

        def sem(key):
            return S[ev.at[key][0]]

        def chunk_no(key, i=0):
            n, per = chunk[key]
            return n, (n + per * i if per else n)

        def slot(key):
            return ring[:, chunk[key][0] % RING]

        def half_free(key, j, i):
            other, before = splits[key], i if splits[key] != last_split(key) else i - 1
            if j == 0:
                return at(("half", other), before)
            c, per = chunk[other]
            return S["chunk_done"], c + 1 + per * before

        def last_split(key):
            return splits[key] if chunk[splits[key]][0] > chunk[key][0] else None

        def landed(key, i=0):
            n, per = chunk[key]
            return S[f"landed{n % RING}"], 16 * (n // RING + 1) + (16 * (per // RING) * i if per else 0)

        def room(key, i=0):
            p, n, per, _ = fill[key]
            assert n > 0
            return S[f"freed{p}"], n + per * i if per else n

        def filled(key, i=0, ck=None):
            ready = fill[key][3]
            if ready is None:
                return at(("full", key), i)
            if ready == "chunk":
                return S["chunk_done"], chunk_no(ck or key, i)[1] + 1
            return at(ready, i)

        def emptied(key, i=0):
            p, n, per, _ = fill[key]
            return S[f"freed{p}"], n + 1 + (per * i if per else 0)

        def psum(key):
            return pair[fill[key][0]]

        def freed(key):
            return S[f"freed{fill[key][0]}"]

        def fullsem(key):
            return S[f"full{fill[key][0]}"]

        def segs(w):
            return [(0, min(w, LAT))] + ([(LAT, w)] if w > LAT else [])

        def is_q(b, n):
            return n < BR[b]["nq"]

        def colv(l, which, n):
            return vec[:, 2 * l + which, n:n + 1]

        lg = tiny[:, 0:16]
        neg_lam = tiny[:, 16:18]
        pp1 = tiny[:, 20:36]
        cs = tiny[:, 40:56].rearrange("p (s k) -> p s k", s=2)
        a1 = tiny[:, 64:96].rearrange("p (w k s) -> p w k s", w=2, k=KT)
        nmx = tiny[:, 96:104]
        rsum = [tiny[:, 104:112], tiny[:, 184:192]]
        dtmp = tiny[:, 112:120]
        oss = tiny[:, 120:144]
        lamt = tiny[:, 144:148]
        eps = tiny[:, 150:151]
        rd = tiny[:, 152:184]
        neg_lg, lg_ctx, lg_lat = tiny[:, 192:208], tiny[:, 208:224], tiny[:, 224:240]

        last = DEPTH - 1
        W = {l: (T if l < last else LAT) for l in range(DEPTH)}
        NQ = {l: W[l] // P for l in range(DEPTH)}

        def cut(*sizes):
            o, res = scratch0, []
            for s in sizes:
                res.append(arena[:, o:o + s])
                o += s
            assert o <= arena.shape[1], (o, arena.shape)
            return res

        xin = arena[:, 0:6 * D].rearrange("p (t d) -> p t d", t=NT)
        sqb, rs, tb = cut(2 * T, T, 2 * T)
        sqb = sqb.rearrange("p (b t) -> p b t", b=2)
        tb = tb.rearrange("p (b t) -> p b t", b=2)
        o_flat, prep_flat = cut(6 * 256, 2 * T)
        o_sb = o_flat.rearrange("p (t c) -> p t c", c=256)
        prep = prep_flat.rearrange("p (b t) -> p b t", b=2)
        NEAR, FAR = 7 * P, 5 * P
        _, strip, pt_r = cut(6 * 256 + 2 * T, 4 * (NEAR + FAR), 2 * T)
        e0, e2, e1 = pt_r[:, 0:NEAR], pt_r[:, NEAR:NEAR + FAR], o_flat[:, 0:NEAR]
        strip = strip.rearrange("p (h n) -> p h n", h=4)
        pt_r = pt_r.rearrange("p (b t) -> p b t", b=2)
        _, prob, pt_s = cut(6 * 256 + 2 * T, 4 * T, 2 * T)
        prob = prob.rearrange("p (b m t) -> p b m t", b=2, m=2)
        pt_s = pt_s.rearrange("p (b t) -> p b t", b=2)
        G = {}
        _, bT, el, work = cut(6 * 256, 4 * T, 4 * NT, 9 * 512)
        bT = bT.rearrange("p (c t) -> p c t", t=T)
        el = el.rearrange("p (c t) -> p c t", c=4)
        for n, name in enumerate(["lx", "la", "ab", "ex", "kd"]):
            G[name] = work[:, 512 * n:512 * (n + 1)]
        quad = [work[:, 512 * n:512 * (n + 1)].rearrange("p (d c t) -> p d c t", d=2, c=2) for n in range(9)]
        G["dd"], G["ql"], G["kl"], G["qe"], G["eb"] = quad[0:2], quad[2:4], quad[4:6], quad[6], quad[7]
        G["pt"] = work[:, 4096:4608].rearrange("p (s c t) -> p s c t", s=2, c=2)
        yfree = yT.rearrange("p c t -> p (c t)")[:, 4 * T:8 * T]
        G["U"] = yfree[:, 0:1536].rearrange("p (t c n) -> p t c n", t=NT, c=4)
        G["S"] = yfree[:, 1536:3072].rearrange("p (t c n) -> p t c n", t=NT, c=4)
        mT, sig, prod = cut(KT * T, 4 * T, T)
        mT = mT.rearrange("p (c t) -> p c t", t=T)
        sig = sig.rearrange("p (c t) -> p c t", t=T)
        ff = arena[:, 0:FT * T].rearrange("p (c t) -> p c t", t=T)
        conv = arena[:, FT * T:(FT + 2) * T].rearrange("p (c t) -> p c t", t=T)
        rests = nc.alloc_sbuf_tensor_at("rests", [P, KT, T], F32R, offset=hT_at)
        lead = {1: nc.alloc_sbuf_tensor_at("lead1", [P, KT, T], F32R, offset=arena_at),
                2: nc.alloc_sbuf_tensor_at("lead2", [P, KT, T], F32R, offset=arena_at + 4 * (FT + 2) * T)}
        res = arena[:, 0:TL * D].rearrange("p (t d) -> p t d", t=TL)

        mask_in = arena[:, 6 * D:6 * D + 2 * len(LEVELS) * P]
        loads = [(small[:], A["k_small"]), (rope[:].rearrange("p c t -> p (c t)"), A["k_rope"]),
                 (dist[:], A["k_dist"]), (mask_in, A["k_mask"]),
                 (decay[:], A["ret_decay"].rearrange("l d h -> (l d h)").partition_broadcast(P)),
                 (lams[:], A["dif_lambda"].rearrange("l m d -> (l m d)").partition_broadcast(P)),
                 (gate_b[:].rearrange("p l n -> p (l n)"), A["gla_gate_b"].rearrange("l d n -> (l d n)").partition_broadcast(P)),
                 (onorm[:, 0].rearrange("p l n -> p (l n)"), A["gla_norm"].rearrange("l n -> (l n)").partition_broadcast(P)),
                 (onorm[:, 1].rearrange("p l n -> p (l n)"), A["dif_subln"].rearrange("l n -> (l n)").partition_broadcast(P))]
        for l in range(DEPTH):
            for r0, name, n in ((VA_BMOD, "b_mod", MODT), (VA_N1, "norm1", KT), (VA_N2, "norm2", KT), (VA_CB, "conv_b", FT)):
                loads.append((rows[r0:r0 + n, 2 * l], A[name][l].rearrange("(r n) -> r n", n=P)))
            loads.append((rows[VB_CW:VB_CW + 3 * FT, 2 * l + 1], A["conv_w"][l].rearrange("w (r n) -> (w r) n", n=P)))
            loads.append((rows[VB_C:VB_C + KT, 2 * l + 1], A["c"].rearrange("b (r n) -> (b r) n", n=P)))
            loads.append((rows[VB_C + KT:VB_C + 2 * KT, 2 * l + 1], A["c_ctx"].rearrange("(r n) -> r n", n=P)))
            for r, name, dim in ((0, "gqa_qnorm", 64), (1, "gqa_knorm", 64), (2, "dif_qnorm", 32), (3, "dif_knorm", 32)):
                for s in range(P // dim):
                    loads.append((rows[VB_QN + r:VB_QN + r + 1, 2 * l + 1, s * dim:(s + 1) * dim], A[name][l:l + 1]))
        late_loads = [(gate_up[RANK * d:RANK * (d + 1), l, 256 * d:256 * (d + 1)], A["gla_gate_up"][l, d])
                      for l in range(DEPTH) for d in range(2)]
        N_CONST = len(loads) + len(late_loads)

        block = ctx.enter_context(nc.Block())

        w_in_v = [A["w_in"][l].rearrange("(k p) n -> p k n", p=P) for l in range(DEPTH)]

        @block.sync
        def _(sp):
            def load(key, src, i=None, k=KT, w=P, ahead=0):
                n, now = chunk_no(key, 0 if i is None else i)
                if n >= RING or i is not None:
                    if ahead >= 0:
                        sp.wait_ge(S["chunk_done"], now - RING + 1 + ahead)
                sp.dma_start(slot(key)[:, 0:k, 0:w], src).then_inc(S[f"landed{n % RING}"], 16)

            sp.dma_start(xin[:, 0:TL], A["x"].rearrange("b (t p) d -> p (b t) d", p=P)).then_inc(S["x_in"], 16)
            sp.dma_start(xin[:, TL:NT], A["ctx"].rearrange("b (t p) d -> p (b t) d", p=P)).then_inc(S["x_in"], 16)
            for l in range(DEPTH):
                wm = A["w_mod"][l].rearrange("(k p) (c n) -> c p k n", p=P, n=P)
                if l == 0:
                    for u in range(4):
                        load(("mod", l, u), wm[u])
                    with sp.Fori(0, MOD0 // 4 - 1) as i:
                        for u in range(4):
                            load(("mod", l, u), wm[bass.ds(4 * i + (4 + u), 1)].squeeze(0), i + 1)
                else:
                    for m in range(4 * (FT // 2), MODT):
                        load(("modx", l, m), wm[m])
                between = between_projections(l)
                for b in ("ret", "gla", "gqa", "dif"):
                    for kind in ("feat", "tok"):
                        for n, c in enumerate(BR[b][kind]):
                            key = (kind[0], l, b, n)
                            w = 32 if c == 2048 else P
                            load(key, w_in_v[l][:, :, c:c + w], w=w)
                            for m in between.get(key, []):
                                load(("modx", l, m), wm[m])
                wg = A["w_in"][l, :, GATES:].rearrange("(k p) (c n) -> c p k n", p=P, n=P)
                wb = A["w_branch"][l].rearrange("b (k p) (c n) -> c p (b k) n", p=P, n=P)
                with sp.Fori(0, 2) as i:
                    for u in range(4):
                        for b in range(4):
                            load(("g", l, u, b), wg[bass.ds(4 * i + u + KT * b, 1)].squeeze(0), i, ahead=b // 3)
                        load(("g", l, u, 4), wb[bass.ds(4 * i + u, 1)].squeeze(0), i, ahead=-1)
                wo = A["w_out"][l].rearrange("(k p) (c n) -> c p k n", p=P, n=P)
                with sp.Fori(0, 2) as i:
                    for u in range(4):
                        load(("out", l, u), wo[bass.ds(4 * i + u, 1)].squeeze(0), i)
                wu = A["w_up"][l].rearrange("(k p) (s c n) -> s c p k n", p=P, s=2, n=P)
                if l < last:
                    wn = A["w_mod"][l + 1].rearrange("(k p) (c n) -> c p k n", p=P, n=P)
                with sp.Fori(0, FT // 2) as i:
                    for u in range(4):
                        load(("up", l, u), wu[u % 2, bass.ds(2 * i + u // 2, 1)].squeeze(0), i)
                        for m in (BEHIND_UP[u] if l < last else ()):
                            load(("mod", l + 1, m), wn[bass.ds(4 * i + m, 1)].squeeze(0), i)
                wd = A["w_down"][l].rearrange("(k p) (c n) -> c p k n", p=P, n=P)
                with sp.Fori(0, 2) as i:
                    for u in range(4):
                        for j in range(3):
                            k = min(8, FT - 8 * j)
                            load(("down", l, u, j), wd[bass.ds(4 * i + u, 1), :, 8 * j:8 * j + k].squeeze(0), i, k=k)
            sp.wait_ge(S["out_done"], 16 * TL)

        @block.tensor
        def _(pe):
            pe.wait_ge(S["consts"], 16 * N_CONST)

            def projection(key, rhs, width, i=0, M=P, kt=KT):
                pe.wait_ge(*room(key, i))
                acc = psum(key)
                pe.wait_ge(*landed(key, i))
                for a, b in segs(width):
                    for k in range(kt):
                        mm = pe.matmul(acc[0:M, a:b], slot(key)[:, k, 0:M], rhs[:, k, a:b], start=k == 0, stop=k == kt - 1)
                mm.then_inc(S["chunk_done"], 1)

            def split_projection(key, which, width, i):
                pe.wait_ge(*room(key, i))
                acc = psum(key)
                for j in range(2):
                    pe.wait_ge(*at(("split", key, j), i))
                    for a, b in segs(width):
                        for k in range(KT // 2):
                            n = KT // 2 * j + k
                            pe.matmul(acc[:, a:b], w_hi[:, j, k], lead[which][:, n, a:b], start=n == 0, stop=False)
                            pe.matmul(acc[:, a:b], w_hi[:, j, k], rests[:, n, a:b], start=False, stop=False)
                            mm = pe.matmul(acc[:, a:b], w_lo[:, j, k], lead[which][:, n, a:b], start=False, stop=n == KT - 1)
                    mm.then_inc(sem(("half", key)) if j == 0 else S["chunk_done"], 1)

            def token_projection(key, tiles):
                pe.wait_ge(*room(key))
                acc = psum(key)
                pe.wait_ge(*landed(key))
                for t in range(tiles):
                    for k in range(KT):
                        mm = pe.matmul(acc[:, t * P:(t + 1) * P], hT[:, k, t * P:(t + 1) * P], slot(key)[:, k],
                                       start=k == 0, stop=k == KT - 1)
                mm.then_inc(S["chunk_done"], 1)

            def modulation(key, col, i=0):
                pe.wait_ge(*landed(key, i))
                for k in range(KT):
                    mm = pe.matmul(pair[3][:, col], slot(key)[:, k], cs[:, :, k], start=k == 0, stop=k == KT - 1)
                mm.then_inc(S["chunk_done"], 1)

            def norm(l, which):
                pe.wait_ge(*room(("norm", l, which)))
                acc = psum(("norm", l, which))
                for k in range(KT):
                    pe.wait_ge(*at(("sq", l, which, k)))
                    for a, b in segs(W[l] if which == 2 else T):
                        mm = pe.matmul(acc[:, a:b], K["ones"], sqb[:, k % 2, a:b], start=k == 0, stop=k == KT - 1)
                    mm.then_inc(sem(("squ", l, which, k)), 1)

            def prep_tiles(l, b):
                dim = 32 if b == "dif" else 64
                for n in range(len(BR[b]["feat"])):
                    w = W[l] if is_q(b, n) else T
                    if b != "ret":
                        pe.wait_ge(*room(("qkn", l, b, n)))
                        acc = psum(("qkn", l, b, n))
                        pe.wait_ge(*at(("qksq", l, b, n)))
                        for x, y in segs(w):
                            mm = pe.matmul(acc[:, x:y], K[f"sum{dim}"], prep[:, 0, x:y], start=True, stop=True)
                        mm.then_inc(fullsem(("qkn", l, b, n)), 1)
                    pe.wait_ge(*room(("rope", l, b, n)))
                    acc = psum(("rope", l, b, n))
                    if b == "ret":
                        pe.wait_ge(*emptied(("f", l, b, n)))
                    else:
                        pe.wait_ge(*at(("turnable", l, b, n)))
                    pe.matmul(acc[:, 0:LAT], K[f"perm{dim}"], q[:, n, 0:LAT], start=True, stop=True).then_inc(
                        fullsem(("rope", l, b, n)), 1)

            def retention(l):
                b = "ret"

                def scores(t, h):
                    pe.wait_ge(*room(("s", l, b, t, h)))
                    acc = psum(("s", l, b, t, h))
                    pb = 64 * (h % 2)
                    for m in (range(NT) if t < TL else range(TL, NT)):
                        mm = pe.matmul(acc[:, m * P:(m + 1) * P], q[pb:pb + 64, 2 + h // 2, m * P:(m + 1) * P],
                                       q[pb:pb + 64, h // 2, t * P:(t + 1) * P], start=True, stop=True)
                    mm.then_inc(fullsem(("s", l, b, t, h)), 1)

                order = [(t, h) for t in range(NQ[l]) for h in range(4)]
                pe.wait_ge(*at(("turned", l, b, 3)))
                scores(*order[0])
                for n in range(len(order)):
                    if n + 1 < len(order):
                        scores(*order[n + 1])
                    if n >= 1:
                        values(l, b, *order[n - 1], pt_r)
                values(l, b, *order[-1], pt_r)

            def values(l, b, t, h, weights):
                pt = weights[:, h % 2].rearrange("p (m n) -> p m n", n=P)
                if h == 0:
                    pe.wait_ge(*room(("o", l, b, t)))
                acc = psum(("o", l, b, t))
                pe.wait_ge(*emptied(("s", l, b, t, h) if b == "ret" else ("pt", l, b, t, h)))
                ms = list(range(NT) if t < TL else range(TL, NT))
                hv = h // 2 if b == "gqa" else h
                for m in ms:
                    mm = pe.matmul(acc[:, 64 * h:64 * h + 64], pt[:, m], v[:, hv // 2, m, 64 * (hv % 2):64 * (hv % 2) + 64],
                                   start=m == ms[0], stop=m == ms[-1])
                mm.then_inc(sem(("pv", l, b, t, h)), 1)

            def softmax(l, b):
                maps = 2 if b == "dif" else 1

                def scores(t, h):
                    for m in range(maps):
                        pe.wait_ge(*room(("s", l, b, t, h, m)))
                        acc = psum(("s", l, b, t, h, m))
                        if b == "dif":
                            lo, n, qi, ki = 64 * (h % 2) + 32 * m, 32, h // 2, 2 + h // 2
                        else:
                            lo, n, qi, ki = 64 * (h % 2), 64, h // 2, 2 if h // 2 == h % 2 else 3
                        for x, y in (segs(T) if t < TL else [(LAT, T)]):
                            mm = pe.matmul(acc[:, x:y], q[lo:lo + n, qi, t * P:(t + 1) * P], q[lo:lo + n, ki, x:y],
                                           start=True, stop=True)
                        mm.then_inc(fullsem(("s", l, b, t, h, m)), 1)

                order = [(t, h) for t in range(NQ[l]) for h in range(4)]
                pe.wait_ge(*at(("turned", l, b, len(BR[b]["feat"]) - 1)))
                if b == "gqa":
                    pe.wait_ge(*room(("swap", l)))
                    acc = psum(("swap", l))
                    for x, y in segs(T):
                        mm = pe.matmul(acc[:, x:y], K["swap"], q[:, 2, x:y], start=True, stop=True)
                    mm.then_inc(fullsem(("swap", l)), 1)
                    pe.wait_ge(*emptied(("swap", l)))
                ahead = 1 if b == "dif" else 2
                for n in range(ahead):
                    scores(*order[n])
                for n, (t, h) in enumerate(order):
                    if n + ahead < len(order):
                        scores(*order[n + ahead])
                    if n >= 1:
                        values(l, b, *order[n - 1], pt_s)
                    pe.wait_ge(*room(("pt", l, b, t, h)))
                    acc = psum(("pt", l, b, t, h))
                    if b == "dif":
                        pe.wait_ge(*at(("dif", l, b, t, h)))
                    else:
                        pe.wait_ge(*emptied(("s", l, b, t, h, 0)))
                    for m in (range(NT) if t < TL else range(TL, NT)):
                        mm = pe.transpose(acc[:, m * P:(m + 1) * P], prob[:, h % 2, 0, m * P:(m + 1) * P], ident)
                    mm.then_inc(fullsem(("pt", l, b, t, h)), 1)
                values(l, b, *order[-1], pt_s)

            def gla(l):
                pe.wait_ge(*emptied(("f", l, "gla", 4)))
                pe.wait_ge(*emptied(("t", l, "gla", 1)))
                for t in range(NT):
                    ts = slice(t * P, (t + 1) * P)
                    pe.wait_ge(*room(("logit", l, t)))
                    acc = psum(("logit", l, t))
                    pe.matmul(acc[:, 0:512], q[0:32, 4, ts], gate_up[:, l], start=True, stop=True).then_inc(
                        fullsem(("logit", l, t)), 1)
                    pe.wait_ge(*room(("ktok", l, t)))
                    acc = psum(("ktok", l, t))
                    for c in range(2):
                        mm = pe.transpose(acc[:, c * P:(c + 1) * P], q[:, 2 + c, ts], ident)
                    mm.then_inc(fullsem(("ktok", l, t)), 1)
                    pe.wait_ge(*room(("cum", l, t)))
                    acc = psum(("cum", l, t))
                    pe.wait_ge(*at(("la", l, t)))
                    for d in range(2):
                        for c in range(2):
                            lo = d * 256 + c * P
                            mm = pe.matmul(acc[:, (2 * d + c) * P:(2 * d + c + 1) * P], G["la"][:, lo:lo + P],
                                           K["tri"][:, d * P:(d + 1) * P], start=True, stop=True)
                    mm.then_inc(fullsem(("cum", l, t)), 1)
                    pe.wait_ge(*room(("rest", l, t)))
                    acc = psum(("rest", l, t))
                    for d in range(2):
                        mm = pe.matmul(acc[:, d * 256:d * 256 + 256], K["rest"][:, d * P:(d + 1) * P],
                                       G["la"][:, d * 256:d * 256 + 256], start=True, stop=True)
                    mm.then_inc(fullsem(("rest", l, t)), 1)
                    pe.wait_ge(*room(("U", l, t)))
                    acc = psum(("U", l, t))
                    pe.wait_ge(*emptied(("ktok", l, t)))
                    for d in range(2):
                        for c in range(2):
                            mm = pe.matmul(acc[:, (2 * d + c) * P:(2 * d + c + 1) * P],
                                           G["kd"][:, d * 256 + c * P:d * 256 + (c + 1) * P], v[:, c, t], start=True, stop=True)
                    mm.then_inc(fullsem(("U", l, t)), 1)
                for t in range(NQ[l]):
                    ts = slice(t * P, (t + 1) * P)
                    pe.wait_ge(*room(("diag", l, t)))
                    acc = psum(("diag", l, t))
                    for h in range(4):
                        pb = 64 * (h % 2)
                        lo = 512 * (h % 2) + P * (h // 2)
                        mm = pe.matmul(acc[:, lo:lo + P], q[pb:pb + 64, 2 + h // 2, ts], q[pb:pb + 64, h // 2, ts],
                                       start=True, stop=True)
                    mm.then_inc(fullsem(("diag", l, t)), 1)
                    for n in range(len(LEVELS)):
                        pe.wait_ge(*room(("lev", l, t, n)))
                        acc = psum(("lev", l, t, n))
                        pe.wait_ge(*at(("qk", l, t, n)))
                        for d in range(2):
                            for h in range(4):
                                pb = 64 * (h % 2)
                                lo = 512 * (h % 2) + 256 * d + P * (h // 2)
                                mm = pe.matmul(acc[:, lo:lo + P],
                                               G["kl"][n % 2][pb:pb + 64, d, h // 2], G["ql"][n % 2][pb:pb + 64, d, h // 2],
                                               start=True, stop=True)
                        mm.then_inc(fullsem(("lev", l, t, n)), 1)
                    pe.wait_ge(*room(("o", l, "gla", t)))
                    acc = psum(("o", l, "gla", t))
                    pe.wait_ge(*emptied(("lev", l, t, len(LEVELS) - 1)))
                    for h in range(4):
                        pb = 64 * (h % 2)
                        lo = 512 * (h % 2) + 64 * (h // 2)
                        pe.matmul(acc[:, lo:lo + 64], G["pt"][:, h % 2, h // 2], v[:, h // 2, t, pb:pb + 64], start=True, stop=False)
                        for d in range(2):
                            mm = pe.matmul(acc[:, lo:lo + 64], G["qe"][pb:pb + 64, d, h // 2],
                                           G["S"][pb:pb + 64, t, 2 * d + h // 2], start=False, stop=d == 1)
                    mm.then_inc(fullsem(("o", l, "gla", t)), 1)

            def turn_outputs(l, b):
                if b == "gqa":
                    pe.wait_ge(*emptied(("o", l, b, NQ[l] - 1)))
                else:
                    pe.wait_ge(*at(("onorm", l, b)))
                for c in range(2):
                    pe.wait_ge(*room(("y", l, b, c)))
                    acc = psum(("y", l, b, c))
                    for t in range(NQ[l]):
                        mm = pe.transpose(acc[:, t * P:(t + 1) * P], o_sb[:, t, c * P:(c + 1) * P], ident)
                    mm.then_inc(fullsem(("y", l, b, c)), 1)

            pe.wait_ge(S["x_in"], 16 * 2)
            for k in range(KT):
                if k >= 4:
                    pe.wait_ge(*room(("x", k)))
                acc = psum(("x", k))
                for t in range(NT):
                    mm = pe.transpose(acc[:, t * P:(t + 1) * P], xin[:, t, k * P:(k + 1) * P], ident)
                mm.then_inc(fullsem(("x", k)), 1)
            for i in range(2 * DEPTH):
                pe.wait_ge(*room(("vec", i)))
                acc = psum(("vec", i))
                nr = VA_ROWS if i % 2 == 0 else VB_ROWS
                pe.transpose(acc[:, 0:nr], rows[0:nr, i], ident[0:nr, 0:nr]).then_inc(fullsem(("vec", i)), 1)
            pe.wait_ge(S["set0"], 1)

            for l in range(DEPTH):
                if l == 0:
                    pe.wait_ge(*emptied(("vec", 3)))
                    with pe.Fori(0, MOD0 // 4) as i:
                        for u in range(4):
                            modulation(("mod", l, u), bass.ds(MODCOL + 8 * i + 2 * u, 2), i)
                else:
                    pe.wait_ge(*emptied(("up", l - 1, 3), FT // 2 - 1))
                    for m in range(4 * (FT // 2), MODT):
                        modulation(("modx", l, m), slice(MODCOL + 2 * m, MODCOL + 2 * m + 2))
                between = between_projections(l)

                def behind(key):
                    for m in between.get(key, []):
                        modulation(("modx", l, m), slice(MODCOL + 2 * m, MODCOL + 2 * m + 2))

                norm(l, 1)
                pe.wait_ge(*at(("h", l, 1, KT - 1)))
                for b in ("ret", "gla", "gqa", "dif"):
                    for n, c in enumerate(BR[b]["feat"]):
                        projection(("f", l, b, n), hT, W[l] if is_q(b, n) else T, M=32 if c == 2048 else P)
                        behind(("f", l, b, n))
                    for n in range(len(BR[b]["tok"])):
                        token_projection(("t", l, b, n), NQ[l] if n >= 2 else NT)
                        behind(("t", l, b, n))
                    if b == "gla":
                        gla(l)
                    else:
                        prep_tiles(l, b)
                        pe.wait_ge(*emptied(("t", l, b, len(BR[b]["tok"]) - 1)))
                        pe.wait_ge(*emptied(("t", l, b, max(0, len(BR[b]["tok"]) - 2))))
                        if b == "ret":
                            retention(l)
                        else:
                            softmax(l, b)
                    turn_outputs(l, b)
                pe.wait_ge(*emptied(("y", l, "dif", 0)))
                pe.wait_ge(*emptied(("y", l, "dif", 1)))
                if l == 0:
                    pe.wait_ge(*at(("modr", l, 1)))
                pe.wait_ge(*at(("hsplit", l, 1)))
                with pe.Fori(0, 2) as i:
                    for u in range(4):
                        for b in range(4):
                            split_projection(("g", l, u, b), 1, W[l], i)
                        pe.wait_ge(*landed(("g", l, u, 4), i))
                        for b in range(4):
                            pe.wait_ge(*room(("yb", l, u, b), i))
                            acc = psum(("yb", l, u, b))
                            for x, y in segs(W[l]):
                                for k in range(2):
                                    mm = pe.matmul(acc[:, x:y], slot(("g", l, u, 4))[:, 2 * b + k], yT[:, 2 * b + k, x:y],
                                                   start=k == 0, stop=k == 1)
                            mm.then_inc(fullsem(("yb", l, u, b)) if b < 3 else S["chunk_done"], 1)
                pe.wait_ge(*at(("merged", l, 3), 1))
                with pe.Fori(0, 2) as i:
                    for u in range(4):
                        projection(("out", l, u), mT, W[l], i)
                norm(l, 2)
                pe.wait_ge(*at(("hsplit", l, 2)))
                with pe.Fori(0, FT // 2) as i:
                    for u in range(4):
                        split_projection(("up", l, u), 2, W[l], i)
                        for m in (BEHIND_UP[u] if l < last else ()):
                            pe.wait_ge(*room(("up", l, 3), i))
                            modulation(("mod", l + 1, m), bass.ds(MODCOL + 8 * i + 2 * m, 2), i)
                pe.wait_ge(*emptied(("up", l, 3), FT // 2 - 1))
                with pe.Fori(0, 2) as i:
                    for u in range(4):
                        pe.wait_ge(*room(("down", l, u), i))
                        acc = psum(("down", l, u))
                        for j in range(3):
                            key = ("down", l, u, j)
                            pe.wait_ge(*landed(key, i))
                            for x, y in segs(W[l]):
                                for k in range(min(8, FT - 8 * j)):
                                    mm = pe.matmul(acc[:, x:y], slot(key)[:, k], ff[:, 8 * j + k, x:y],
                                                   start=j == 0 and k == 0, stop=8 * j + k == FT - 1)
                            mm.then_inc(S["chunk_done"], 1)
            pe.wait_ge(*emptied(("down", last, 3), 1))
            for t in range(TL):
                pe.wait_ge(*room(("final", t)))
                acc = psum(("final", t))
                for k in range(KT):
                    mm = pe.transpose(acc[:, k * P:(k + 1) * P], xT[:, k, t * P:(t + 1) * P], ident)
                mm.then_inc(fullsem(("final", t)), 1)

        @block.gpsimd
        def _(pool):
            link = Chain(pool, S["pool"])
            pool.memset(one[:], 1.0).then_inc(sem(("one",)), 1)
            pool.wait_ge(*at(("one",)))

            def split(key, i):
                pool.wait_ge(*landed(key, i))
                for j in range(2):
                    w = slot(key)[:, KT // 2 * j:KT // 2 * (j + 1)]
                    pool.wait_ge(*half_free(key, j, i))
                    link(pool.tensor_tensor(w_hi[:, j], w, one[:].unsqueeze(2).to_broadcast([P, KT // 2, P]), ALU.mult))
                    pool.tensor_tensor(w_lo[:, j], w, w_hi[:, j].bitcast(F32), ALU.subtract).then_inc(
                        sem(("split", key, j)), 1)

            for l in range(DEPTH):
                with pool.Fori(0, 2) as i:
                    link.enter(i, 4 * 4 * 2)
                    for u in range(4):
                        for b in range(4):
                            split(("g", l, u, b), i)
                    link.leave(2)
                with pool.Fori(0, FT // 2) as i:
                    link.enter(i, 4 * 2)
                    for u in range(4):
                        split(("up", l, u), i)
                    link.leave(FT // 2)

        @block.scalar
        def _(act):
            link = Chain(act, S["act"])
            for dst, src in loads:
                act.dma_start(dst, src).then_inc(S["consts"], 16)
            act.wait_ge(S["set7"], 1)
            for dst, src in late_loads:
                act.dma_start(dst, src).then_inc(S["consts"], 16)
            for k in range(KT):
                act.wait_ge(*filled(("x", k)))
                acc = psum(("x", k))
                act.activation(xT[:, k], acc[:, 0:T], ACT.Copy).then_inc(freed(("x", k)), 1)
            act.wait_ge(*emptied(("vec", 1)))
            act.activation(tiny[:, 40:56], vec[:, 1, VB_C:VB_C + 2 * KT], ACT.Silu).then_inc(S["set0"], 1)
            act.wait_ge(S["set1"], 1)
            link(act.activation(pp1, pp1, ACT.Exp))
            act.activation(lamt, lamt, ACT.Exp).then_inc(S["set2"], 1)
            act.activation(pp1, pp1, ACT.Ln, bias=1.0).then_inc(S["set3"], 1)

            def norm(l, which):
                w = W[l] if which == 2 else T
                act.wait_ge(*filled(("norm", l, which)))
                acc = psum(("norm", l, which))
                act.activation(rs[:, 0:w], acc[:, 0:w], ACT.Sqrt, bias=eps).then_inc(freed(("norm", l, which)), 1)
                act.wait_ge(*at(("modr", l, 0 if l == 0 and which == 1 else 1)))
                for k in range(KT):
                    act.wait_ge(*at(("scaled", l, which, k)))
                    for s, (x, y) in enumerate(segs(w)):
                        ins = act.activation(hT[:, k, x:y], tb[:, k % 2, x:y], ACT.Identity,
                                             scale=a1[:, which - 1, k, s:s + 1],
                                             bias=modv[:, 24 * (which - 1) + k, s:s + 1])
                    ins.then_inc(sem(("h", l, which, k)), 1)

            def out_of_psum(dst, key, w, scale=1.0):
                act.wait_ge(*filled(key))
                acc = psum(key)
                act.activation(dst, acc[0:dst.shape[0], 0:w], ACT.Copy, scale=scale).then_inc(freed(key), 1)

            def softmax(l, b):
                maps = 2 if b == "dif" else 1
                scale = (32 if b == "dif" else 64) ** -0.5
                order = [(t, h) for t in range(NQ[l]) for h in range(4)]

                def transposed(n):
                    t, h = order[n]
                    lo = 0 if t < TL else LAT
                    if n >= 2:
                        act.wait_ge(*at(("pv", l, b, *order[n - 2])))
                    act.wait_ge(*filled(("pt", l, b, t, h)))
                    acc = psum(("pt", l, b, t, h))
                    act.activation(pt_s[:, h % 2, lo:T], acc[:, lo:T], ACT.Copy).then_inc(freed(("pt", l, b, t, h)), 1)

                for n, (t, h) in enumerate(order):
                    lo = 0 if t < TL else LAT
                    if n >= 2:
                        act.wait_ge(*filled(("pt", l, b, *order[n - 2])))
                    for m in range(maps):
                        key = ("s", l, b, t, h, m)
                        act.wait_ge(*at(("max", l, b, t, h, m)))
                        c = (h * maps + m) % 8
                        act.activation(prob[:, h % 2, m, lo:T], pair[fill[key][0]][:, lo:T], ACT.Exp, scale=scale,
                                       bias=nmx[:, c:c + 1],
                                       accum_out=rsum[t % 2][:, 4 * m + h:4 * m + h + 1]).then_inc(freed(key), 1)
                    if b == "dif" and n >= 1:
                        transposed(n - 1)
                if b == "dif":
                    transposed(len(order) - 1)

            def gla(l):
                for t in range(NT):
                    ts = slice(t * P, (t + 1) * P)
                    act.wait_ge(*at(("abs", l, t)))
                    link(act.activation(G["ab"], G["ab"], ACT.Exp))
                    act.activation(G["ab"], G["ab"], ACT.Ln, bias=1.0).then_inc(sem(("ln", l, t)), 1)
                    act.wait_ge(*filled(("cum", l, t)))
                    acc = psum(("cum", l, t))
                    cum = acc[:, 0:512].rearrange("p (c t) -> p c t", c=4)
                    act.activation(bT[:, :, ts], cum, ACT.Copy)
                    act.activation(el[:, 0:2, t:t + 1], cum[:, 0:2, P - 1:P], ACT.Exp)
                    act.activation(el[:, 2:4, t:t + 1], cum[:, 2:4, 0:1], ACT.Exp).then_inc(freed(("cum", l, t)), 1)
                    act.wait_ge(*filled(("rest", l, t)))
                    acc = psum(("rest", l, t))
                    act.activation(G["ex"], acc[:, 0:512], ACT.Exp).then_inc(freed(("rest", l, t)), 1)
                act.wait_ge(*emptied(("U", l, NT - 1)))
                act.wait_ge(*emptied(("cum", l, NT - 1)))
                for t in range(NQ[l]):
                    act.activation(G["eb"].rearrange("p d c t -> p (d c) t"), bT[:, :, t * P:(t + 1) * P], ACT.Exp).then_inc(
                        sem(("eb", l, t)), 1)
                    for n in range(len(LEVELS)):
                        act.wait_ge(*at(("dd", l, t, n)))
                        act.activation(G["dd"][n % 2], G["dd"][n % 2], ACT.Exp).then_inc(sem(("e", l, t, n)), 1)

            for l in range(DEPTH):
                norm(l, 1)
                for b in ("ret", "gla", "gqa", "dif"):
                    for n, c in enumerate(BR[b]["feat"]):
                        w = W[l] if is_q(b, n) else T
                        M = 32 if c == 2048 else P
                        act.wait_ge(*filled(("f", l, b, n)))
                        acc = psum(("f", l, b, n))
                        act.activation(q[0:M, n, 0:w], acc[0:M, 0:w], ACT.Copy,
                                       scale=0.125 if b == "gla" and is_q(b, n) else 1.0).then_inc(freed(("f", l, b, n)), 1)
                    for n in range(len(BR[b]["tok"])):
                        nt = NQ[l] if n >= 2 else NT
                        act.wait_ge(*filled(("t", l, b, n)))
                        acc = psum(("t", l, b, n))
                        act.activation(v[:, n, 0:nt].rearrange("p n t -> p (n t)"), acc[:, 0:nt * P], ACT.Copy).then_inc(
                            freed(("t", l, b, n)), 1)
                    if b == "ret":
                        for h in range(4):
                            act.wait_ge(*at(("sti", l, h)))
                            act.activation(e0, e0, ACT.Exp)
                            act.activation(e1, e1, ACT.Exp, scale=-1.0)
                            c0, c1 = 8 * l + h, 8 * l + 4 + h
                            act.activation(strip[:, h, NEAR:], dist[:, 0:FAR], ACT.Exp, scale=lg[:, c0:c0 + 1],
                                           bias=lg_ctx[:, c0:c0 + 1])
                            act.activation(e2, dist[:, 0:FAR], ACT.Exp, scale=neg_lg[:, c1:c1 + 1],
                                           bias=lg_lat[:, c1:c1 + 1]).then_inc(sem(("ste", l, h)), 1)
                    if b in ("gqa", "dif"):
                        for n in range(len(BR[b]["feat"])):
                            w = W[l] if is_q(b, n) else T
                            act.wait_ge(*filled(("qkn", l, b, n)))
                            acc = psum(("qkn", l, b, n))
                            act.activation(prep[:, 1, 0:w], acc[:, 0:w], ACT.Sqrt, bias=eps).then_inc(
                                freed(("qkn", l, b, n)), 1)
                        if b == "gqa":
                            out_of_psum(q[:, 3, :], ("swap", l), T)
                        softmax(l, b)
                    if b == "gla":
                        gla(l)
                    if b != "gqa":
                        act.wait_ge(*at(("osq", l, b)))
                        act.activation(oss[:, 0:4 * NQ[l]], oss[:, 0:4 * NQ[l]], ACT.Sqrt, scale=1.0 / 64,
                                       bias=eps).then_inc(sem(("oroot", l, b)), 1)
                    if b in ("ret", "gla"):
                        for c in range(2):
                            act.wait_ge(*emptied(("t", l, b, 2 + c)))
                        act.activation(v[:, 2:4, 0:NQ[l]], v[:, 2:4, 0:NQ[l]], ACT.Silu).then_inc(sem(("osilu", l, b)), 1)
                    for c in range(2):
                        out_of_psum(yT[:, 2 * BR[b]["n"] + c, 0:W[l]], ("y", l, b, c), W[l])
                with act.Fori(0, 2) as i:
                    for u in range(4):
                        for b in range(4):
                            p, n, per, _ = fill[("yb", l, u, 1)]
                            act.wait_ge(S[f"freed{p}"], n + per * i)
                            act.wait_ge(*filled(("g", l, u, b), i))
                            acc = psum(("g", l, u, b))
                            act.activation(sig[:, b, 0:W[l]], acc[:, 0:W[l]], ACT.Sigmoid).then_inc(freed(("g", l, u, b)), 1)
                norm(l, 2)
                cb, cw = vec[:, 2 * l, VA_CB:VA_CB + FT], vec[:, 2 * l + 1, VB_CW:VB_CW + 3 * FT]
                with act.Fori(0, FT // 2) as i:
                    for u in range(2):
                        p, n, per, _ = fill[("up", l, 2 * u + 1)]
                        act.wait_ge(S[f"freed{p}"], n + per * i)
                        act.wait_ge(*filled(("up", l, 2 * u), i))
                        acc = psum(("up", l, 2 * u))
                        act.activation(conv[:, u, 0:W[l]], acc[:, 0:W[l]], ACT.Identity,
                                       scale=cw[:, bass.ds(FT + 2 * i + u, 1)],
                                       bias=cb[:, bass.ds(2 * i + u, 1)]).then_inc(sem(("cc", l, u)), 1)
                        act.wait_ge(*emptied(("up", l, 2 * u), i))
                        act.activation(conv[:, u, 0:W[l]], conv[:, u, 0:W[l]], ACT.Silu).then_inc(sem(("cs", l, u)), 1)
            for t in range(TL):
                act.wait_ge(*at(("fr", t)))
                act.dma_start(out[0, t * P:(t + 1) * P, :], res[:, t]).then_inc(S["out_done"], 16)

        @block.vector
        def _(dve):
            link = Chain(dve, S["dve"])
            dve.memset(eps, EPS)
            dve.memset(gate_up[:], 0.0).then_inc(S["set7"], 1)
            dve.wait_ge(S["consts"], 16 * N_CONST)
            link(dve.tensor_copy(mask[:].rearrange("p d l t -> p (d l t)"), mask_in))
            for i in range(2 * DEPTH):
                dve.wait_ge(*filled(("vec", i)))
                acc = psum(("vec", i))
                nr = VA_ROWS if i % 2 == 0 else VB_ROWS
                dve.tensor_copy(vec[:, i, 0:nr], acc[:, 0:nr]).then_inc(freed(("vec", i)), 1)
                dve.wait_ge(*emptied(('vec', i)))
            dve.scalar_tensor_tensor(out=pp1, in0=decay[:], scalar=-1.0, in1=decay[:], op0=ALU.mult, op1=ALU.min)
            lv = lams[:].rearrange("p (a b d) -> p a b d", b=2, d=32)
            link(dve.tensor_tensor(lv[:, :, 0], lv[:, :, 0], lv[:, :, 1], ALU.mult))
            dve.tensor_reduce(lamt, lv[:, :, 0], AX, ALU.add).then_inc(S["set1"], 1)
            dve.wait_ge(S["set3"], 1)
            link(dve.scalar_tensor_tensor(out=lg, in0=decay[:], scalar=0.0, in1=pp1, op0=ALU.min, op1=ALU.subtract))
            for cols, factor in ((neg_lg, -1.0), (lg_ctx, float(CTX)), (lg_lat, float(LAT))):
                link(dve.tensor_scalar(cols, lg, factor, None, ALU.mult))
            for l in range(DEPTH):
                init = 0.8 - 0.6 * math.exp(-0.3 * l)
                link(dve.tensor_tensor(neg_lam[:, l:l + 1], lamt[:, 2 * l + 1:2 * l + 2], lamt[:, 2 * l:2 * l + 1], ALU.subtract))
                link(dve.tensor_scalar(neg_lam[:, l:l + 1], neg_lam[:, l:l + 1], -init, None, ALU.add))
                link(dve.tensor_scalar(onorm[:, 1, l], onorm[:, 1, l], 1.0 - init, None, ALU.mult))

            def modulation(l, part, first, end):
                key = ("mod", l, 3) if part == 0 else ("modx", l, MODT - 1)
                dve.wait_ge(S["chunk_done"], chunk_no(key, MOD0 // 4 - 1)[1] + 1)
                link(dve.tensor_tensor(modv[:, first:end],
                                       pair[3][:, MODCOL + 2 * first:MODCOL + 2 * end].rearrange("p (m s) -> p m s", s=2),
                                       vec[:, 2 * l, VA_BMOD + first:VA_BMOD + end].unsqueeze(2).to_broadcast([P, end - first, 2]),
                                       ALU.add))
                for w in range(2):
                    if first <= 24 * w + 8 < end:
                        nv = vec[:, 2 * l, VA_N1 + KT * w:VA_N1 + KT * (w + 1)].unsqueeze(2).to_broadcast([P, KT, 2])
                        ins = dve.scalar_tensor_tensor(out=a1[:, w], in0=modv[:, 24 * w + 8:24 * w + 16], scalar=1.0, in1=nv,
                                                       op0=ALU.add, op1=ALU.mult)
                ins.then_inc(sem(("modr", l, part)), 1)
                dve.wait_ge(*at(("modr", l, part)))

            def norm(l, which):
                w = W[l] if which == 2 else T
                for k in range(KT):
                    if l == 0 and which == 1:
                        dve.wait_ge(*emptied(("x", k)))
                    if k >= 2:
                        dve.wait_ge(*at(("squ", l, which, k - 2)))
                    dve.tensor_tensor(sqb[:, k % 2, 0:w], xT[:, k, 0:w], xT[:, k, 0:w], ALU.mult).then_inc(
                        sem(("sq", l, which, k)), 1)
                    dve.wait_ge(*at(('sq', l, which, k)))
                dve.wait_ge(*emptied(("norm", l, which)))
                link(dve.reciprocal(rs[:, 0:w], rs[:, 0:w]))
                for k in range(KT):
                    if k >= 2:
                        dve.wait_ge(*at(("h", l, which, k - 2)))
                    dve.tensor_tensor(tb[:, k % 2, 0:w], xT[:, k, 0:w], rs[:, 0:w], ALU.mult).then_inc(
                        sem(("scaled", l, which, k)), 1)
                    dve.wait_ge(*at(('scaled', l, which, k)))
                    if which == 2 and k >= 1:
                        dve.wait_ge(*at(("h", l, which, k - 1)))
                        split_stream(l, which, k - 1)
                if which == 2:
                    dve.wait_ge(*at(("h", l, which, KT - 1)))
                    split_stream(l, which, KT - 1)

            def split_stream(l, which, k):
                w = W[l]
                hi, h = lead[which][:, k, 0:w], hT[:, k, 0:w]
                link(dve.tensor_copy(hi, h))
                ins = dve.tensor_tensor(rests[:, k, 0:w], h, hi.bitcast(F32), ALU.subtract)
                if k < KT - 1:
                    link(ins)
                else:
                    ins.then_inc(sem(("hsplit", l, which)), 1)
                    dve.wait_ge(*at(("hsplit", l, which)))

            def prep_tiles(l, b):
                cos_sin = {"ret": 0, "gqa": 2, "dif": 4}[b]
                for n in range(len(BR[b]["feat"])):
                    w = W[l] if is_q(b, n) else T
                    z = q[:, n, 0:w]
                    dve.wait_ge(*emptied(("f", l, b, n)))
                    if b != "ret":
                        dve.tensor_tensor(prep[:, 0, 0:w], z, z, ALU.mult).then_inc(sem(("qksq", l, b, n)), 1)
                        dve.wait_ge(*at(('qksq', l, b, n)))
                        dve.wait_ge(*emptied(("qkn", l, b, n)))
                        link(dve.reciprocal(prep[:, 1, 0:w], prep[:, 1, 0:w]))
                        c = VB_QN + (0 if b == "gqa" else 2) + (0 if is_q(b, n) else 1)
                        dve.scalar_tensor_tensor(out=z, in0=z, scalar=colv(l, 1, c), in1=prep[:, 1, 0:w],
                                                 op0=ALU.mult, op1=ALU.mult).then_inc(sem(("turnable", l, b, n)), 1)
                        dve.wait_ge(*at(("turnable", l, b, n)))
                    dve.wait_ge(*filled(("rope", l, b, n)))
                    acc = psum(("rope", l, b, n))
                    z = q[:, n, 0:LAT]
                    dve.tensor_tensor(prep[:, 1, 0:LAT], acc[:, 0:LAT], rope[:, cos_sin + 1], ALU.mult).then_inc(
                        freed(("rope", l, b, n)), 1)
                    dve.wait_ge(*emptied(('rope', l, b, n)))
                    link(dve.tensor_tensor(z, z, rope[:, cos_sin], ALU.mult))
                    dve.wait_ge(*emptied(("rope", l, b, n)))
                    dve.tensor_tensor(z, z, prep[:, 1, 0:LAT], ALU.add).then_inc(sem(("turned", l, b, n)), 1)
                    dve.wait_ge(*at(('turned', l, b, n)))
                dve.wait_ge(*at(("turned", l, b, len(BR[b]["feat"]) - 1)))

            def strips(l):
                D = dist[:, 0:NEAR]
                for h in range(4):
                    dve.tensor_scalar(e0, D, 0.0, lg[:, 8 * l + h:8 * l + h + 1], ALU.max, ALU.mult)
                    dve.tensor_scalar(e1, D, 0.0, lg[:, 8 * l + 4 + h:8 * l + 5 + h], ALU.min, ALU.mult).then_inc(
                        sem(("sti", l, h)), 1)
                    dve.wait_ge(*at(("ste", l, h)))
                    link(dve.scalar_tensor_tensor(out=strip[:, h, 0:NEAR], in0=D, scalar=0.0, in1=e0, op0=ALU.is_ge, op1=ALU.mult))
                    link(dve.scalar_tensor_tensor(out=e1, in0=D, scalar=0.0, in1=e1, op0=ALU.is_le, op1=ALU.mult))
                    link(dve.tensor_tensor(strip[:, h, 0:NEAR], strip[:, h, 0:NEAR], e1, ALU.add))
                    link(dve.tensor_tensor(strip[:, h, NEAR:], strip[:, h, NEAR:], e2, ALU.add))

            def retention(l):
                b = "ret"
                order = [(t, h) for t in range(NQ[l]) for h in range(4)]
                for n, (t, h) in enumerate(order):
                    key = ("s", l, b, t, h)
                    if n >= 2:
                        dve.wait_ge(*at(("pv", l, b, *order[n - 2])))
                    dve.wait_ge(*filled(key))
                    acc = psum(key)
                    pt = pt_r[:, h % 2]
                    if t < TL:
                        dve.scalar_tensor_tensor(out=pt[:, 0:LAT], in0=acc[:, 0:LAT], scalar=0.125,
                                                 in1=strip[:, h, P * (3 - t):P * (3 - t) + LAT], op0=ALU.mult, op1=ALU.mult)
                        far = strip[:, h, NEAR + P * (3 - t):NEAR + P * (3 - t) + CTX]
                    else:
                        far = strip[:, h, P * (3 - t + TL):P * (3 - t + TL) + CTX]
                    dve.scalar_tensor_tensor(out=pt[:, LAT:T], in0=acc[:, LAT:T], scalar=0.125, in1=far,
                                             op0=ALU.mult, op1=ALU.mult).then_inc(freed(key), 1)
                    dve.wait_ge(*emptied(key))
                    if h == 0 and t > 0:
                        output(l, b, t - 1)
                output(l, b, NQ[l] - 1)

            def output(l, b, t):
                dve.wait_ge(*filled(("o", l, b, t)))
                acc = psum(("o", l, b, t))
                if b == "gla":
                    src = acc[:].rearrange("p (s c d) -> p c s d", s=2, d=64)[:, 0:2]
                else:
                    src = acc[:, 0:256].rearrange("p (c s d) -> p c s d", s=2, d=64)
                dve.tensor_copy(o_sb[:, t].rearrange("p (c s d) -> p c s d", s=2, d=64), src).then_inc(freed(("o", l, b, t)), 1)
                dve.wait_ge(*emptied(('o', l, b, t)))

            def softmax(l, b):
                maps = 2 if b == "dif" else 1
                scale = (32 if b == "dif" else 64) ** -0.5
                order = [(t, h) for t in range(NQ[l]) for h in range(4)]

                def maxima(n):
                    t, h = order[n]
                    lo = 0 if t < TL else LAT
                    for m in range(maps):
                        c = (h * maps + m) % 8
                        dve.wait_ge(*filled(("s", l, b, t, h, m)))
                        acc = psum(("s", l, b, t, h, m))
                        link(dve.tensor_reduce(nmx[:, c:c + 1], acc[:, lo:T], AX, ALU.max))
                        dve.tensor_scalar(nmx[:, c:c + 1], nmx[:, c:c + 1], -scale, None, ALU.mult).then_inc(
                            sem(("max", l, b, t, h, m)), 1)
                        dve.wait_ge(*at(('max', l, b, t, h, m)))

                def normalised(t):
                    dve.wait_ge(*filled(("o", l, b, t)))
                    acc = psum(("o", l, b, t))
                    r = rd[:, 4 * (t % 2):4 * (t % 2) + 4]
                    link(dve.reciprocal(r, rsum[t % 2][:, 0:4]))
                    dve.tensor_tensor(o_sb[:, t].rearrange("p (h d) -> p h d", d=64),
                                      acc[:, 0:256].rearrange("p (h d) -> p h d", d=64),
                                      r.unsqueeze(2).to_broadcast([P, 4, 64]), ALU.mult).then_inc(freed(("o", l, b, t)), 1)
                    dve.wait_ge(*emptied(('o', l, b, t)))

                def differ(n):
                    t, h = order[n]
                    lo = 0 if t < TL else LAT
                    for m in range(2):
                        dve.wait_ge(*emptied(("s", l, b, t, h, m)))
                    s0, s1 = (rsum[t % 2][:, 4 * m + h:4 * m + h + 1] for m in range(2))
                    r = rd[:, 16 + h:17 + h]
                    link(dve.reciprocal(r, s1))
                    link(dve.scalar_tensor_tensor(out=r, in0=r, scalar=s0, in1=neg_lam[:, l:l + 1], op0=ALU.mult, op1=ALU.mult))
                    dve.scalar_tensor_tensor(out=prob[:, h % 2, 0, lo:T], in0=prob[:, h % 2, 1, lo:T], scalar=r,
                                             in1=prob[:, h % 2, 0, lo:T], op0=ALU.mult, op1=ALU.add).then_inc(
                        sem(("dif", l, b, t, h)), 1)
                    dve.wait_ge(*at(("dif", l, b, t, h)))

                def transposed(n):
                    t, h = order[n]
                    lo = 0 if t < TL else LAT
                    if n >= 2:
                        dve.wait_ge(*at(("pv", l, b, *order[n - 2])))
                    dve.wait_ge(*filled(("pt", l, b, t, h)))
                    acc = psum(("pt", l, b, t, h))
                    dve.tensor_copy(pt_s[:, h % 2, lo:T], acc[:, lo:T]).then_inc(freed(("pt", l, b, t, h)), 1)
                    dve.wait_ge(*emptied(("pt", l, b, t, h)))

                ahead = 1 if b == "dif" else 2
                for n in range(ahead):
                    maxima(n)
                for n, (t, h) in enumerate(order):
                    if b == "dif":
                        differ(n)
                    elif n >= 1:
                        transposed(n - 1)
                    if n + ahead < len(order):
                        maxima(n + ahead)
                    if h == 0 and t > 0:
                        normalised(t - 1)
                if b == "gqa":
                    transposed(len(order) - 1)
                normalised(NQ[l] - 1)

            def gla(l):
                for n in range(len(BR["gla"]["feat"])):
                    dve.wait_ge(*emptied(("f", l, "gla", n)))
                for t in range(NT):
                    dve.wait_ge(*filled(("logit", l, t)))
                    acc = psum(("logit", l, t))
                    dve.tensor_tensor(G["lx"], acc[:, 0:512], gate_b[:, l], ALU.add).then_inc(freed(("logit", l, t)), 1)
                    dve.wait_ge(*emptied(("logit", l, t)))
                    dve.scalar_tensor_tensor(out=G["ab"], in0=G["lx"], scalar=-1.0, in1=G["lx"], op0=ALU.mult, op1=ALU.min).then_inc(sem(("abs", l, t)), 1)
                    dve.wait_ge(*at(("ln", l, t)))
                    dve.scalar_tensor_tensor(out=G["la"], in0=G["lx"], scalar=0.0, in1=G["ab"], op0=ALU.min,
                                             op1=ALU.subtract).then_inc(sem(("la", l, t)), 1)
                    dve.wait_ge(*at(('la', l, t)))
                    dve.wait_ge(*filled(("ktok", l, t)))
                    acc = psum(("ktok", l, t))
                    dve.wait_ge(*emptied(("rest", l, t)))
                    for d in range(2):
                        ins = dve.tensor_tensor(G["kd"][:, 256 * d:256 * d + 256], acc[:, 0:256],
                                                G["ex"][:, 256 * d:256 * d + 256], ALU.mult)
                    ins.then_inc(freed(("ktok", l, t)), 1)
                    dve.wait_ge(*emptied(('ktok', l, t)))
                    dve.wait_ge(*filled(("U", l, t)))
                    acc = psum(("U", l, t))
                    blocks = acc[:, 0:512].rearrange("p (c n) -> p c n", c=4)
                    dve.tensor_copy(G["U"][0:64, t], blocks[0:64, :, 0:64])
                    dve.tensor_copy(G["U"][64:128, t], blocks[64:128, :, 64:128]).then_inc(freed(("U", l, t)), 1)
                    dve.wait_ge(*emptied(('U', l, t)))
                dve.wait_ge(*emptied(("U", l, NT - 1)))
                dve.wait_ge(*emptied(("cum", l, NT - 1)))
                orders = ([4, 5, 0, 1, 2, 3], [5, 4, 3, 2, 1, 0])
                for d in range(2):
                    link(dve.memset(G["S"][:, orders[d][0], 2 * d:2 * d + 2], 0.0))
                for s in range(NT - 1):
                    for d in range(2):
                        cur, nxt = orders[d][s], orders[d][s + 1]
                        for c in (2 * d, 2 * d + 1):
                            link(dve.scalar_tensor_tensor(out=G["S"][:, nxt, c], in0=G["S"][:, cur, c],
                                                          scalar=el[:, c, cur:cur + 1], in1=G["U"][:, cur, c],
                                                          op0=ALU.mult, op1=ALU.add))
                for t in range(NQ[l]):
                    ts = slice(t * P, (t + 1) * P)
                    qt = q[:, 0:2, ts].unsqueeze(1).to_broadcast([P, 2, 2, P])
                    kt = q[:, 2:4, ts].unsqueeze(1).to_broadcast([P, 2, 2, P])

                    def exponents(n):
                        h = LEVELS[n]
                        for d in range(2):
                            bb = bT[:, 2 * d:2 * d + 2, ts].rearrange("p c (n s h) -> p c n s h", s=2, h=h)
                            dd = G["dd"][n % 2][:, d].rearrange("p c (n s h) -> p c n s h", s=2, h=h)
                            lo, up = bb[:, :, :, 0], bb[:, :, :, 1]
                            ref = (lo[..., h - 1:h] if d == 0 else up[..., 0:1]).to_broadcast([P, 2, P // (2 * h), h])
                            q_half, k_half = (1, 0) if d == 0 else (0, 1)
                            dve.tensor_tensor(dd[:, :, :, q_half], bb[:, :, :, q_half], ref, ALU.subtract)
                            ins = dve.tensor_tensor(dd[:, :, :, k_half], ref, bb[:, :, :, k_half], ALU.subtract)
                        ins.then_inc(sem(("dd", l, t, n)), 1)
                        dve.wait_ge(*at(('dd', l, t, n)))

                    def select(n):
                        dve.wait_ge(*filled(("lev", l, t, n)))
                        acc = psum(("lev", l, t, n))
                        for d in range(2):
                            ins = dve.copy_predicated(G["pt"], mask[:, d, n].unsqueeze(1).unsqueeze(1).to_broadcast([P, 2, 2, P]),
                                                      acc[:].rearrange("p (s d c t) -> p d s c t", s=2, d=2, c=2)[:, d])
                            if d == 0:
                                link(ins)
                        ins.then_inc(freed(("lev", l, t, n)), 1)
                        dve.wait_ge(*emptied(("lev", l, t, n)))

                    dve.wait_ge(*at(("eb", l, t)))
                    dve.tensor_tensor(G["qe"], qt, G["eb"], ALU.mult)
                    exponents(0)
                    dve.wait_ge(*filled(("diag", l, t)))
                    acc = psum(("diag", l, t))
                    dve.tensor_tensor(G["pt"], acc[:].rearrange("p (s c t) -> p s c t", s=2, t=P)[:, :, 0:2],
                                      K["two"].unsqueeze(1).unsqueeze(1).to_broadcast([P, 2, 2, P]), ALU.mult).then_inc(freed(("diag", l, t)), 1)
                    dve.wait_ge(*emptied(("diag", l, t)))
                    for n in range(len(LEVELS)):
                        if n + 1 < len(LEVELS):
                            exponents(n + 1)
                        dve.wait_ge(*at(("e", l, t, n)))
                        dve.tensor_tensor(G["ql"][n % 2], qt, G["dd"][n % 2], ALU.mult)
                        dve.tensor_tensor(G["kl"][n % 2], kt, G["dd"][n % 2], ALU.mult).then_inc(sem(("qk", l, t, n)), 1)
                        dve.wait_ge(*at(('qk', l, t, n)))
                        if n >= 1:
                            select(n - 1)
                    select(len(LEVELS) - 1)
                    output(l, "gla", t)

            def finish(l, b):
                nq = NQ[l]
                dve.wait_ge(*emptied(("o", l, b, nq - 1)))
                if b == "gqa":
                    return
                o4 = o_flat[:, 0:256 * nq].rearrange("p (g d) -> p g d", d=64)
                sq4 = prep_flat[:, 0:256 * nq].rearrange("p (g d) -> p g d", d=64)
                link(dve.tensor_tensor(sq4, o4, o4, ALU.mult))
                dve.tensor_reduce(oss[:, 0:4 * nq], sq4, AX, ALU.add).then_inc(sem(("osq", l, b)), 1)
                dve.wait_ge(*at(("oroot", l, b)))
                link(dve.reciprocal(oss[:, 0:4 * nq], oss[:, 0:4 * nq]))
                ins = dve.tensor_tensor(o4, o4, oss[:, 0:4 * nq].unsqueeze(2).to_broadcast([P, 4 * nq, 64]), ALU.mult)
                if b != "ret":
                    link(ins)
                    ins = dve.tensor_tensor(o4, o4, onorm[:, 0 if b == "gla" else 1, l].unsqueeze(1).to_broadcast([P, 4 * nq, 64]),
                                            ALU.mult)
                if b != "dif":
                    link(ins)
                    dve.wait_ge(*at(("osilu", l, b)))
                    oc = o_sb[:, 0:nq].rearrange("p t (c n) -> p c t n", c=2)
                    ins = dve.tensor_tensor(oc, oc, v[:, 2:4, 0:nq], ALU.mult)
                ins.then_inc(sem(("onorm", l, b)), 1)
                dve.wait_ge(*at(('onorm', l, b)))

            def residual(kind, l):
                g0 = 16 if kind == "out" else 40
                segments = segs(W[l])
                with dve.Fori(0, 2) as i:
                    for u in range(4):
                        key = (kind, l, u)
                        dve.wait_ge(*filled(key, i, ck=key if kind == "out" else ("down", l, u, 2)))
                        acc = psum(key)
                        for s, (x, y) in enumerate(segments):
                            xs = xT[:, bass.ds(4 * i + u, 1), x:y].squeeze(1)
                            ins = dve.scalar_tensor_tensor(out=xs, in0=acc[:, x:y],
                                                           scalar=modv[:, bass.ds(g0 + 4 * i + u, 1), s], in1=xs,
                                                           op0=ALU.mult, op1=ALU.add)
                        ins.then_inc(freed(key), 1)
                        dve.wait_ge(*emptied(key, i))
                for u in range(4):
                    dve.wait_ge(*emptied((kind, l, u), 1))

            for l in range(DEPTH):
                if l == 0:
                    modulation(l, 0, 0, MOD0)
                else:
                    modulation(l, 1, 0, MODT)
                norm(l, 1)
                for b in ("ret", "gla", "gqa", "dif"):
                    if b == "ret":
                        strips(l)
                    if b == "gla":
                        gla(l)
                    else:
                        prep_tiles(l, b)
                        retention(l) if b == "ret" else softmax(l, b)
                    finish(l, b)
                if l == 0:
                    modulation(l, 1, MOD0, MODT)
                dve.wait_ge(*at(("pv", l, "dif", NQ[l] - 1, 3)))
                for k in range(KT):
                    split_stream(l, 1, k)
                w = W[l]
                per = 4 * 2
                with dve.Fori(0, 2) as i:
                    link.enter(i, per)
                    for u in range(4):
                        m = mT[:, bass.ds(4 * i + u, 1), 0:w].squeeze(1)
                        for b in range(4):
                            key = ("yb", l, u, b)
                            dve.wait_ge(*emptied(("g", l, u, b), i))
                            dve.wait_ge(*filled(key, i, ck=("g", l, u, 4)))
                            acc = psum(key)
                            if b == 0:
                                dve.tensor_tensor(m, acc[:, 0:w], sig[:, b, 0:w], ALU.mult).then_inc(freed(key), 1)
                                dve.wait_ge(*emptied(key, i))
                            else:
                                dve.tensor_tensor(prod[:, 0:w], acc[:, 0:w], sig[:, b, 0:w], ALU.mult).then_inc(freed(key), 1)
                                dve.wait_ge(*emptied(key, i))
                                ins = dve.tensor_tensor(m, m, prod[:, 0:w], ALU.add)
                                if b < 3:
                                    link(ins)
                                else:
                                    ins.then_inc(sem(("merged", l, u)), 1)
                                    dve.wait_ge(*at(("merged", l, u), i))
                    link.leave(2)
                residual("out", l)
                norm(l, 2)
                cw = vec[:, 2 * l + 1, VB_CW:VB_CW + 3 * FT]
                with dve.Fori(0, FT // 2) as i:
                    link.enter(i, 2 * len(segs(w)))
                    for u in range(2):
                        dve.wait_ge(*filled(("up", l, 2 * u), i))
                        acc = psum(("up", l, 2 * u))
                        dve.wait_ge(*at(("cc", l, u), i))
                        cu = conv[:, u]
                        for x, y in segs(w):
                            left = dve.scalar_tensor_tensor(out=cu[:, x + 1:y], in0=acc[:, x:y - 1],
                                                            scalar=cw[:, bass.ds(2 * i + u, 1)], in1=cu[:, x + 1:y],
                                                            op0=ALU.mult, op1=ALU.add)
                            link(left)
                        for x, y in segs(w):
                            right = dve.scalar_tensor_tensor(out=cu[:, x:y - 1], in0=acc[:, x + 1:y],
                                                             scalar=cw[:, bass.ds(2 * FT + 2 * i + u, 1)], in1=cu[:, x:y - 1],
                                                             op0=ALU.mult, op1=ALU.add)
                        right.then_inc(freed(("up", l, 2 * u)), 1)
                        dve.wait_ge(*emptied(('up', l, 2 * u), i))
                        dve.wait_ge(*at(("cs", l, u), i))
                        dve.wait_ge(*filled(("up", l, 2 * u + 1), i))
                        acc = psum(("up", l, 2 * u + 1))
                        dve.tensor_tensor(ff[:, bass.ds(2 * i + u, 1), 0:w].squeeze(1), cu[:, 0:w], acc[:, 0:w],
                                          ALU.mult).then_inc(freed(("up", l, 2 * u + 1)), 1)
                        dve.wait_ge(*emptied(('up', l, 2 * u + 1), i))
                    link.leave(FT // 2)
                residual("down", l)
            for t in range(TL):
                dve.wait_ge(*filled(("final", t)))
                acc = psum(("final", t))
                dve.tensor_copy(res[:, t], acc[:, 0:D]).then_inc(sem(("fr", t)), 1)
                dve.wait_ge(*at(('fr', t)))


_INS = ["x", "c", "ctx", "c_ctx", "w_mod", "b_mod", "norm1", "norm2", "w_in", "ret_decay", "gla_gate_up", "gla_gate_b",
        "gla_norm", "gqa_qnorm", "gqa_knorm", "dif_qnorm", "dif_knorm", "dif_lambda", "dif_subln", "w_branch", "w_out",
        "w_up", "conv_w", "conv_b", "w_down"]


def kernel(**inputs):
    import concourse.bacc as bacc
    from concourse.bass_utils import run_bass_kernel_spmd as run

    nc = bacc.Bacc("TRN2", target_bir_lowering=False, num_devices=1)
    arrays, args = {}, {}
    given = {name: np.ascontiguousarray(inputs[name]) for name in _INS}
    for name, a in {**given, **constants()}.items():
        arrays[f"in_{name}"] = a
        args[name] = nc.dram_tensor(f"in_{name}", a.shape, mybir.dt.from_np(a.dtype), kind="ExternalInput").ap()
    out = nc.dram_tensor("out_0", (1, LAT, D), F32, kind="ExternalOutput").ap()
    bass_hybrid_backbone(nc, args, out)
    r = run(nc, [arrays], core_ids=[0])
    return r.results[0]["out_0"]
```

```python
import math
from contextlib import ExitStack

import numpy as np
import concourse.bass as bass
import concourse.mybir as mybir
from concourse.alu_op_type import AluOpType as ALU

F32 = mybir.dt.float32
F32R = mybir.dt.float32r
U8 = mybir.dt.uint8
ACT = mybir.ActivationFunctionType
AX = mybir.AxisListType.X

P = 128
D = 1024
KT = D // P
LAT, CTX = 512, 256
T = LAT + CTX
TL, TC = LAT // P, CTX // P
NT = TL + TC
DEPTH = 2
GRID_W = 64
DFF = 2816
FT = DFF // P
MODT = 6 * D // P
RANK = 16
EPS = 1e-6
GATES = 3360
RING = 4
MOD0 = 16
MODCOL = 768
BEHIND_UP = [(), (0, 1), (2, 3), ()]
LEVELS = [64, 32, 16, 8, 4, 2, 1]

BR = {
    "ret": dict(n=0, feat=[0, 128, 256, 384], nq=2, tok=[512, 640, 768, 896]),
    "gla": dict(n=1, feat=[1024, 1152, 1280, 1408, 2048], nq=2, tok=[1536, 1664, 1792, 1920]),
    "gqa": dict(n=2, feat=[2080, 2208, 2336], nq=2, tok=[2464]),
    "dif": dict(n=3, feat=[2592, 2720, 2848, 2976], nq=2, tok=[3104, 3232]),
}
BEFORE = {"gla": "ret", "gqa": "gla", "dif": "gqa"}
VA_BMOD, VA_N1, VA_N2, VA_CB, VA_ROWS = 0, MODT, MODT + KT, MODT + 2 * KT, MODT + 2 * KT + FT
VB_CW, VB_C, VB_QN, VB_ROWS = 0, 3 * FT, 3 * FT + 2 * KT, 3 * FT + 2 * KT + 4
SMALL = [("ident", P), ("ones", P), ("sum64", P), ("sum32", P), ("perm64", P), ("perm32", P),
         ("tri", 2 * P), ("rest", 2 * P), ("two", P), ("swap", P)]


def constants():
    f = np.float32
    j, i = np.arange(P)[:, None], np.arange(P)[None, :]
    c = {}
    c["ident"] = (j == i).astype(f)
    c["two"] = 2 * c["ident"]
    c["swap"] = (j == (i + P // 2) % P).astype(f)
    c["ones"] = np.full((P, P), 1.0 / D, f)
    for d in (64, 32):
        c[f"sum{d}"] = (j // d == i // d).astype(f) / d
        half = d // 2
        first = i % d < half
        c[f"perm{d}"] = (((j == i + half) & first) * -1.0 + ((j == i - half) & ~first) * 1.0).astype(f)
    c["tri"] = np.concatenate([(j <= i), (j >= i)], 1).astype(f) / 16
    c["rest"] = np.concatenate([(j > i), (j < i)], 1).astype(f) / 16
    small = np.concatenate([c[n] for n, _ in SMALL], 1).astype(f)

    def rot(ang, dim):
        cs, sn = np.cos(ang).astype(f).T, np.sin(ang).astype(f).T
        reps = P // (dim // 2)
        return np.tile(cs, (reps, 1)), np.tile(sn, (reps, 1))

    freqs = f(10000.0) ** (-np.linspace(0.0, 1.0, 32, dtype=f))
    ret = rot(np.arange(LAT, dtype=f)[:, None] * freqs, 64)

    def axial(dim):
        ax = dim // 2
        fr = f(10000.0) ** (-np.arange(0, ax, 2, dtype=f) / f(ax))
        tok = np.arange(LAT)
        return rot(np.concatenate([(tok // GRID_W).astype(f)[:, None] * fr,
                                   (tok % GRID_W).astype(f)[:, None] * fr], -1), dim)

    rope = np.concatenate([*ret, *axial(64), *axial(32)], 1).astype(f)
    p = np.arange(P)[:, None]
    e = np.arange(7 * P)[None, :]
    dist = (P * (3 - e // P) + e % P - p).astype(f)
    mask = np.stack([(j // (2 * h) == i // (2 * h)) & (j // h != i // h) for h in LEVELS], 1).astype(f)
    return dict(k_small=small, k_rope=rope, k_dist=dist, k_mask=mask.reshape(P, -1))


class Tally:

    def __init__(self):
        self.count, self.at = {}, {}

    def add(self, sem, key, by=1):
        self.count[sem] = self.count.get(sem, 0) + by
        self.at[key] = (sem, self.count[sem], 0)

    def loop(self, keys, iters, by=1):
        per = {}
        for sem, key in keys:
            per[sem] = per.get(sem, 0) + by
        seen = {}
        for sem, key in keys:
            seen[sem] = seen.get(sem, 0) + by
            self.at[key] = (sem, self.count.get(sem, 0) + seen[sem], per[sem])
        for sem, n in per.items():
            self.count[sem] = self.count.get(sem, 0) + n * iters


class Chain:

    def __init__(self, eng, sem):
        self.eng, self.sem, self.n, self.it = eng, sem, 0, None

    def __call__(self, ins):
        ins.then_inc(self.sem, 1)
        self.n += 1
        if self.it is None:
            self.eng.wait_ge(self.sem, self.n)
        else:
            self.eng.wait_ge(self.sem, self.it[0] * self.it[1] + self.n)

    def enter(self, i, per):
        self.it, self.start = (i, per), self.n

    def leave(self, iters):
        i, per = self.it
        assert self.n - self.start == per, (self.n - self.start, per)
        self.n, self.it = self.start + per * iters, None


def schedule(depth=DEPTH):
    ev = Tally()
    chunk, fill, fills = {}, {}, [0] * 4
    nch, turn = [0], [0]
    splits = {}
    ev.add("half_used", ("one",))

    def split_chunks(keys, iters):
        for n, key in enumerate(keys):
            splits[key] = keys[n - 1]
        ev.loop([("split_ready", ("split", key, j)) for key in keys for j in range(2)], iters)
        ev.loop([("half_used", ("half", key)) for key in keys], iters)

    def chunks(keys, iters=1):
        for n, key in enumerate(keys):
            chunk[key] = (nch[0] + n, len(keys) if iters > 1 else 0)
        nch[0] += len(keys) * iters

    def take(key, p, ready=None, iters=1, per=0):
        fill[key] = (p, fills[p], per, ready)
        fills[p] += 1
        if ready is None:
            ev.add(f"full{p}", ("full", key))

    for l in range(depth):
        nq = NT if l < depth - 1 else TL
        if l == 0:
            for k in range(KT):
                take(("x", k), k % 4)
            for i in range(2 * depth):
                take(("vec", i), i % 4)
        if l == 0:
            chunks([("mod", l, u) for u in range(4)], MOD0 // 4)
            ev.add("mod_ready", ("modr", l, 0))
        else:
            chunks([("modx", l, m) for m in range(4 * (FT // 2), MODT)])
            ev.add("mod_ready", ("modr", l, 1))
        for which in (1, 2):
            if which == 2:
                between = between_projections(l)
                for b in ("ret", "gla", "gqa", "dif"):
                    for kind in ("feat", "tok"):
                        for n in range(len(BR[b][kind])):
                            key = (kind[0], l, b, n)
                            chunks([key])
                            take(key, turn[0] % 2, "chunk")
                            turn[0] += 1
                            chunks([("modx", l, m) for m in between.get(key, [])])
                    if b in BEFORE:
                        take(("y", l, BEFORE[b], 0), 0)
                        take(("y", l, BEFORE[b], 1), 1)
                    if b == "ret":
                        for h in range(4):
                            ev.add("strip_exponents", ("sti", l, h))
                            ev.add("strip_exps", ("ste", l, h))
                    if b != "gla":
                        for n in range(len(BR[b]["feat"])):
                            if b != "ret":
                                ev.add("squares", ("qksq", l, b, n))
                                take(("qkn", l, b, n), 2)
                                ev.add("turnable", ("turnable", l, b, n))
                            take(("rope", l, b, n), 3)
                            ev.add("turned", ("turned", l, b, n))
                    if b == "gla":
                        for g in range(NT // 2):
                            take(("logit", l, g), g % 2)
                            ev.add("gla_abs", ("abs", l, g))
                            ev.add("gla_ln", ("ln", l, g))
                            ev.add("gla_la", ("la", l, g))
                        for t in range(NT):
                            take(("cum", l, t), 1)
                            take(("rest", l, t), 2)
                            take(("ktok", l, t), 3)
                            take(("U", l, t), 0)
                        for t in range(nq):
                            ev.add("gla_eb", ("eb", l, t))
                            take(("diag", l, t), 2)
                            for n in range(len(LEVELS)):
                                ev.add("gla_dd", ("dd", l, t, n))
                                ev.add("gla_e", ("e", l, t, n))
                                ev.add("gla_qk", ("qk", l, t, n))
                                take(("lev", l, t, n), n % 2)
                            take(("o", l, b, t), 3)
                    if b == "gqa":
                        take(("swap", l), 2)
                    for t in range(nq):
                        for h in range(4):
                            if b == "ret":
                                take(("s", l, b, t, h), h % 2)
                                ev.add("weights_used", ("pv", l, b, t, h))
                            if b in ("gqa", "dif"):
                                for m in range(2 if b == "dif" else 1):
                                    take(("s", l, b, t, h, m), m if b == "dif" else h % 2)
                                    ev.add("max_ready", ("max", l, b, t, h, m))
                                if b == "dif":
                                    ev.add("differed", ("dif", l, b, t, h))
                                take(("pt", l, b, t, h), 2)
                                ev.add("weights_used", ("pv", l, b, t, h))
                        if b != "gla":
                            take(("o", l, b, t), 3, ("pv", l, b, t, 3))
                    if b != "gqa":
                        ev.add("o_squares", ("osq", l, b))
                        ev.add("o_roots", ("oroot", l, b))
                        if b in ("ret", "gla"):
                            ev.add("o_silu", ("osilu", l, b))
                        ev.add("o_normed", ("onorm", l, b))
                    if b == "dif":
                        take(("y", l, b, 0), 0)
                        take(("y", l, b, 1), 1)
                if l == 0:
                    ev.add("mod_ready", ("modr", l, 1))
                keys = [("g", l, u, b) for u in range(4) for b in range(5)]
                chunks(keys, 2)
                for k in range(KT):
                    ev.add("stream_split", ("hsplit", l, 1, k))
                split_chunks([key for key in keys if key[3] < 4], 2)
                base = list(fills)
                for u in range(4):
                    for b in range(4):
                        take(("g", l, u, b), b % 2, "chunk")
                    for b in range(4):
                        fill[("yb", l, u, b)] = (2 + b % 2, fills[2 + b % 2], 0, "chunk" if b == 3 else None)
                        fills[2 + b % 2] += 1
                close(fill, fills, base, 2, [k for k in fill if k[0] in ("g", "yb") and k[1] == l])
                ev.loop([(f"full{2 + b % 2}", ("full", ("yb", l, u, b))) for u in range(4) for b in range(3)], 2)
                ev.loop([("merged", ("merged", l, u)) for u in range(4)], 2)
                chunks([("out", l, u) for u in range(4)], 2)
                base = list(fills)
                for u in range(4):
                    take(("out", l, u), u % 2, "chunk")
                close(fill, fills, base, 2, [("out", l, u) for u in range(4)])
            for k in range(KT):
                ev.add("squares", ("sq", l, which, k))
                ev.add("squares_used", ("squ", l, which, k))
            take(("norm", l, which), 2, ("squ", l, which, KT - 1))
            for k in range(KT):
                ev.add("scaled", ("scaled", l, which, k))
                ev.add("h_ready", ("h", l, which, k))
        keys = []
        for u in range(4):
            keys += [("up", l, u)] + ([("mod", l + 1, m) for m in BEHIND_UP[u]] if l + 1 < depth else [])
        chunks(keys, FT // 2)
        for k in range(KT):
            ev.add("stream_split", ("hsplit", l, 2, k))
        split_chunks([("up", l, u) for u in range(4)], FT // 2)
        base = list(fills)
        for u in range(4):
            take(("up", l, u), u, "chunk")
        close(fill, fills, base, FT // 2, [("up", l, u) for u in range(4)])
        ev.loop([("conv_centre", ("cc", l, u)) for u in range(2)], FT // 2)
        ev.loop([("conv_silu", ("cs", l, u)) for u in range(2)], FT // 2)
        chunks([("down", l, u, j) for u in range(4) for j in range(3)], 2)
        base = list(fills)
        for u in range(4):
            take(("down", l, u), u % 2, "chunk")
        close(fill, fills, base, 2, [("down", l, u) for u in range(4)])
    for t in range(TL):
        take(("final", t), t)
        ev.add("final_ready", ("fr", t))
    return ev, chunk, fill, splits


def between_projections(l):
    keys = [(kind[0], l, b, n) for b in ("ret", "gla", "gqa", "dif") for kind in ("feat", "tok")
            for n in range(len(BR[b][kind]))]
    left = list(range(MOD0, MODT)) if l == 0 else []
    extra = len(left) - len(keys)
    return {key: [left.pop(0) for _ in range(2 if n < extra else 1)] for n, key in enumerate(keys) if left}


def close(fill, fills, base, iters, keys):
    per = [a - b for a, b in zip(fills, base)]
    for key in keys:
        p, n, _, ready = fill[key]
        fill[key] = (p, n, per[p], ready)
    for p in range(4):
        fills[p] = base[p] + per[p] * iters


def bass_hybrid_backbone(nc, A, out):
    ev, chunk, fill, splits = schedule()
    ctx = ExitStack()
    with ctx:
        def sb(name, shape, dt=F32):
            return ctx.enter_context(nc.sbuf_tensor(name, shape, dt))

        xT = sb("xT", [P, KT, T])
        hT_at = nc.sbuf_base
        hT = sb("hT", [P, KT, T])
        ring = sb("ring", [P, RING, KT, P])
        small = sb("small", [P, sum(w for _, w in SMALL)])
        rope = sb("rope", [P, 6, LAT])
        dist = sb("dist", [P, 7 * P])
        mask = sb("mask", [P, len(LEVELS), P], U8)
        rows = sb("rows", [P, 2 * DEPTH, P])
        vec = sb("vec", [P, 2 * DEPTH, P])
        gate_b = sb("gate_b", [P, DEPTH, 512])
        gate_up = sb("gate_up", [32, DEPTH, 512])
        onorm = sb("onorm", [P, 2, DEPTH, 64])
        decay = sb("decay", [P, DEPTH * 8])
        lams = sb("lams", [P, DEPTH * 4 * 32])
        tiny = sb("tiny", [P, 256])
        modv = sb("modv", [P, MODT, 2])
        arena_at = nc.sbuf_base
        arena = sb("arena", [P, (FT + 2 + KT) * T])
        w_hi = sb("w_hi", [P, 2, KT // 2, P], F32R)
        w_lo = sb("w_lo", [P, 2, KT // 2, P], F32R)
        one = sb("one", [P, 1])
        used = [0]

        def part(n):
            used[0] += n
            return arena[:, used[0] - n:used[0]]

        q = part(5 * T).rearrange("p (c t) -> p c t", t=T)
        v = part(4 * T).rearrange("p (c n t) -> p c n t", c=4, n=NT)
        yT = part(8 * T).rearrange("p (c t) -> p c t", t=T)
        scratch0 = used[0]
        scratch = arena[:, scratch0:]
        size = {n: w for n, w in SMALL}
        offs, o = {}, 0
        for n, w in SMALL:
            offs[n] = o
            o += w
        K = {n: small[:, offs[n]:offs[n] + w] for n, w in SMALL}
        ident = K["ident"]

        pair = [ctx.enter_context(nc.psum_tensor(f"pair{i}", [P, 1024], F32)) for i in range(4)]

        S = {}
        for name in (["consts", "ident_in", "vectors_in", "x_in", "out_done", "chunk_done", "dve", "act", "pool"]
                     + [f"landed{i}" for i in range(RING)] + [f"freed{i}" for i in range(4)]
                     + [f"full{i}" for i in range(4)] + sorted(k for k in ev.count if not k.startswith("full"))
                     + [f"set{i}" for i in range(8)]):
            S[name] = ctx.enter_context(nc.semaphore(name))

        def at(key, i=0):
            sem, n, per = ev.at[key]
            return S[sem], n + per * i if per else n

        def sem(key):
            return S[ev.at[key][0]]

        def chunk_no(key, i=0):
            n, per = chunk[key]
            return n, (n + per * i if per else n)

        def slot(key):
            return ring[:, chunk[key][0] % RING]

        def half_free(key, j, i):
            other, before = splits[key], i if splits[key] != last_split(key) else i - 1
            if j == 0:
                return at(("half", other), before)
            c, per = chunk[other]
            return S["chunk_done"], c + 1 + per * before

        def last_split(key):
            return splits[key] if chunk[splits[key]][0] > chunk[key][0] else None

        def landed(key, i=0):
            n, per = chunk[key]
            return S[f"landed{n % RING}"], 16 * (n // RING + 1) + (16 * (per // RING) * i if per else 0)

        def room(key, i=0):
            p, n, per, _ = fill[key]
            assert n > 0
            return S[f"freed{p}"], n + per * i if per else n

        def filled(key, i=0, ck=None):
            ready = fill[key][3]
            if ready is None:
                return at(("full", key), i)
            if ready == "chunk":
                return S["chunk_done"], chunk_no(ck or key, i)[1] + 1
            return at(ready, i)

        def emptied(key, i=0):
            p, n, per, _ = fill[key]
            return S[f"freed{p}"], n + 1 + (per * i if per else 0)

        def psum(key):
            return pair[fill[key][0]]

        def freed(key):
            return S[f"freed{fill[key][0]}"]

        def fullsem(key):
            return S[f"full{fill[key][0]}"]

        def segs(w):
            return [(0, min(w, LAT))] + ([(LAT, w)] if w > LAT else [])

        def is_q(b, n):
            return n < BR[b]["nq"]

        def colv(l, which, n):
            return vec[:, 2 * l + which, n:n + 1]

        lg = tiny[:, 0:16]
        neg_lam = tiny[:, 16:18]
        pp1 = tiny[:, 20:36]
        cs = tiny[:, 40:56].rearrange("p (s k) -> p s k", s=2)
        a1 = tiny[:, 64:96].rearrange("p (w k s) -> p w k s", w=2, k=KT)
        nmx = tiny[:, 96:104]
        rsum = [tiny[:, 104:112], tiny[:, 184:192]]
        dtmp = tiny[:, 112:120]
        oss = tiny[:, 120:144]
        lamt = tiny[:, 144:148]
        eps = tiny[:, 150:151]
        rd = tiny[:, 152:184]
        neg_lg, lg_ctx, lg_lat = tiny[:, 192:208], tiny[:, 208:224], tiny[:, 224:240]

        last = DEPTH - 1
        W = {l: (T if l < last else LAT) for l in range(DEPTH)}
        NQ = {l: W[l] // P for l in range(DEPTH)}

        def cut(*sizes):
            o, res = scratch0, []
            for s in sizes:
                res.append(arena[:, o:o + s])
                o += s
            assert o <= arena.shape[1], (o, arena.shape)
            return res

        xin = arena[:, 0:6 * D].rearrange("p (t d) -> p t d", t=NT)
        sqb, rs, tb = cut(2 * T, T, 2 * T)
        sqb = sqb.rearrange("p (b t) -> p b t", b=2)
        tb = tb.rearrange("p (b t) -> p b t", b=2)
        o_flat, prep_flat = cut(6 * 256, 2 * T)
        o_sb = o_flat.rearrange("p (t c) -> p t c", c=256)
        prep = prep_flat.rearrange("p (b t) -> p b t", b=2)
        NEAR, FAR = 7 * P, 5 * P
        _, strip, pt_r = cut(6 * 256 + 2 * T, 4 * (NEAR + FAR), 2 * T)
        e0, e2, e1 = pt_r[:, 0:NEAR], pt_r[:, NEAR:NEAR + FAR], o_flat[:, 0:NEAR]
        strip = strip.rearrange("p (h n) -> p h n", h=4)
        pt_r = pt_r.rearrange("p (b t) -> p b t", b=2)
        _, prob, pt_s = cut(6 * 256 + 2 * T, 4 * T, 2 * T)
        prob = prob.rearrange("p (b m t) -> p b m t", b=2, m=2)
        pt_s = pt_s.rearrange("p (b t) -> p b t", b=2)
        G = {}
        _, bT, el, work, kd1 = cut(6 * 256, 4 * T, 4 * NT, 9 * 512, 512)
        bT = bT.rearrange("p (c t) -> p c t", t=T)
        el = el.rearrange("p (c t) -> p c t", c=4)
        quad = [work[:, 512 * n:512 * (n + 1)].rearrange("p (d c t) -> p d c t", d=2, c=2) for n in range(9)]
        G["dd"], G["qe"], G["eb"] = quad[0:2], quad[6], quad[7]
        G["ql"], G["kl"] = [quad[2 + n][:, 0] for n in range(2)], [quad[2 + n][:, 1] for n in range(2)]
        G["pt"] = work[:, 4096:4608].rearrange("p (s c t) -> p s c t", s=2, c=2)
        yfree = yT.rearrange("p c t -> p (c t)")[:, 4 * T:8 * T]
        G["U"] = yfree[:, 0:1536].rearrange("p (t c n) -> p t c n", t=NT, c=4)
        G["S"] = yfree[:, 1536:3072].rearrange("p (t c n) -> p t c n", t=NT, c=4)
        G["lx"] = [work[:, 1024 * g:1024 * (g + 1)] for g in range(3)]
        G["la"] = [yfree[:, 1536:2560], o_flat[:, 0:1024], work[:, 3072:4096]]
        G["ex"] = [yfree[:, 2560:3072], work[:, 4096:4608]]
        G["kd"] = [o_flat[:, 1024:1536], kd1]
        mT, sig, prod = cut(KT * T, 4 * T, T)
        mT = mT.rearrange("p (c t) -> p c t", t=T)
        sig = sig.rearrange("p (c t) -> p c t", t=T)
        ff = arena[:, 0:FT * T].rearrange("p (c t) -> p c t", t=T)
        conv = arena[:, FT * T:(FT + 2) * T].rearrange("p (c t) -> p c t", t=T)
        rests = nc.alloc_sbuf_tensor_at("rests", [P, KT, T], F32R, offset=hT_at)
        lead = {1: nc.alloc_sbuf_tensor_at("lead1", [P, KT, T], F32R, offset=arena_at),
                2: nc.alloc_sbuf_tensor_at("lead2", [P, KT, T], F32R, offset=arena_at + 4 * (FT + 2) * T)}
        res = arena[:, 0:TL * D].rearrange("p (t d) -> p t d", t=TL)

        mask_in = arena[:, 6 * D:6 * D + len(LEVELS) * P]
        loads = [(small[:], A["k_small"]), (rope[:].rearrange("p c t -> p (c t)"), A["k_rope"]),
                 (dist[:], A["k_dist"]), (mask_in, A["k_mask"]),
                 (decay[:], A["ret_decay"].rearrange("l d h -> (l d h)").partition_broadcast(P)),
                 (lams[:], A["dif_lambda"].rearrange("l m d -> (l m d)").partition_broadcast(P)),
                 (gate_b[:].rearrange("p l n -> p (l n)"), A["gla_gate_b"].rearrange("l d n -> (l d n)").partition_broadcast(P)),
                 (onorm[:, 0].rearrange("p l n -> p (l n)"), A["gla_norm"].rearrange("l n -> (l n)").partition_broadcast(P)),
                 (onorm[:, 1].rearrange("p l n -> p (l n)"), A["dif_subln"].rearrange("l n -> (l n)").partition_broadcast(P))]
        for l in range(DEPTH):
            for r0, name, n in ((VA_BMOD, "b_mod", MODT), (VA_N1, "norm1", KT), (VA_N2, "norm2", KT), (VA_CB, "conv_b", FT)):
                loads.append((rows[r0:r0 + n, 2 * l], A[name][l].rearrange("(r n) -> r n", n=P)))
            loads.append((rows[VB_CW:VB_CW + 3 * FT, 2 * l + 1], A["conv_w"][l].rearrange("w (r n) -> (w r) n", n=P)))
            loads.append((rows[VB_C:VB_C + KT, 2 * l + 1], A["c"].rearrange("b (r n) -> (b r) n", n=P)))
            loads.append((rows[VB_C + KT:VB_C + 2 * KT, 2 * l + 1], A["c_ctx"].rearrange("(r n) -> r n", n=P)))
            for r, name, dim in ((0, "gqa_qnorm", 64), (1, "gqa_knorm", 64), (2, "dif_qnorm", 32), (3, "dif_knorm", 32)):
                for s in range(P // dim):
                    loads.append((rows[VB_QN + r:VB_QN + r + 1, 2 * l + 1, s * dim:(s + 1) * dim], A[name][l:l + 1]))
        late_loads = [(gate_up[RANK * d:RANK * (d + 1), l, 256 * d:256 * (d + 1)], A["gla_gate_up"][l, d])
                      for l in range(DEPTH) for d in range(2)]
        N_HW = len(loads) // 2
        N_CONST = N_HW - 1 + len(late_loads)

        block = ctx.enter_context(nc.Block())

        w_in_v = [A["w_in"][l].rearrange("(k p) n -> p k n", p=P) for l in range(DEPTH)]

        @block.sync
        def _(sp):
            def load(key, src, i=None, k=KT, w=P, ahead=0):
                n, now = chunk_no(key, 0 if i is None else i)
                if n >= RING or i is not None:
                    if ahead >= 0:
                        sp.wait_ge(S["chunk_done"], now - RING + 1 + ahead)
                sp.dma_start(slot(key)[:, 0:k, 0:w], src).then_inc(S[f"landed{n % RING}"], 16)

            sp.dma_start(*loads[0]).then_inc(S["ident_in"], 16)
            sp.dma_start(xin[:, 0:TL], A["x"].rearrange("b (t p) d -> p (b t) d", p=P)).then_inc(S["x_in"], 16)
            sp.dma_start(xin[:, TL:NT], A["ctx"].rearrange("b (t p) d -> p (b t) d", p=P)).then_inc(S["x_in"], 16)
            for dst, src in loads[1:4]:
                sp.dma_start(dst, src).then_inc(S["consts"], 16)
            for l in range(DEPTH):
                wm = A["w_mod"][l].rearrange("(k p) (c n) -> c p k n", p=P, n=P)
                if l == 0:
                    for u in range(4):
                        load(("mod", l, u), wm[u])
                    with sp.Fori(0, MOD0 // 4 - 1) as i:
                        for u in range(4):
                            load(("mod", l, u), wm[bass.ds(4 * i + (4 + u), 1)].squeeze(0), i + 1)
                else:
                    for m in range(4 * (FT // 2), MODT):
                        load(("modx", l, m), wm[m])
                between = between_projections(l)
                for b in ("ret", "gla", "gqa", "dif"):
                    for kind in ("feat", "tok"):
                        for n, c in enumerate(BR[b][kind]):
                            key = (kind[0], l, b, n)
                            w = 32 if c == 2048 else P
                            load(key, w_in_v[l][:, :, c:c + w], w=w)
                            for m in between.get(key, []):
                                load(("modx", l, m), wm[m])
                wg = A["w_in"][l, :, GATES:].rearrange("(k p) (c n) -> c p k n", p=P, n=P)
                wb = A["w_branch"][l].rearrange("b (k p) (c n) -> c p (b k) n", p=P, n=P)
                with sp.Fori(0, 2) as i:
                    for u in range(4):
                        for b in range(4):
                            load(("g", l, u, b), wg[bass.ds(4 * i + u + KT * b, 1)].squeeze(0), i, ahead=b // 3)
                        load(("g", l, u, 4), wb[bass.ds(4 * i + u, 1)].squeeze(0), i, ahead=-1)
                wo = A["w_out"][l].rearrange("(k p) (c n) -> c p k n", p=P, n=P)
                with sp.Fori(0, 2) as i:
                    for u in range(4):
                        load(("out", l, u), wo[bass.ds(4 * i + u, 1)].squeeze(0), i)
                wu = A["w_up"][l].rearrange("(k p) (s c n) -> s c p k n", p=P, s=2, n=P)
                if l < last:
                    wn = A["w_mod"][l + 1].rearrange("(k p) (c n) -> c p k n", p=P, n=P)
                with sp.Fori(0, FT // 2) as i:
                    for u in range(4):
                        load(("up", l, u), wu[u % 2, bass.ds(2 * i + u // 2, 1)].squeeze(0), i)
                        for m in (BEHIND_UP[u] if l < last else ()):
                            load(("mod", l + 1, m), wn[bass.ds(4 * i + m, 1)].squeeze(0), i)
                wd = A["w_down"][l].rearrange("(k p) (c n) -> c p k n", p=P, n=P)
                with sp.Fori(0, 2) as i:
                    for u in range(4):
                        for j in range(3):
                            k = min(8, FT - 8 * j)
                            load(("down", l, u, j), wd[bass.ds(4 * i + u, 1), :, 8 * j:8 * j + k].squeeze(0), i, k=k)
            sp.wait_ge(S["out_done"], 16 * TL)

        @block.tensor
        def _(pe):
            def projection(key, rhs, width, i=0, M=P, kt=KT, first=False):
                pe.wait_ge(*room(key, i))
                acc = psum(key)
                pe.wait_ge(*landed(key, i))
                for a, b in segs(width):
                    for k in range(kt):
                        if first:
                            pe.wait_ge(*at(("h", key[1], 1, k)))
                        mm = pe.matmul(acc[0:M, a:b], slot(key)[:, k, 0:M], rhs[:, k, a:b], start=k == 0, stop=k == kt - 1)
                mm.then_inc(S["chunk_done"], 1)

            def split_projection(key, which, width, i):
                pe.wait_ge(*room(key, i))
                acc = psum(key)
                for j in range(2):
                    if key in (("g", key[1], 0, 0), ("up", key[1], 0)):
                        pe.wait_ge(*at(("hsplit", key[1], which, KT // 2 * (j + 1) - 1)))
                    pe.wait_ge(*at(("split", key, j), i))
                    for a, b in segs(width):
                        for k in range(KT // 2):
                            n = KT // 2 * j + k
                            pe.matmul(acc[:, a:b], w_hi[:, j, k], lead[which][:, n, a:b], start=n == 0, stop=False)
                            pe.matmul(acc[:, a:b], w_hi[:, j, k], rests[:, n, a:b], start=False, stop=False)
                            mm = pe.matmul(acc[:, a:b], w_lo[:, j, k], lead[which][:, n, a:b], start=False, stop=n == KT - 1)
                    mm.then_inc(sem(("half", key)) if j == 0 else S["chunk_done"], 1)

            def token_projection(key, tiles):
                pe.wait_ge(*room(key))
                acc = psum(key)
                pe.wait_ge(*landed(key))
                for t in range(tiles):
                    for k in range(KT):
                        mm = pe.matmul(acc[:, t * P:(t + 1) * P], hT[:, k, t * P:(t + 1) * P], slot(key)[:, k],
                                       start=k == 0, stop=k == KT - 1)
                mm.then_inc(S["chunk_done"], 1)

            def modulation(key, col, i=0):
                pe.wait_ge(*landed(key, i))
                for k in range(KT):
                    mm = pe.matmul(pair[3][:, col], slot(key)[:, k], cs[:, :, k], start=k == 0, stop=k == KT - 1)
                mm.then_inc(S["chunk_done"], 1)

            def norm(l, which):
                pe.wait_ge(*room(("norm", l, which)))
                acc = psum(("norm", l, which))
                for k in range(KT):
                    pe.wait_ge(*at(("sq", l, which, k)))
                    for a, b in segs(W[l] if which == 2 else T):
                        mm = pe.matmul(acc[:, a:b], K["ones"], sqb[:, k % 2, a:b], start=k == 0, stop=k == KT - 1)
                    mm.then_inc(sem(("squ", l, which, k)), 1)

            def mean_squares(l, b, n):
                pe.wait_ge(*room(("qkn", l, b, n)))
                acc = psum(("qkn", l, b, n))
                pe.wait_ge(*at(("qksq", l, b, n)))
                for x, y in segs(W[l] if is_q(b, n) else T):
                    mm = pe.matmul(acc[:, x:y], K["sum32" if b == "dif" else "sum64"], prep[:, 0, x:y], start=True, stop=True)
                mm.then_inc(fullsem(("qkn", l, b, n)), 1)

            def rotate(l, b, n):
                pe.wait_ge(*room(("rope", l, b, n)))
                acc = psum(("rope", l, b, n))
                if b == "ret":
                    pe.wait_ge(*emptied(("f", l, b, n)))
                else:
                    pe.wait_ge(*at(("turnable", l, b, n)))
                pe.matmul(acc[:, 0:LAT], K["perm32" if b == "dif" else "perm64"], q[:, n, 0:LAT], start=True, stop=True).then_inc(
                    fullsem(("rope", l, b, n)), 1)

            def retention(l):
                b = "ret"

                def step(now, before):
                    if now:
                        t, h = now
                        pe.wait_ge(*room(("s", l, b, t, h)))
                        acc = psum(("s", l, b, t, h))
                        pb = 64 * (h % 2)
                    if before:
                        values_ready(l, b, *before)
                    for m in range(NT):
                        if now and m in key_tiles(t):
                            mm = pe.matmul(acc[:, m * P:(m + 1) * P], q[pb:pb + 64, 2 + h // 2, m * P:(m + 1) * P],
                                           q[pb:pb + 64, h // 2, t * P:(t + 1) * P], start=True, stop=True)
                            if m == NT - 1:
                                mm.then_inc(fullsem(("s", l, b, t, h)), 1)
                        if before:
                            value_product(l, b, *before, m, pt_r)

                order = [(t, h) for t in range(NQ[l]) for h in range(4)]
                pe.wait_ge(*at(("turned", l, b, 3)))
                step(order[0], None)
                step(order[1], None)
                for n in range(len(order)):
                    step(order[n + 2] if n + 2 < len(order) else None, order[n])

            def key_tiles(t):
                return range(NT) if t < TL else range(TL, NT)

            def values_ready(l, b, t, h):
                if h == 0:
                    pe.wait_ge(*room(("o", l, b, t)))
                pe.wait_ge(*emptied(("s", l, b, t, h) if b == "ret" else ("pt", l, b, t, h)))

            def value_product(l, b, t, h, m, weights):
                if m not in key_tiles(t):
                    return
                pt = weights[:, h % 2].rearrange("p (m n) -> p m n", n=P)
                hv = h // 2 if b == "gqa" else h
                mm = pe.matmul(psum(("o", l, b, t))[:, 64 * h:64 * h + 64], pt[:, m],
                               v[:, hv // 2, m, 64 * (hv % 2):64 * (hv % 2) + 64], start=m == key_tiles(t)[0], stop=m == NT - 1)
                if m == NT - 1:
                    mm.then_inc(sem(("pv", l, b, t, h)), 1)

            def softmax(l, b):
                maps = 2 if b == "dif" else 1

                def scores(t, h):
                    for m in range(maps):
                        pe.wait_ge(*room(("s", l, b, t, h, m)))
                        acc = psum(("s", l, b, t, h, m))
                        if b == "dif":
                            lo, n, qi, ki = 64 * (h % 2) + 32 * m, 32, h // 2, 2 + h // 2
                        else:
                            lo, n, qi, ki = 64 * (h % 2), 64, h // 2, 2 if h // 2 == h % 2 else 3
                        for x, y in (segs(T) if t < TL else [(LAT, T)]):
                            mm = pe.matmul(acc[:, x:y], q[lo:lo + n, qi, t * P:(t + 1) * P], q[lo:lo + n, ki, x:y],
                                           start=True, stop=True)
                        mm.then_inc(fullsem(("s", l, b, t, h, m)), 1)

                def step(now, before):
                    if before:
                        values_ready(l, b, *before)
                    if now:
                        t, h = now
                        pe.wait_ge(*room(("pt", l, b, t, h)))
                        acc = psum(("pt", l, b, t, h))
                        if b == "dif":
                            pe.wait_ge(*at(("dif", l, b, t, h)))
                        else:
                            pe.wait_ge(*emptied(("s", l, b, t, h, 0)))
                    for m in range(NT):
                        if before:
                            value_product(l, b, *before, m, pt_s)
                        if now and m in key_tiles(t):
                            mm = pe.transpose(acc[:, m * P:(m + 1) * P], prob[:, h % 2, 0, m * P:(m + 1) * P], ident)
                            if m == NT - 1:
                                mm.then_inc(fullsem(("pt", l, b, t, h)), 1)

                order = [(t, h) for t in range(NQ[l]) for h in range(4)]
                pe.wait_ge(*at(("turned", l, b, len(BR[b]["feat"]) - 1)))
                if b == "gqa":
                    pe.wait_ge(*room(("swap", l)))
                    acc = psum(("swap", l))
                    for x, y in segs(T):
                        mm = pe.matmul(acc[:, x:y], K["swap"], q[:, 2, x:y], start=True, stop=True)
                    mm.then_inc(fullsem(("swap", l)), 1)
                    pe.wait_ge(*emptied(("swap", l)))
                ahead = 1 if b == "dif" else 2
                for n in range(ahead):
                    scores(*order[n])
                for n in range(len(order)):
                    if n + ahead < len(order):
                        scores(*order[n + ahead])
                    step(order[n], order[n - 1] if n >= 1 else None)
                step(None, order[-1])

            def gla(l):
                pe.wait_ge(*emptied(("f", l, "gla", 4)))
                pe.wait_ge(*emptied(("t", l, "gla", 1)))
                for g in range(NT // 2):
                    pe.wait_ge(*room(("logit", l, g)))
                    acc = psum(("logit", l, g))
                    for t in (2 * g, 2 * g + 1):
                        mm = pe.matmul(acc[:, 512 * (t % 2):512 * (t % 2) + 512], q[0:32, 4, t * P:(t + 1) * P], gate_up[:, l],
                                       start=True, stop=True)
                    mm.then_inc(fullsem(("logit", l, g)), 1)

                def update(t):
                    pe.wait_ge(*room(("U", l, t)))
                    acc = psum(("U", l, t))
                    pe.wait_ge(*emptied(("ktok", l, t)))
                    for d in range(2):
                        for c in range(2):
                            mm = pe.matmul(acc[:, (2 * d + c) * P:(2 * d + c + 1) * P],
                                           G["kd"][t % 2][:, d * 256 + c * P:d * 256 + (c + 1) * P], v[:, c, t],
                                           start=True, stop=True)
                    mm.then_inc(fullsem(("U", l, t)), 1)

                for t in range(NT):
                    la = G["la"][t // 2][:, 512 * (t % 2):512 * (t % 2) + 512]
                    pe.wait_ge(*room(("cum", l, t)))
                    acc = psum(("cum", l, t))
                    pe.wait_ge(*at(("la", l, t // 2)))
                    for d in range(2):
                        for c in range(2):
                            lo = d * 256 + c * P
                            mm = pe.matmul(acc[:, (2 * d + c) * P:(2 * d + c + 1) * P], la[:, lo:lo + P],
                                           K["tri"][:, d * P:(d + 1) * P], start=True, stop=True)
                    mm.then_inc(fullsem(("cum", l, t)), 1)
                    pe.wait_ge(*room(("rest", l, t)))
                    acc = psum(("rest", l, t))
                    for d in range(2):
                        mm = pe.matmul(acc[:, d * 256:d * 256 + 256], K["rest"][:, d * P:(d + 1) * P],
                                       la[:, d * 256:d * 256 + 256], start=True, stop=True)
                    mm.then_inc(fullsem(("rest", l, t)), 1)
                    if t >= 1:
                        update(t - 1)
                    pe.wait_ge(*room(("ktok", l, t)))
                    acc = psum(("ktok", l, t))
                    for c in range(2):
                        mm = pe.transpose(acc[:, c * P:(c + 1) * P], q[:, 2 + c, t * P:(t + 1) * P], ident)
                    mm.then_inc(fullsem(("ktok", l, t)), 1)
                update(NT - 1)
                def diagonal(t):
                    ts = slice(t * P, (t + 1) * P)
                    pe.wait_ge(*room(("diag", l, t)))
                    acc = psum(("diag", l, t))
                    for h in range(4):
                        pb = 64 * (h % 2)
                        lo = 512 * (h % 2) + P * (h // 2)
                        mm = pe.matmul(acc[:, lo:lo + P], q[pb:pb + 64, 2 + h // 2, ts], q[pb:pb + 64, h // 2, ts],
                                       start=True, stop=True)
                    mm.then_inc(fullsem(("diag", l, t)), 1)

                diagonal(0)
                for t in range(NQ[l]):
                    for n in range(len(LEVELS)):
                        pe.wait_ge(*room(("lev", l, t, n)))
                        acc = psum(("lev", l, t, n))
                        pe.wait_ge(*at(("qk", l, t, n)))
                        for h in range(4):
                            pb = 64 * (h % 2)
                            lo = 512 * (h % 2) + P * (h // 2)
                            mm = pe.matmul(acc[:, lo:lo + P], G["kl"][n % 2][pb:pb + 64, h // 2],
                                           G["ql"][n % 2][pb:pb + 64, h // 2], start=True, stop=True)
                        mm.then_inc(fullsem(("lev", l, t, n)), 1)
                    if t + 1 < NQ[l]:
                        diagonal(t + 1)
                    pe.wait_ge(*room(("o", l, "gla", t)))
                    acc = psum(("o", l, "gla", t))
                    pe.wait_ge(*emptied(("lev", l, t, len(LEVELS) - 1)))
                    for c in range(2):
                        for part in range(3):
                            for s in range(2):
                                pb, lo = 64 * s, 512 * s + 64 * c
                                if part == 0:
                                    pe.matmul(acc[:, lo:lo + 64], G["pt"][:, s, c], v[:, c, t, pb:pb + 64],
                                              start=True, stop=False)
                                else:
                                    mm = pe.matmul(acc[:, lo:lo + 64], G["qe"][pb:pb + 64, part - 1, c],
                                                   G["S"][pb:pb + 64, t, 2 * (part - 1) + c], start=False, stop=part == 2)
                    mm.then_inc(fullsem(("o", l, "gla", t)), 1)

            def turn_outputs(l, b):
                if b == "gqa":
                    pe.wait_ge(*emptied(("o", l, b, NQ[l] - 1)))
                else:
                    pe.wait_ge(*at(("onorm", l, b)))
                for c in range(2):
                    pe.wait_ge(*room(("y", l, b, c)))
                    acc = psum(("y", l, b, c))
                    for t in range(NQ[l]):
                        mm = pe.transpose(acc[:, t * P:(t + 1) * P], o_sb[:, t, c * P:(c + 1) * P], ident)
                    mm.then_inc(fullsem(("y", l, b, c)), 1)

            pe.wait_ge(S["x_in"], 16 * 2)
            pe.wait_ge(S["ident_in"], 16)
            for k in range(KT):
                if k >= 4:
                    pe.wait_ge(*room(("x", k)))
                acc = psum(("x", k))
                for t in range(NT):
                    mm = pe.transpose(acc[:, t * P:(t + 1) * P], xin[:, t, k * P:(k + 1) * P], ident)
                mm.then_inc(fullsem(("x", k)), 1)
            pe.wait_ge(S["consts"], 16 * N_CONST)
            pe.wait_ge(S["vectors_in"], 16 * (len(loads) - N_HW))
            for i in range(2 * DEPTH):
                pe.wait_ge(*room(("vec", i)))
                acc = psum(("vec", i))
                nr = VA_ROWS if i % 2 == 0 else VB_ROWS
                pe.transpose(acc[:, 0:nr], rows[0:nr, i], ident[0:nr, 0:nr]).then_inc(fullsem(("vec", i)), 1)
            pe.wait_ge(S["set0"], 1)

            for l in range(DEPTH):
                if l == 0:
                    pe.wait_ge(*emptied(("vec", 3)))
                    with pe.Fori(0, MOD0 // 4) as i:
                        for u in range(4):
                            modulation(("mod", l, u), bass.ds(MODCOL + 8 * i + 2 * u, 2), i)
                else:
                    pe.wait_ge(*emptied(("up", l - 1, 3), FT // 2 - 1))
                    for m in range(4 * (FT // 2), MODT):
                        modulation(("modx", l, m), slice(MODCOL + 2 * m, MODCOL + 2 * m + 2))
                between = between_projections(l)

                def behind(key):
                    for m in between.get(key, []):
                        modulation(("modx", l, m), slice(MODCOL + 2 * m, MODCOL + 2 * m + 2))

                norm(l, 1)
                for b in ("ret", "gla", "gqa", "dif"):
                    nf, nt = len(BR[b]["feat"]), len(BR[b]["tok"])
                    lag = 4 if b == "ret" else 2
                    for j in range(nf + lag):
                        if j < nf:
                            projection(("f", l, b, j), hT, W[l] if is_q(b, j) else T, M=32 if BR[b]["feat"][j] == 2048 else P,
                                       first=b == "ret" and j == 0)
                            if b == "gqa" and j == 0:
                                pe.wait_ge(*emptied(("o", l, "gla", NQ[l] - 1)))
                            behind(("f", l, b, j))
                        elif j < nf + nt:
                            token_projection(("t", l, b, j - nf), NQ[l] if j - nf >= 2 else NT)
                            behind(("t", l, b, j - nf))
                        if b in ("gqa", "dif") and 1 <= j <= nf:
                            mean_squares(l, b, j - 1)
                        if b != "gla" and j >= lag:
                            rotate(l, b, j - lag)
                    for n in range(lag, nt):
                        token_projection(("t", l, b, n), NQ[l] if n >= 2 else NT)
                        behind(("t", l, b, n))
                    if b in BEFORE:
                        turn_outputs(l, BEFORE[b])
                    if b == "gla":
                        gla(l)
                    else:
                        pe.wait_ge(*emptied(("t", l, b, len(BR[b]["tok"]) - 1)))
                        pe.wait_ge(*emptied(("t", l, b, max(0, len(BR[b]["tok"]) - 2))))
                        if b == "ret":
                            retention(l)
                        else:
                            softmax(l, b)
                turn_outputs(l, "dif")
                pe.wait_ge(*emptied(("y", l, "dif", 0)))
                pe.wait_ge(*emptied(("y", l, "dif", 1)))
                if l == 0:
                    pe.wait_ge(*at(("modr", l, 1)))
                with pe.Fori(0, 2) as i:
                    for u in range(4):
                        for b in range(4):
                            split_projection(("g", l, u, b), 1, W[l], i)
                        pe.wait_ge(*landed(("g", l, u, 4), i))
                        for b in range(4):
                            pe.wait_ge(*room(("yb", l, u, b), i))
                            acc = psum(("yb", l, u, b))
                            for x, y in segs(W[l]):
                                for k in range(2):
                                    mm = pe.matmul(acc[:, x:y], slot(("g", l, u, 4))[:, 2 * b + k], yT[:, 2 * b + k, x:y],
                                                   start=k == 0, stop=k == 1)
                            mm.then_inc(fullsem(("yb", l, u, b)) if b < 3 else S["chunk_done"], 1)
                pe.wait_ge(*at(("merged", l, 3), 1))
                with pe.Fori(0, 2) as i:
                    for u in range(4):
                        projection(("out", l, u), mT, W[l], i)
                norm(l, 2)
                with pe.Fori(0, FT // 2) as i:
                    for u in range(4):
                        split_projection(("up", l, u), 2, W[l], i)
                        for m in (BEHIND_UP[u] if l < last else ()):
                            pe.wait_ge(*room(("up", l, 3), i))
                            modulation(("mod", l + 1, m), bass.ds(MODCOL + 8 * i + 2 * m, 2), i)
                pe.wait_ge(*emptied(("up", l, 3), FT // 2 - 1))
                with pe.Fori(0, 2) as i:
                    for u in range(4):
                        pe.wait_ge(*room(("down", l, u), i))
                        acc = psum(("down", l, u))
                        for j in range(3):
                            key = ("down", l, u, j)
                            pe.wait_ge(*landed(key, i))
                            for x, y in segs(W[l]):
                                for k in range(min(8, FT - 8 * j)):
                                    mm = pe.matmul(acc[:, x:y], slot(key)[:, k], ff[:, 8 * j + k, x:y],
                                                   start=j == 0 and k == 0, stop=8 * j + k == FT - 1)
                            mm.then_inc(S["chunk_done"], 1)
            pe.wait_ge(*emptied(("down", last, 3), 1))
            for t in range(TL):
                pe.wait_ge(*room(("final", t)))
                acc = psum(("final", t))
                for k in range(KT):
                    mm = pe.transpose(acc[:, k * P:(k + 1) * P], xT[:, k, t * P:(t + 1) * P], ident)
                mm.then_inc(fullsem(("final", t)), 1)

        @block.gpsimd
        def _(pool):
            link = Chain(pool, S["pool"])
            for dst, src in loads[N_HW:]:
                pool.dma_start(dst, src).then_inc(S["vectors_in"], 16)
            pool.memset(one[:], 1.0).then_inc(sem(("one",)), 1)
            pool.wait_ge(*at(("one",)))

            def split(key, i):
                pool.wait_ge(*landed(key, i))
                for j in range(2):
                    w = slot(key)[:, KT // 2 * j:KT // 2 * (j + 1)]
                    pool.wait_ge(*half_free(key, j, i))
                    link(pool.tensor_tensor(w_hi[:, j], w, one[:].unsqueeze(2).to_broadcast([P, KT // 2, P]), ALU.mult))
                    pool.tensor_tensor(w_lo[:, j], w, w_hi[:, j].bitcast(F32), ALU.subtract).then_inc(
                        sem(("split", key, j)), 1)

            def gla_exponents(l):
                pool.wait_ge(*emptied(("cum", l, NT - 1)))
                pool.wait_ge(*emptied(("U", l, NT - 1)))
                order = [(t, n) for t in range(NQ[l]) for n in range(len(LEVELS))]
                for m, (t, n) in enumerate(order):
                    if m >= 2:
                        pool.wait_ge(*at(("qk", l, *order[m - 2])))
                    h = LEVELS[n]
                    side = [G["dd"][(len(LEVELS) * t + n) % 2][:, s].rearrange("p c (n s h) -> p c n s h", s=2, h=h) for s in range(2)]
                    for d in range(2):
                        bb = bT[:, 2 * d:2 * d + 2, t * P:(t + 1) * P].rearrange("p c (n s h) -> p c n s h", s=2, h=h)
                        border = bb[:, :, :, 0, h - 1:h] if d == 0 else bb[:, :, :, 1, 0:1]
                        ref = border.to_broadcast([P, 2, P // (2 * h), h])
                        pool.tensor_tensor(side[0][:, :, :, 1 - d], bb[:, :, :, 1 - d], ref, ALU.subtract)
                        ins = pool.tensor_tensor(side[1][:, :, :, d], ref, bb[:, :, :, d], ALU.subtract)
                    ins.then_inc(sem(("dd", l, t, n)), 1)

            for l in range(DEPTH):
                gla_exponents(l)
                with pool.Fori(0, 2) as i:
                    link.enter(i, 4 * 4 * 2)
                    for u in range(4):
                        for b in range(4):
                            split(("g", l, u, b), i)
                    link.leave(2)
                with pool.Fori(0, FT // 2) as i:
                    link.enter(i, 4 * 2)
                    for u in range(4):
                        split(("up", l, u), i)
                    link.leave(FT // 2)

        @block.scalar
        def _(act):
            link = Chain(act, S["act"])
            for dst, src in loads[4:N_HW]:
                act.dma_start(dst, src).then_inc(S["consts"], 16)
            act.wait_ge(S["set7"], 1)
            for dst, src in late_loads:
                act.dma_start(dst, src).then_inc(S["consts"], 16)
            for k in range(KT):
                act.wait_ge(*filled(("x", k)))
                acc = psum(("x", k))
                act.activation(xT[:, k], acc[:, 0:T], ACT.Copy).then_inc(freed(("x", k)), 1)
            act.wait_ge(*emptied(("vec", 1)))
            act.activation(tiny[:, 40:56], vec[:, 1, VB_C:VB_C + 2 * KT], ACT.Silu).then_inc(S["set0"], 1)
            act.wait_ge(S["set1"], 1)
            link(act.activation(pp1, pp1, ACT.Exp))
            act.activation(lamt, lamt, ACT.Exp).then_inc(S["set2"], 1)
            act.activation(pp1, pp1, ACT.Ln, bias=1.0).then_inc(S["set3"], 1)

            def norm(l, which):
                w = W[l] if which == 2 else T
                act.wait_ge(*filled(("norm", l, which)))
                acc = psum(("norm", l, which))
                act.activation(rs[:, 0:w], acc[:, 0:w], ACT.Sqrt, bias=eps).then_inc(freed(("norm", l, which)), 1)
                act.wait_ge(*at(("modr", l, 0 if l == 0 and which == 1 else 1)))
                for k in range(KT):
                    act.wait_ge(*at(("scaled", l, which, k)))
                    for s, (x, y) in enumerate(segs(w)):
                        ins = act.activation(hT[:, k, x:y], tb[:, k % 2, x:y], ACT.Identity,
                                             scale=a1[:, which - 1, k, s:s + 1],
                                             bias=modv[:, 24 * (which - 1) + k, s:s + 1])
                    ins.then_inc(sem(("h", l, which, k)), 1)

            def out_of_psum(dst, key, w, scale=1.0):
                act.wait_ge(*filled(key))
                acc = psum(key)
                act.activation(dst, acc[0:dst.shape[0], 0:w], ACT.Copy, scale=scale).then_inc(freed(key), 1)

            def turned_outputs(l, b):
                for c in range(2):
                    out_of_psum(yT[:, 2 * BR[b]["n"] + c, 0:W[l]], ("y", l, b, c), W[l])

            def root(l, b, n):
                w = W[l] if is_q(b, n) else T
                act.wait_ge(*filled(("qkn", l, b, n)))
                acc = psum(("qkn", l, b, n))
                act.activation(prep[:, 1, 0:w], acc[:, 0:w], ACT.Sqrt, bias=eps).then_inc(freed(("qkn", l, b, n)), 1)

            def softmax(l, b):
                maps = 2 if b == "dif" else 1
                scale = (32 if b == "dif" else 64) ** -0.5
                order = [(t, h) for t in range(NQ[l]) for h in range(4)]

                def transposed(n):
                    t, h = order[n]
                    lo = 0 if t < TL else LAT
                    if n >= 2:
                        act.wait_ge(*at(("pv", l, b, *order[n - 2])))
                    act.wait_ge(*filled(("pt", l, b, t, h)))
                    acc = psum(("pt", l, b, t, h))
                    act.activation(pt_s[:, h % 2, lo:T], acc[:, lo:T], ACT.Copy).then_inc(freed(("pt", l, b, t, h)), 1)

                for n, (t, h) in enumerate(order):
                    lo = 0 if t < TL else LAT
                    if n >= 2:
                        act.wait_ge(*filled(("pt", l, b, *order[n - 2])))
                    for m in range(maps):
                        key = ("s", l, b, t, h, m)
                        act.wait_ge(*at(("max", l, b, t, h, m)))
                        c = (h * maps + m) % 8
                        act.activation(prob[:, h % 2, m, lo:T], pair[fill[key][0]][:, lo:T], ACT.Exp, scale=scale,
                                       bias=nmx[:, c:c + 1],
                                       accum_out=rsum[t % 2][:, 4 * m + h:4 * m + h + 1]).then_inc(freed(key), 1)
                    if b == "dif" and n >= 1:
                        transposed(n - 1)
                if b == "dif":
                    transposed(len(order) - 1)

            def gla(l):
                for g in range(NT // 2):
                    act.wait_ge(*at(("abs", l, g)))
                    link(act.activation(G["la"][g], G["la"][g], ACT.Exp))
                for g in range(NT // 2):
                    act.activation(G["la"][g], G["la"][g], ACT.Ln, bias=1.0).then_inc(sem(("ln", l, g)), 1)
                for t in range(NT):
                    ts = slice(t * P, (t + 1) * P)
                    act.wait_ge(*filled(("cum", l, t)))
                    acc = psum(("cum", l, t))
                    cum = acc[:, 0:512].rearrange("p (c t) -> p c t", c=4)
                    act.activation(bT[:, :, ts], cum, ACT.Copy)
                    act.activation(el[:, 0:2, t:t + 1], cum[:, 0:2, P - 1:P], ACT.Exp)
                    act.activation(el[:, 2:4, t:t + 1], cum[:, 2:4, 0:1], ACT.Exp).then_inc(freed(("cum", l, t)), 1)
                    if t >= 2:
                        act.wait_ge(*emptied(("ktok", l, t - 2)))
                    act.wait_ge(*filled(("rest", l, t)))
                    acc = psum(("rest", l, t))
                    act.activation(G["ex"][t % 2], acc[:, 0:512], ACT.Exp).then_inc(freed(("rest", l, t)), 1)
                act.wait_ge(*emptied(("U", l, NT - 1)))
                act.wait_ge(*emptied(("cum", l, NT - 1)))
                for t in range(NQ[l]):
                    act.activation(G["eb"].rearrange("p d c t -> p (d c) t"), bT[:, :, t * P:(t + 1) * P], ACT.Exp).then_inc(
                        sem(("eb", l, t)), 1)
                    for n in range(len(LEVELS)):
                        act.wait_ge(*at(("dd", l, t, n)))
                        act.activation(G["dd"][(len(LEVELS) * t + n) % 2], G["dd"][(len(LEVELS) * t + n) % 2], ACT.Exp).then_inc(sem(("e", l, t, n)), 1)

            for l in range(DEPTH):
                norm(l, 1)
                for b in ("ret", "gla", "gqa", "dif"):
                    nf, nt = len(BR[b]["feat"]), len(BR[b]["tok"])
                    for j in range(nf + nt):
                        if j < nf:
                            w = W[l] if is_q(b, j) else T
                            M = 32 if BR[b]["feat"][j] == 2048 else P
                            out_of_psum(q[0:M, j, 0:w], ("f", l, b, j), w, scale=0.125 if b == "gla" and is_q(b, j) else 1.0)
                        else:
                            n = j - nf
                            tiles = NQ[l] if n >= 2 else NT
                            if n == 2 and b in BEFORE:
                                act.wait_ge(*at(("onorm", l, BEFORE[b])))
                            out_of_psum(v[:, n, 0:tiles].rearrange("p n t -> p (n t)"), ("t", l, b, n), tiles * P)
                        if b == "ret" and j < 4:
                            h = j
                            act.wait_ge(*at(("sti", l, h)))
                            act.activation(e0, e0, ACT.Exp)
                            act.activation(e1, e1, ACT.Exp, scale=-1.0)
                            c0, c1 = 8 * l + h, 8 * l + 4 + h
                            act.activation(strip[:, h, NEAR:], dist[:, 0:FAR], ACT.Exp, scale=lg[:, c0:c0 + 1],
                                           bias=lg_ctx[:, c0:c0 + 1])
                            act.activation(e2, dist[:, 0:FAR], ACT.Exp, scale=neg_lg[:, c1:c1 + 1],
                                           bias=lg_lat[:, c1:c1 + 1]).then_inc(sem(("ste", l, h)), 1)
                        if b in ("gqa", "dif") and 1 <= j <= nf:
                            root(l, b, j - 1)
                    if b in BEFORE:
                        turned_outputs(l, BEFORE[b])
                    if b in ("ret", "gla"):
                        for c in range(2):
                            act.wait_ge(*emptied(("t", l, b, 2 + c)))
                        act.activation(v[:, 2:4, 0:NQ[l]], v[:, 2:4, 0:NQ[l]], ACT.Silu).then_inc(sem(("osilu", l, b)), 1)
                    if b in ("gqa", "dif"):
                        if b == "gqa":
                            out_of_psum(q[:, 3, :], ("swap", l), T)
                        softmax(l, b)
                    if b == "gla":
                        gla(l)
                    if b != "gqa":
                        act.wait_ge(*at(("osq", l, b)))
                        act.activation(oss[:, 0:4 * NQ[l]], oss[:, 0:4 * NQ[l]], ACT.Sqrt, scale=1.0 / 64,
                                       bias=eps).then_inc(sem(("oroot", l, b)), 1)
                turned_outputs(l, "dif")
                with act.Fori(0, 2) as i:
                    for u in range(4):
                        for b in range(4):
                            p, n, per, _ = fill[("yb", l, u, 1)]
                            act.wait_ge(S[f"freed{p}"], n + per * i)
                            act.wait_ge(*filled(("g", l, u, b), i))
                            acc = psum(("g", l, u, b))
                            act.activation(sig[:, b, 0:W[l]], acc[:, 0:W[l]], ACT.Sigmoid).then_inc(freed(("g", l, u, b)), 1)
                norm(l, 2)
                cb, cw = vec[:, 2 * l, VA_CB:VA_CB + FT], vec[:, 2 * l + 1, VB_CW:VB_CW + 3 * FT]
                with act.Fori(0, FT // 2) as i:
                    for u in range(2):
                        p, n, per, _ = fill[("up", l, 2 * u + 1)]
                        act.wait_ge(S[f"freed{p}"], n + per * i)
                        act.wait_ge(*filled(("up", l, 2 * u), i))
                        acc = psum(("up", l, 2 * u))
                        act.activation(conv[:, u, 0:W[l]], acc[:, 0:W[l]], ACT.Identity,
                                       scale=cw[:, bass.ds(FT + 2 * i + u, 1)],
                                       bias=cb[:, bass.ds(2 * i + u, 1)]).then_inc(sem(("cc", l, u)), 1)
                        act.wait_ge(*emptied(("up", l, 2 * u), i))
                        act.activation(conv[:, u, 0:W[l]], conv[:, u, 0:W[l]], ACT.Silu).then_inc(sem(("cs", l, u)), 1)
            for t in range(TL):
                act.wait_ge(*at(("fr", t)))
                act.dma_start(out[0, t * P:(t + 1) * P, :], res[:, t]).then_inc(S["out_done"], 16)

        @block.vector
        def _(dve):
            link = Chain(dve, S["dve"])
            dve.memset(eps, EPS)
            dve.memset(gate_up[:], 0.0).then_inc(S["set7"], 1)
            dve.wait_ge(S["ident_in"], 16)
            dve.wait_ge(S["consts"], 16 * N_CONST)
            dve.wait_ge(S["vectors_in"], 16 * (len(loads) - N_HW))
            link(dve.tensor_copy(mask[:].rearrange("p l t -> p (l t)"), mask_in))
            for i in range(2 * DEPTH):
                dve.wait_ge(*filled(("vec", i)))
                acc = psum(("vec", i))
                nr = VA_ROWS if i % 2 == 0 else VB_ROWS
                dve.tensor_copy(vec[:, i, 0:nr], acc[:, 0:nr]).then_inc(freed(("vec", i)), 1)
                dve.wait_ge(*emptied(('vec', i)))
            dve.scalar_tensor_tensor(out=pp1, in0=decay[:], scalar=-1.0, in1=decay[:], op0=ALU.mult, op1=ALU.min)
            lv = lams[:].rearrange("p (a b d) -> p a b d", b=2, d=32)
            link(dve.tensor_tensor(lv[:, :, 0], lv[:, :, 0], lv[:, :, 1], ALU.mult))
            dve.tensor_reduce(lamt, lv[:, :, 0], AX, ALU.add).then_inc(S["set1"], 1)
            dve.wait_ge(S["set3"], 1)
            link(dve.scalar_tensor_tensor(out=lg, in0=decay[:], scalar=0.0, in1=pp1, op0=ALU.min, op1=ALU.subtract))
            for cols, factor in ((neg_lg, -1.0), (lg_ctx, float(CTX)), (lg_lat, float(LAT))):
                link(dve.tensor_scalar(cols, lg, factor, None, ALU.mult))
            for l in range(DEPTH):
                init = 0.8 - 0.6 * math.exp(-0.3 * l)
                link(dve.tensor_tensor(neg_lam[:, l:l + 1], lamt[:, 2 * l + 1:2 * l + 2], lamt[:, 2 * l:2 * l + 1], ALU.subtract))
                link(dve.tensor_scalar(neg_lam[:, l:l + 1], neg_lam[:, l:l + 1], -init, None, ALU.add))
                link(dve.tensor_scalar(onorm[:, 1, l], onorm[:, 1, l], 1.0 - init, None, ALU.mult))

            def modulation(l, part, first, end):
                key = ("mod", l, 3) if part == 0 else ("modx", l, MODT - 1)
                dve.wait_ge(S["chunk_done"], chunk_no(key, MOD0 // 4 - 1)[1] + 1)
                link(dve.tensor_tensor(modv[:, first:end],
                                       pair[3][:, MODCOL + 2 * first:MODCOL + 2 * end].rearrange("p (m s) -> p m s", s=2),
                                       vec[:, 2 * l, VA_BMOD + first:VA_BMOD + end].unsqueeze(2).to_broadcast([P, end - first, 2]),
                                       ALU.add))
                for w in range(2):
                    if first <= 24 * w + 8 < end:
                        nv = vec[:, 2 * l, VA_N1 + KT * w:VA_N1 + KT * (w + 1)].unsqueeze(2).to_broadcast([P, KT, 2])
                        ins = dve.scalar_tensor_tensor(out=a1[:, w], in0=modv[:, 24 * w + 8:24 * w + 16], scalar=1.0, in1=nv,
                                                       op0=ALU.add, op1=ALU.mult)
                ins.then_inc(sem(("modr", l, part)), 1)
                dve.wait_ge(*at(("modr", l, part)))

            def norm(l, which):
                w = W[l] if which == 2 else T
                for k in range(KT):
                    if l == 0 and which == 1:
                        dve.wait_ge(*emptied(("x", k)))
                    if k >= 2:
                        dve.wait_ge(*at(("squ", l, which, k - 2)))
                    dve.tensor_tensor(sqb[:, k % 2, 0:w], xT[:, k, 0:w], xT[:, k, 0:w], ALU.mult).then_inc(
                        sem(("sq", l, which, k)), 1)
                    dve.wait_ge(*at(('sq', l, which, k)))
                dve.wait_ge(*emptied(("norm", l, which)))
                link(dve.reciprocal(rs[:, 0:w], rs[:, 0:w]))
                for k in range(KT):
                    if k >= 2:
                        dve.wait_ge(*at(("h", l, which, k - 2)))
                    dve.tensor_tensor(tb[:, k % 2, 0:w], xT[:, k, 0:w], rs[:, 0:w], ALU.mult).then_inc(
                        sem(("scaled", l, which, k)), 1)
                    dve.wait_ge(*at(('scaled', l, which, k)))
                    if which == 2 and k >= 1:
                        dve.wait_ge(*at(("h", l, which, k - 1)))
                        split_stream(l, which, k - 1)
                if which == 2:
                    dve.wait_ge(*at(("h", l, which, KT - 1)))
                    split_stream(l, which, KT - 1)

            def split_stream(l, which, k):
                w = W[l]
                hi, h = lead[which][:, k, 0:w], hT[:, k, 0:w]
                link(dve.tensor_copy(hi, h))
                dve.tensor_tensor(rests[:, k, 0:w], h, hi.bitcast(F32), ALU.subtract).then_inc(sem(("hsplit", l, which, k)), 1)
                dve.wait_ge(*at(("hsplit", l, which, k)))

            def prep_tiles(l, b):
                cos_sin = {"ret": 0, "gqa": 2, "dif": 4}[b]
                tiles = len(BR[b]["feat"])

                def squares(n):
                    z = q[:, n, 0:W[l] if is_q(b, n) else T]
                    dve.wait_ge(*emptied(("f", l, b, n)))
                    dve.tensor_tensor(prep[:, 0, 0:z.shape[1]], z, z, ALU.mult).then_inc(sem(("qksq", l, b, n)), 1)
                    dve.wait_ge(*at(("qksq", l, b, n)))

                def normalise(n):
                    w = W[l] if is_q(b, n) else T
                    z = q[:, n, 0:w]
                    dve.wait_ge(*emptied(("qkn", l, b, n)))
                    link(dve.reciprocal(prep[:, 1, 0:w], prep[:, 1, 0:w]))
                    c = VB_QN + (0 if b == "gqa" else 2) + (0 if is_q(b, n) else 1)
                    dve.scalar_tensor_tensor(out=z, in0=z, scalar=colv(l, 1, c), in1=prep[:, 1, 0:w],
                                             op0=ALU.mult, op1=ALU.mult).then_inc(sem(("turnable", l, b, n)), 1)
                    dve.wait_ge(*at(("turnable", l, b, n)))

                def turn(n):
                    dve.wait_ge(*emptied(("f", l, b, n)))
                    dve.wait_ge(*filled(("rope", l, b, n)))
                    acc = psum(("rope", l, b, n))
                    z = q[:, n, 0:LAT]
                    part = prep[:, 1, 0:LAT] if b == "ret" else prob[:, 0, 0, 0:LAT]
                    dve.tensor_tensor(part, acc[:, 0:LAT], rope[:, cos_sin + 1], ALU.mult).then_inc(freed(("rope", l, b, n)), 1)
                    link(dve.tensor_tensor(z, z, rope[:, cos_sin], ALU.mult))
                    dve.wait_ge(*emptied(("rope", l, b, n)))
                    dve.tensor_tensor(z, z, part, ALU.add).then_inc(sem(("turned", l, b, n)), 1)
                    dve.wait_ge(*at(("turned", l, b, n)))

                if b == "ret":
                    for n in range(tiles):
                        turn(n)
                    return
                squares(0)
                normalise(0)
                for n in range(1, tiles):
                    squares(n)
                    turn(n - 1)
                    normalise(n)
                turn(tiles - 1)

            def strips(l):
                D = dist[:, 0:NEAR]
                for h in range(4):
                    dve.tensor_scalar(e0, D, 0.0, lg[:, 8 * l + h:8 * l + h + 1], ALU.max, ALU.mult)
                    dve.tensor_scalar(e1, D, 0.0, lg[:, 8 * l + 4 + h:8 * l + 5 + h], ALU.min, ALU.mult).then_inc(
                        sem(("sti", l, h)), 1)
                    dve.wait_ge(*at(("ste", l, h)))
                    link(dve.scalar_tensor_tensor(out=strip[:, h, 0:NEAR], in0=D, scalar=0.0, in1=e0, op0=ALU.is_ge, op1=ALU.mult))
                    link(dve.scalar_tensor_tensor(out=e1, in0=D, scalar=0.0, in1=e1, op0=ALU.is_le, op1=ALU.mult))
                    link(dve.tensor_tensor(strip[:, h, 0:NEAR], strip[:, h, 0:NEAR], e1, ALU.add))
                    link(dve.tensor_tensor(strip[:, h, NEAR:], strip[:, h, NEAR:], e2, ALU.add))

            def retention(l):
                b = "ret"
                order = [(t, h) for t in range(NQ[l]) for h in range(4)]
                for n, (t, h) in enumerate(order):
                    key = ("s", l, b, t, h)
                    if n >= 2:
                        dve.wait_ge(*at(("pv", l, b, *order[n - 2])))
                    dve.wait_ge(*filled(key))
                    acc = psum(key)
                    pt = pt_r[:, h % 2]
                    if t < TL:
                        dve.scalar_tensor_tensor(out=pt[:, 0:LAT], in0=acc[:, 0:LAT], scalar=0.125,
                                                 in1=strip[:, h, P * (3 - t):P * (3 - t) + LAT], op0=ALU.mult, op1=ALU.mult)
                        far = strip[:, h, NEAR + P * (3 - t):NEAR + P * (3 - t) + CTX]
                    else:
                        far = strip[:, h, P * (3 - t + TL):P * (3 - t + TL) + CTX]
                    dve.scalar_tensor_tensor(out=pt[:, LAT:T], in0=acc[:, LAT:T], scalar=0.125, in1=far,
                                             op0=ALU.mult, op1=ALU.mult).then_inc(freed(key), 1)
                    dve.wait_ge(*emptied(key))
                    if h == 0 and t > 0:
                        output(l, b, t - 1)
                output(l, b, NQ[l] - 1)

            def output(l, b, t):
                dve.wait_ge(*filled(("o", l, b, t)))
                acc = psum(("o", l, b, t))
                if b == "gla":
                    src = acc[:].rearrange("p (s c d) -> p c s d", s=2, d=64)[:, 0:2]
                else:
                    src = acc[:, 0:256].rearrange("p (c s d) -> p c s d", s=2, d=64)
                dve.tensor_copy(o_sb[:, t].rearrange("p (c s d) -> p c s d", s=2, d=64), src).then_inc(freed(("o", l, b, t)), 1)
                dve.wait_ge(*emptied(('o', l, b, t)))

            def softmax(l, b):
                maps = 2 if b == "dif" else 1
                scale = (32 if b == "dif" else 64) ** -0.5
                order = [(t, h) for t in range(NQ[l]) for h in range(4)]

                def maxima(n):
                    t, h = order[n]
                    lo = 0 if t < TL else LAT
                    for m in range(maps):
                        c = (h * maps + m) % 8
                        dve.wait_ge(*filled(("s", l, b, t, h, m)))
                        acc = psum(("s", l, b, t, h, m))
                        link(dve.tensor_reduce(nmx[:, c:c + 1], acc[:, lo:T], AX, ALU.max))
                        dve.tensor_scalar(nmx[:, c:c + 1], nmx[:, c:c + 1], -scale, None, ALU.mult).then_inc(
                            sem(("max", l, b, t, h, m)), 1)
                        dve.wait_ge(*at(('max', l, b, t, h, m)))

                def normalised(t):
                    dve.wait_ge(*filled(("o", l, b, t)))
                    acc = psum(("o", l, b, t))
                    r = rd[:, 4 * (t % 2):4 * (t % 2) + 4]
                    link(dve.reciprocal(r, rsum[t % 2][:, 0:4]))
                    dve.tensor_tensor(o_sb[:, t].rearrange("p (h d) -> p h d", d=64),
                                      acc[:, 0:256].rearrange("p (h d) -> p h d", d=64),
                                      r.unsqueeze(2).to_broadcast([P, 4, 64]), ALU.mult).then_inc(freed(("o", l, b, t)), 1)
                    dve.wait_ge(*emptied(('o', l, b, t)))

                def differ(n):
                    t, h = order[n]
                    lo = 0 if t < TL else LAT
                    for m in range(2):
                        dve.wait_ge(*emptied(("s", l, b, t, h, m)))
                    s0, s1 = (rsum[t % 2][:, 4 * m + h:4 * m + h + 1] for m in range(2))
                    r = rd[:, 16 + h:17 + h]
                    link(dve.reciprocal(r, s1))
                    link(dve.scalar_tensor_tensor(out=r, in0=r, scalar=s0, in1=neg_lam[:, l:l + 1], op0=ALU.mult, op1=ALU.mult))
                    dve.scalar_tensor_tensor(out=prob[:, h % 2, 0, lo:T], in0=prob[:, h % 2, 1, lo:T], scalar=r,
                                             in1=prob[:, h % 2, 0, lo:T], op0=ALU.mult, op1=ALU.add).then_inc(
                        sem(("dif", l, b, t, h)), 1)
                    dve.wait_ge(*at(("dif", l, b, t, h)))

                def transposed(n):
                    t, h = order[n]
                    lo = 0 if t < TL else LAT
                    if n >= 2:
                        dve.wait_ge(*at(("pv", l, b, *order[n - 2])))
                    dve.wait_ge(*filled(("pt", l, b, t, h)))
                    acc = psum(("pt", l, b, t, h))
                    dve.tensor_copy(pt_s[:, h % 2, lo:T], acc[:, lo:T]).then_inc(freed(("pt", l, b, t, h)), 1)
                    dve.wait_ge(*emptied(("pt", l, b, t, h)))

                ahead = 1 if b == "dif" else 2
                for n in range(ahead):
                    maxima(n)
                for n, (t, h) in enumerate(order):
                    if b == "dif":
                        differ(n)
                    elif n >= 1:
                        transposed(n - 1)
                    if n + ahead < len(order):
                        maxima(n + ahead)
                    if h == 0 and t > 0:
                        normalised(t - 1)
                if b == "gqa":
                    transposed(len(order) - 1)
                normalised(NQ[l] - 1)

            def gla(l):
                for n in range(len(BR["gla"]["feat"])):
                    dve.wait_ge(*emptied(("f", l, "gla", n)))
                for g in range(NT // 2):
                    dve.wait_ge(*filled(("logit", l, g)))
                    acc = psum(("logit", l, g))
                    lx, la = G["lx"][g], G["la"][g]
                    dve.tensor_tensor(lx.rearrange("p (t n) -> p t n", t=2), acc[:].rearrange("p (t n) -> p t n", t=2),
                                      gate_b[:, l].unsqueeze(1).to_broadcast([P, 2, 512]), ALU.add).then_inc(freed(("logit", l, g)), 1)
                    dve.wait_ge(*emptied(("logit", l, g)))
                    dve.scalar_tensor_tensor(out=la, in0=lx, scalar=-1.0, in1=lx, op0=ALU.mult, op1=ALU.min).then_inc(
                        sem(("abs", l, g)), 1)
                    dve.wait_ge(*at(("abs", l, g)))
                for g in range(NT // 2):
                    dve.wait_ge(*at(("ln", l, g)))
                    dve.scalar_tensor_tensor(out=G["la"][g], in0=G["lx"][g], scalar=0.0, in1=G["la"][g], op0=ALU.min,
                                             op1=ALU.subtract).then_inc(sem(("la", l, g)), 1)
                    dve.wait_ge(*at(("la", l, g)))

                def take_update(t):
                    dve.wait_ge(*filled(("U", l, t)))
                    acc = psum(("U", l, t))
                    blocks = acc[:, 0:512].rearrange("p (c n) -> p c n", c=4)
                    dve.tensor_copy(G["U"][0:64, t], blocks[0:64, :, 0:64])
                    dve.tensor_copy(G["U"][64:128, t], blocks[64:128, :, 64:128]).then_inc(freed(("U", l, t)), 1)
                    dve.wait_ge(*emptied(("U", l, t)))

                for t in range(NT):
                    if t >= 2:
                        take_update(t - 2)
                    dve.wait_ge(*filled(("ktok", l, t)))
                    acc = psum(("ktok", l, t))
                    dve.wait_ge(*emptied(("rest", l, t)))
                    for d in range(2):
                        ins = dve.tensor_tensor(G["kd"][t % 2][:, 256 * d:256 * d + 256], acc[:, 0:256],
                                                G["ex"][t % 2][:, 256 * d:256 * d + 256], ALU.mult)
                    ins.then_inc(freed(("ktok", l, t)), 1)
                    dve.wait_ge(*emptied(("ktok", l, t)))
                take_update(NT - 2)
                take_update(NT - 1)
                dve.wait_ge(*emptied(("U", l, NT - 1)))
                dve.wait_ge(*emptied(("cum", l, NT - 1)))
                orders = ([4, 5, 0, 1, 2, 3], [5, 4, 3, 2, 1, 0])
                for d in range(2):
                    link(dve.memset(G["S"][:, orders[d][0], 2 * d:2 * d + 2], 0.0))

                def state_step(s):
                    for d in range(2):
                        cur, nxt = orders[d][s], orders[d][s + 1]
                        for c in (2 * d, 2 * d + 1):
                            ins = dve.scalar_tensor_tensor(out=G["S"][:, nxt, c], in0=G["S"][:, cur, c],
                                                           scalar=el[:, c, cur:cur + 1], in1=G["U"][:, cur, c],
                                                           op0=ALU.mult, op1=ALU.add)
                    link(ins)

                def weighted(t, n):
                    ts = slice(t * P, (t + 1) * P)
                    dve.wait_ge(*at(("e", l, t, n)))
                    if n >= 2:
                        dve.wait_ge(*filled(("lev", l, t, n - 2)))
                    e = G["dd"][(len(LEVELS) * t + n) % 2]
                    dve.tensor_tensor(G["ql"][n % 2], q[:, 0:2, ts], e[:, 0], ALU.mult)
                    dve.tensor_tensor(G["kl"][n % 2], q[:, 2:4, ts], e[:, 1], ALU.mult).then_inc(sem(("qk", l, t, n)), 1)
                    dve.wait_ge(*at(("qk", l, t, n)))

                weighted(0, 0)
                for t in range(NQ[l]):
                    ts = slice(t * P, (t + 1) * P)
                    qt = q[:, 0:2, ts].unsqueeze(1).to_broadcast([P, 2, 2, P])

                    def select(n):
                        dve.wait_ge(*filled(("lev", l, t, n)))
                        acc = psum(("lev", l, t, n))
                        dve.copy_predicated(G["pt"], mask[:, n].unsqueeze(1).unsqueeze(1).to_broadcast([P, 2, 2, P]),
                                            acc[:].rearrange("p (s c t) -> p s c t", s=2, t=P)[:, :, 0:2]).then_inc(
                            freed(("lev", l, t, n)), 1)
                        dve.wait_ge(*emptied(("lev", l, t, n)))

                    dve.wait_ge(*at(("eb", l, t)))
                    dve.tensor_tensor(G["qe"], qt, G["eb"], ALU.mult)
                    dve.wait_ge(*filled(("diag", l, t)))
                    acc = psum(("diag", l, t))
                    dve.tensor_tensor(G["pt"], acc[:].rearrange("p (s c t) -> p s c t", s=2, t=P)[:, :, 0:2],
                                      K["two"].unsqueeze(1).unsqueeze(1).to_broadcast([P, 2, 2, P]), ALU.mult).then_inc(freed(("diag", l, t)), 1)
                    dve.wait_ge(*emptied(("diag", l, t)))
                    for n in range(len(LEVELS)):
                        if n >= 1:
                            weighted(t, n)
                        if t == 0 and n < NT - 1:
                            state_step(n)
                        if n >= 1:
                            select(n - 1)
                    select(len(LEVELS) - 1)
                    if t + 1 < NQ[l]:
                        weighted(t + 1, 0)
                    output(l, "gla", t)

            def finish(l, b):
                nq = NQ[l]
                dve.wait_ge(*emptied(("o", l, b, nq - 1)))
                if b == "gqa":
                    return
                o4 = o_flat[:, 0:256 * nq].rearrange("p (g d) -> p g d", d=64)
                sq4 = prep_flat[:, 0:256 * nq].rearrange("p (g d) -> p g d", d=64)
                link(dve.tensor_tensor(sq4, o4, o4, ALU.mult))
                dve.tensor_reduce(oss[:, 0:4 * nq], sq4, AX, ALU.add).then_inc(sem(("osq", l, b)), 1)
                dve.wait_ge(*at(("oroot", l, b)))
                link(dve.reciprocal(oss[:, 0:4 * nq], oss[:, 0:4 * nq]))
                ins = dve.tensor_tensor(o4, o4, oss[:, 0:4 * nq].unsqueeze(2).to_broadcast([P, 4 * nq, 64]), ALU.mult)
                if b != "ret":
                    link(ins)
                    ins = dve.tensor_tensor(o4, o4, onorm[:, 0 if b == "gla" else 1, l].unsqueeze(1).to_broadcast([P, 4 * nq, 64]),
                                            ALU.mult)
                if b != "dif":
                    link(ins)
                    dve.wait_ge(*at(("osilu", l, b)))
                    oc = o_sb[:, 0:nq].rearrange("p t (c n) -> p c t n", c=2)
                    ins = dve.tensor_tensor(oc, oc, v[:, 2:4, 0:nq], ALU.mult)
                ins.then_inc(sem(("onorm", l, b)), 1)
                dve.wait_ge(*at(('onorm', l, b)))

            def residual(kind, l):
                g0 = 16 if kind == "out" else 40
                segments = segs(W[l])
                with dve.Fori(0, 2) as i:
                    for u in range(4):
                        key = (kind, l, u)
                        dve.wait_ge(*filled(key, i, ck=key if kind == "out" else ("down", l, u, 2)))
                        acc = psum(key)
                        for s, (x, y) in enumerate(segments):
                            xs = xT[:, bass.ds(4 * i + u, 1), x:y].squeeze(1)
                            ins = dve.scalar_tensor_tensor(out=xs, in0=acc[:, x:y],
                                                           scalar=modv[:, bass.ds(g0 + 4 * i + u, 1), s], in1=xs,
                                                           op0=ALU.mult, op1=ALU.add)
                        ins.then_inc(freed(key), 1)
                        dve.wait_ge(*emptied(key, i))
                for u in range(4):
                    dve.wait_ge(*emptied((kind, l, u), 1))

            for l in range(DEPTH):
                if l == 0:
                    modulation(l, 0, 0, MOD0)
                else:
                    modulation(l, 1, 0, MODT)
                norm(l, 1)
                for b in ("ret", "gla", "gqa", "dif"):
                    if b == "ret":
                        strips(l)
                    if b == "gla":
                        gla(l)
                    else:
                        prep_tiles(l, b)
                        retention(l) if b == "ret" else softmax(l, b)
                    finish(l, b)
                if l == 0:
                    modulation(l, 1, MOD0, MODT)
                dve.wait_ge(*at(("pv", l, "dif", NQ[l] - 1, 3)))
                for k in range(KT):
                    split_stream(l, 1, k)
                w = W[l]
                per = 4 * 2
                with dve.Fori(0, 2) as i:
                    link.enter(i, per)
                    for u in range(4):
                        m = mT[:, bass.ds(4 * i + u, 1), 0:w].squeeze(1)
                        for b in range(4):
                            key = ("yb", l, u, b)
                            dve.wait_ge(*emptied(("g", l, u, b), i))
                            dve.wait_ge(*filled(key, i, ck=("g", l, u, 4)))
                            acc = psum(key)
                            if b == 0:
                                dve.tensor_tensor(m, acc[:, 0:w], sig[:, b, 0:w], ALU.mult).then_inc(freed(key), 1)
                                dve.wait_ge(*emptied(key, i))
                            else:
                                dve.tensor_tensor(prod[:, 0:w], acc[:, 0:w], sig[:, b, 0:w], ALU.mult).then_inc(freed(key), 1)
                                dve.wait_ge(*emptied(key, i))
                                ins = dve.tensor_tensor(m, m, prod[:, 0:w], ALU.add)
                                if b < 3:
                                    link(ins)
                                else:
                                    ins.then_inc(sem(("merged", l, u)), 1)
                                    dve.wait_ge(*at(("merged", l, u), i))
                    link.leave(2)
                residual("out", l)
                norm(l, 2)
                cw = vec[:, 2 * l + 1, VB_CW:VB_CW + 3 * FT]
                with dve.Fori(0, FT // 2) as i:
                    link.enter(i, 2 * len(segs(w)))
                    for u in range(2):
                        dve.wait_ge(*filled(("up", l, 2 * u), i))
                        acc = psum(("up", l, 2 * u))
                        dve.wait_ge(*at(("cc", l, u), i))
                        cu = conv[:, u]
                        for x, y in segs(w):
                            left = dve.scalar_tensor_tensor(out=cu[:, x + 1:y], in0=acc[:, x:y - 1],
                                                            scalar=cw[:, bass.ds(2 * i + u, 1)], in1=cu[:, x + 1:y],
                                                            op0=ALU.mult, op1=ALU.add)
                            link(left)
                        for x, y in segs(w):
                            right = dve.scalar_tensor_tensor(out=cu[:, x:y - 1], in0=acc[:, x + 1:y],
                                                             scalar=cw[:, bass.ds(2 * FT + 2 * i + u, 1)], in1=cu[:, x:y - 1],
                                                             op0=ALU.mult, op1=ALU.add)
                        right.then_inc(freed(("up", l, 2 * u)), 1)
                        dve.wait_ge(*emptied(('up', l, 2 * u), i))
                        dve.wait_ge(*at(("cs", l, u), i))
                        dve.wait_ge(*filled(("up", l, 2 * u + 1), i))
                        acc = psum(("up", l, 2 * u + 1))
                        dve.tensor_tensor(ff[:, bass.ds(2 * i + u, 1), 0:w].squeeze(1), cu[:, 0:w], acc[:, 0:w],
                                          ALU.mult).then_inc(freed(("up", l, 2 * u + 1)), 1)
                        dve.wait_ge(*emptied(('up', l, 2 * u + 1), i))
                    link.leave(FT // 2)
                residual("down", l)
            for t in range(TL):
                dve.wait_ge(*filled(("final", t)))
                acc = psum(("final", t))
                dve.tensor_copy(res[:, t], acc[:, 0:D]).then_inc(sem(("fr", t)), 1)
                dve.wait_ge(*at(('fr', t)))


_INS = ["x", "c", "ctx", "c_ctx", "w_mod", "b_mod", "norm1", "norm2", "w_in", "ret_decay", "gla_gate_up", "gla_gate_b",
        "gla_norm", "gqa_qnorm", "gqa_knorm", "dif_qnorm", "dif_knorm", "dif_lambda", "dif_subln", "w_branch", "w_out",
        "w_up", "conv_w", "conv_b", "w_down"]


def kernel(**inputs):
    import concourse.bacc as bacc
    from concourse.bass_utils import run_bass_kernel_spmd as run

    nc = bacc.Bacc("TRN2", target_bir_lowering=False, num_devices=1)
    arrays, args = {}, {}
    given = {name: np.ascontiguousarray(inputs[name]) for name in _INS}
    for name, a in {**given, **constants()}.items():
        arrays[f"in_{name}"] = a
        args[name] = nc.dram_tensor(f"in_{name}", a.shape, mybir.dt.from_np(a.dtype), kind="ExternalInput").ap()
    out = nc.dram_tensor("out_0", (1, LAT, D), F32, kind="ExternalOutput").ap()
    bass_hybrid_backbone(nc, args, out)
    r = run(nc, [arrays], core_ids=[0])
    return r.results[0]["out_0"]
```
